# Optimizing a Trainium2 kernel written in Bass

```python
import jax
import jax.numpy as jnp
from jax import lax
import numpy as np

D_MODEL = 1024
BATCH = 1
SEQ = 256
DEPTH = 2
DEC_BATCH = 8
DEC_SEQ = 16
PAST_LEN = 256

CHUNK = 64
N_A = DEPTH // 2
N_B = DEPTH - N_A
GMLP_BLOCK = 128
D_GATE = 2 * D_MODEL
N_SG = 8
SG_W = D_GATE // N_SG
N_HEADS = 8
NOPE_DIM = 64
ROPE_DIM = 32
V_DIM = 64
Q_RANK = 384
KV_RANK = 256
ROPE_THETA = 10000.0
Q_BLOCK = 128
SCALE = (NOPE_DIM + ROPE_DIM) ** -0.5
N_EGROUPS = 4
EXPERTS_PER_GROUP = 4
N_EXPERTS = N_EGROUPS * EXPERTS_PER_GROUP
TOP_K = 2
D_EXPERT = 512
EPS = 1e-6
NEG = -1e30

kernel_name = 'yoco_gmlp_mla_hmoe_stream_step'

def rms_norm(x, g):
    xf = x.astype(jnp.float32)
    y = xf * lax.rsqrt(jnp.mean(xf * xf, axis=-1, keepdims=True) + EPS)
    return (y * g.astype(jnp.float32)).astype(x.dtype)

def layer_norm(x, g, b):
    xf = x.astype(jnp.float32)
    mu = jnp.mean(xf, axis=-1, keepdims=True)
    xc = xf - mu
    var = jnp.mean(xc * xc, axis=-1, keepdims=True)
    return (xc * lax.rsqrt(var + EPS) * g.astype(jnp.float32) + b.astype(jnp.float32)).astype(x.dtype)

def rope(x, pos):
    half = ROPE_DIM // 2
    inv_freq = ROPE_THETA ** (-jnp.arange(half, dtype=jnp.float32) / half)
    ang = pos.astype(jnp.float32)[:, None] * inv_freq[None, :]
    bshape = (ang.shape[0],) + (1,) * (x.ndim - 3) + (half,)
    cos = jnp.cos(ang).reshape(bshape)
    sin = jnp.sin(ang).reshape(bshape)
    xf = x.astype(jnp.float32)
    x1, x2 = xf[..., :half], xf[..., half:]
    return jnp.concatenate([x1 * cos - x2 * sin, x1 * sin + x2 * cos], axis=-1).astype(x.dtype)

def gmlp_mixer(xn, w_in, b_in, ln_g, ln_b, w_s, b_s, w_out, b_out):
    bsz, L, _ = xn.shape
    z = jax.nn.gelu(xn @ w_in + b_in)
    u, v = jnp.split(z, 2, axis=-1)
    v = layer_norm(v, ln_g, ln_b)
    n = min(L, GMLP_BLOCK)
    nb = L // n
    idx = jnp.arange(n)
    allowed = (idx[None, :] // CHUNK) <= (idx[:, None] // CHUNK)
    ws = jnp.where(allowed[None], w_s[:, :n, :n], 0.0).astype(v.dtype)
    vb = v.reshape(bsz, nb, n, N_SG, SG_W)
    s = jnp.einsum('gij,bnjgc->bnigc', ws, vb) + b_s[:, :n].T[None, None, :, :, None]
    s = s.reshape(bsz, L, D_GATE)
    return (u * s) @ w_out + b_out, v

def hier_moe(xn, w_group, b_group, w_expert, b_expert, w1, w3, w2):
    shp = xn.shape
    t = xn.reshape(-1, D_MODEL)
    tf = t.astype(jnp.float32)
    lg = tf @ w_group.astype(jnp.float32) + b_group.astype(jnp.float32)
    pg = jax.nn.softmax(lg, axis=-1)
    g_idx = jnp.argmax(lg, axis=-1)
    g_p = jnp.take_along_axis(pg, g_idx[:, None], axis=-1)
    le = (tf @ w_expert.astype(jnp.float32) + b_expert.astype(jnp.float32)).reshape(-1, N_EGROUPS, EXPERTS_PER_GROUP)
    le_sel = jnp.take_along_axis(le, g_idx[:, None, None], axis=1)[:, 0]
    top_v, top_i = lax.top_k(le_sel, TOP_K)
    wts = jax.nn.softmax(top_v, axis=-1) * g_p
    e_idx = g_idx[:, None] * EXPERTS_PER_GROUP + top_i
    gates = jnp.sum(jax.nn.one_hot(e_idx, N_EXPERTS, dtype=jnp.float32) * wts[..., None], axis=1).astype(t.dtype)
    y = jnp.zeros_like(t)
    for e in range(N_EXPERTS):
        hdn = jax.nn.silu(t @ w1[e]) * (t @ w3[e])
        y = y + gates[:, e:e + 1] * (hdn @ w2[e])
    return y.reshape(shp)

def mla_latent(h, pos, kv_norm, w_dkv, kv_a_norm, k_rope_norm):
    c = rms_norm(h, kv_norm) @ w_dkv
    c_kv = rms_norm(c[..., :KV_RANK], kv_a_norm)
    k_rope = rope(rms_norm(c[..., KV_RANK:], k_rope_norm), pos)
    return c_kv, k_rope

def mla_expand(c_kv, w_uk, w_uv, k_nope_norm):
    k_nope = rms_norm(jnp.einsum('blr,rhd->blhd', c_kv, w_uk), k_nope_norm)
    v = jnp.einsum('blr,rhd->blhd', c_kv, w_uv)
    return k_nope, v

def mla_query(xn, pos, w_dq, q_a_norm, w_uq, q_nope_norm, q_rope_norm):
    cq = rms_norm(xn @ w_dq, q_a_norm)
    q = jnp.einsum('blr,rhd->blhd', cq, w_uq)
    q_nope = rms_norm(q[..., :NOPE_DIM], q_nope_norm)
    q_rope = rope(rms_norm(q[..., NOPE_DIM:], q_rope_norm), pos)
    return q_nope, q_rope

def chunk_attend(q_nope, q_rope, q_pos, k_nope, k_rope, v, k_pos):
    s = (jnp.einsum('bqhd,bkhd->bhqk', q_nope, k_nope, preferred_element_type=jnp.float32)
         + jnp.einsum('bqhd,bkd->bhqk', q_rope, k_rope, preferred_element_type=jnp.float32)) * SCALE
    allowed = (k_pos[None, :] // CHUNK) <= (q_pos[:, None] // CHUNK)
    s = jnp.where(allowed[None, None], s, NEG)
    p = jax.nn.softmax(s, axis=-1).astype(v.dtype)
    return jnp.einsum('bhqk,bkhd->bqhd', p, v)

def blocked_attention(q_nope, q_rope, q_pos, k_nope, k_rope, v, k_pos):
    bsz, L = q_nope.shape[:2]
    nq = L // Q_BLOCK
    qn = q_nope.reshape(bsz, nq, Q_BLOCK, N_HEADS, NOPE_DIM).swapaxes(0, 1)
    qr = q_rope.reshape(bsz, nq, Q_BLOCK, N_HEADS, ROPE_DIM).swapaxes(0, 1)
    qp = q_pos.reshape(nq, Q_BLOCK)
    o = lax.map(lambda a: chunk_attend(a[0], a[1], a[2], k_nope, k_rope, v, k_pos), (qn, qr, qp))
    return o.swapaxes(0, 1).reshape(bsz, L, N_HEADS, V_DIM)

def trunk(x, past_ckv, past_krope, norm_mix, norm_ffn, gm_w_in, gm_b_in, gm_ln_g, gm_ln_b, gm_w_s,
          gm_b_s, gm_w_out, gm_b_out, kv_norm, w_dkv, kv_a_norm, k_rope_norm, w_uk, w_uv, k_nope_norm,
          w_dq, q_a_norm, w_uq, q_nope_norm, q_rope_norm, w_o, moe_w_group, moe_b_group, moe_w_expert,
          moe_b_expert, moe_w1, moe_w3, moe_w2):
    bsz, L, _ = x.shape
    past = 0 if past_ckv is None else past_ckv.shape[1]
    pos = past + jnp.arange(L, dtype=jnp.int32)
    h = x
    v_rows = []
    for l in range(N_A):
        mix, v_l = gmlp_mixer(rms_norm(h, norm_mix[l]), gm_w_in[l], gm_b_in[l], gm_ln_g[l], gm_ln_b[l],
                              gm_w_s[l], gm_b_s[l], gm_w_out[l], gm_b_out[l])
        h = h + mix
        v_rows.append(v_l)
        h = h + hier_moe(rms_norm(h, norm_ffn[l]), moe_w_group[l], moe_b_group[l], moe_w_expert[l],
                         moe_b_expert[l], moe_w1[l], moe_w3[l], moe_w2[l])
    c_kv, k_rope = mla_latent(h, pos, kv_norm, w_dkv, kv_a_norm, k_rope_norm)
    if past_ckv is None:
        ckv_all, krope_all = c_kv, k_rope
    else:
        ckv_all = jnp.concatenate([past_ckv.astype(c_kv.dtype), c_kv], axis=1)
        krope_all = jnp.concatenate([past_krope.astype(k_rope.dtype), k_rope], axis=1)
    k_pos = jnp.arange(past + L, dtype=jnp.int32)
    k_nope, v = mla_expand(ckv_all, w_uk, w_uv, k_nope_norm)
    for j in range(N_B):
        l = N_A + j
        q_nope, q_rope = mla_query(rms_norm(h, norm_mix[l]), pos, w_dq[j], q_a_norm[j], w_uq[j],
                                   q_nope_norm[j], q_rope_norm[j])
        if past_ckv is None:
            o = blocked_attention(q_nope, q_rope, pos, k_nope, krope_all, v, k_pos)
        else:
            o = chunk_attend(q_nope, q_rope, pos, k_nope, krope_all, v, k_pos)
        h = h + o.reshape(bsz, L, N_HEADS * V_DIM) @ w_o[j]
        h = h + hier_moe(rms_norm(h, norm_ffn[l]), moe_w_group[l], moe_b_group[l], moe_w_expert[l],
                         moe_b_expert[l], moe_w1[l], moe_w3[l], moe_w2[l])
    return h, c_kv, k_rope, jnp.stack(v_rows)

def setup_inputs(seed: int = 0) -> dict:
    key = jax.random.key(seed)
    ks = iter(jax.random.split(key, 40))
    f32 = jnp.float32

    def w(shape, fan_in):
        return jax.random.normal(next(ks), shape, f32) * fan_in ** -0.5

    def gain(shape):
        return 1.0 + 0.02 * jax.random.normal(next(ks), shape, f32)

    def bias(shape, s=0.02):
        return s * jax.random.normal(next(ks), shape, f32)

    return {
        'x_prompt': jax.random.normal(next(ks), (BATCH, SEQ, D_MODEL), f32),
        'x_sample': jax.random.normal(next(ks), (DEC_BATCH, DEC_SEQ, D_MODEL), f32),
        'cache_ckv': jax.random.normal(next(ks), (DEC_BATCH, PAST_LEN, KV_RANK), f32),
        'cache_krope': jax.random.normal(next(ks), (DEC_BATCH, PAST_LEN, ROPE_DIM), f32),
        'norm_mix': gain((DEPTH, D_MODEL)),
        'norm_ffn': gain((DEPTH, D_MODEL)),
        'gm_w_in': w((N_A, D_MODEL, 2 * D_GATE), D_MODEL),
        'gm_b_in': bias((N_A, 2 * D_GATE)),
        'gm_ln_g': gain((N_A, D_GATE)),
        'gm_ln_b': bias((N_A, D_GATE)),
        'gm_w_s': w((N_A, N_SG, GMLP_BLOCK, GMLP_BLOCK), GMLP_BLOCK),
        'gm_b_s': gain((N_A, N_SG, GMLP_BLOCK)),
        'gm_w_out': w((N_A, D_GATE, D_MODEL), D_GATE),
        'gm_b_out': bias((N_A, D_MODEL)),
        'kv_norm': gain((D_MODEL,)),
        'w_dkv': w((D_MODEL, KV_RANK + ROPE_DIM), D_MODEL),
        'kv_a_norm': gain((KV_RANK,)),
        'k_rope_norm': gain((ROPE_DIM,)),
        'w_uk': w((KV_RANK, N_HEADS, NOPE_DIM), KV_RANK),
        'w_uv': w((KV_RANK, N_HEADS, V_DIM), KV_RANK),
        'k_nope_norm': gain((NOPE_DIM,)),
        'w_dq': w((N_B, D_MODEL, Q_RANK), D_MODEL),
        'q_a_norm': gain((N_B, Q_RANK)),
        'w_uq': w((N_B, Q_RANK, N_HEADS, NOPE_DIM + ROPE_DIM), Q_RANK),
        'q_nope_norm': gain((N_B, NOPE_DIM)),
        'q_rope_norm': gain((N_B, ROPE_DIM)),
        'w_o': w((N_B, N_HEADS * V_DIM, D_MODEL), N_HEADS * V_DIM),
        'moe_w_group': w((DEPTH, D_MODEL, N_EGROUPS), D_MODEL),
        'moe_b_group': bias((DEPTH, N_EGROUPS), 0.01),
        'moe_w_expert': w((DEPTH, D_MODEL, N_EXPERTS), D_MODEL),
        'moe_b_expert': bias((DEPTH, N_EXPERTS), 0.01),
        'moe_w1': w((DEPTH, N_EXPERTS, D_MODEL, D_EXPERT), D_MODEL),
        'moe_w3': w((DEPTH, N_EXPERTS, D_MODEL, D_EXPERT), D_MODEL),
        'moe_w2': w((DEPTH, N_EXPERTS, D_EXPERT, D_MODEL), D_EXPERT),
    }

def reference(x_prompt, x_sample, cache_ckv, cache_krope, norm_mix, norm_ffn, gm_w_in, gm_b_in, gm_ln_g,
              gm_ln_b, gm_w_s, gm_b_s, gm_w_out, gm_b_out, kv_norm, w_dkv, kv_a_norm, k_rope_norm, w_uk,
              w_uv, k_nope_norm, w_dq, q_a_norm, w_uq, q_nope_norm, q_rope_norm, w_o, moe_w_group,
              moe_b_group, moe_w_expert, moe_b_expert, moe_w1, moe_w3, moe_w2):
    weights = (norm_mix, norm_ffn, gm_w_in, gm_b_in, gm_ln_g, gm_ln_b, gm_w_s, gm_b_s, gm_w_out, gm_b_out,
               kv_norm, w_dkv, kv_a_norm, k_rope_norm, w_uk, w_uv, k_nope_norm, w_dq, q_a_norm, w_uq,
               q_nope_norm, q_rope_norm, w_o, moe_w_group, moe_b_group, moe_w_expert, moe_b_expert,
               moe_w1, moe_w3, moe_w2)
    y_prompt, ckv_prompt, krope_prompt, _ = trunk(x_prompt, None, None, *weights)
    y_sample, ckv_sample, krope_sample, gmlp_v_sample = trunk(x_sample, cache_ckv, cache_krope, *weights)
    return (y_prompt, y_sample, ckv_prompt, krope_prompt, ckv_sample, krope_sample, gmlp_v_sample)


_drawn_inputs = setup_inputs


def setup_inputs(seed=0):
    import zlib

    import numpy as np

    out = dict(_drawn_inputs(seed))
    spreads = {}
    factors = {'gm_ln_g': 2.869,
     'gm_ln_b': 2.783,
     'kv_norm': 2.776,
     'kv_a_norm': 2.738,
     'k_rope_norm': 3.848,
     'k_nope_norm': 8.0,
     'q_a_norm': 6.144,
     'q_nope_norm': 5.235,
     'q_rope_norm': 8.0,
     'moe_b_group': 3.379,
     'moe_b_expert': 3.89}
    for name, (base, spread) in spreads.items():
        noise = np.random.default_rng([zlib.crc32(name.encode()), seed]).standard_normal(out[name].shape)
        drawn = base * np.exp(spread * noise) if base else spread * noise
        out[name] = jnp.asarray(drawn.astype(out[name].dtype))
    for name, factor in factors.items():
        out[name] = (out[name] * factor).astype(out[name].dtype)
    return out
```

```python
from contextlib import ExitStack

import numpy as np

import concourse.bass as bass
from concourse import mybir

ALU = mybir.AluOpType
ACT = mybir.ActivationFunctionType
AX = mybir.AxisListType
F32 = mybir.dt.float32
F32R = mybir.dt.float32r
I32 = mybir.dt.int32
U32 = mybir.dt.uint32

P = 128
TILES = 3
SAMPLE = 2
TOK = TILES * P
D = 1024
KD = D // P
DG = 2048
NSG = 8
SGW = DG // NSG
KG = DG // P
SEQ, DECB, DECS, PAST = 256, 8, 16, 256
CHUNK = 64
HEADS, NOPE, ROPE, VD = 8, 64, 32, 64
QK = NOPE + ROPE
QR, KVR = 384, 256
SCALE = QK ** -0.5
NG, EPG = 4, 4
NE = NG * EPG
DE = 512
KE = DE // P
EPS = 1e-6
BIG = 1e30
NEG = -1e30
SLOTS = 2 * TOK
CAP = 96
EXTRA = SLOTS // (CAP + 1)
ROWS = SLOTS + CAP
WCOL = 4096
N_IN, N_OUT = 8, 4
M_MOE = [N_IN + N_OUT, N_IN + N_OUT + 3 * NE]

C_ID, C_UP, C_ONE = 0, 128, 256
C_COS, C_SIN = 384, 384 + TILES * 16
C_MASK = C_SIN + TILES * 16
C_RANKW = C_MASK + 128
C_IOTA = C_RANKW + 16
CONST_W = C_IOTA + 16


def constants():
    c = np.zeros((P, CONST_W), np.float32)
    c[:, C_ID:C_ID + P] = np.eye(P)
    c[:, C_UP:C_UP + P] = np.triu(np.ones((P, P)), 1)
    c[:, C_ONE:C_ONE + P] = 1.0
    half = ROPE // 2
    inv = (np.float32(10000.0) ** (-np.arange(half, dtype=np.float32) / np.float32(half))).astype(np.float32)
    for t in range(TILES):
        pos = np.arange(P) + t * P if t < SAMPLE else PAST + np.arange(P) % DECS
        ang = pos.astype(np.float32)[:, None] * inv[None]
        c[:, C_COS + 16 * t:C_COS + 16 * t + 16] = np.cos(ang)
        c[:, C_SIN + 16 * t:C_SIN + 16 * t + 16] = np.sin(ang)
    c[:CHUNK, C_MASK + CHUNK:C_MASK + P] = NEG
    c[:, C_RANKW:C_RANKW + 16] = 32 - np.arange(16)
    c[:, C_IOTA:C_IOTA + 16] = np.arange(16)
    return c


def build(nc, A, O):
    top = ExitStack()
    with top:
        def sem(name):
            return top.enter_context(nc.semaphore(name))

        def sb(name, shape, dt=F32, scope=top):
            return scope.enter_context(nc.sbuf_tensor(name, shape, dt))

        xrows = nc.dram_tensor("moe_xrows", (ROWS, D), F32, kind="Internal").ap()
        yrows = nc.dram_tensor("moe_yrows", (ROWS, D), F32, kind="Internal").ap()

        h = sb("h", [P, TILES, D])
        const = sb("const", [P, CONST_W])
        ident, upper, ones = const[:, C_ID:C_ID + P], const[:, C_UP:C_UP + P], const[:, C_ONE:C_ONE + P]
        raw = sb("raw", [P, 3, WCOL])
        gain = sb("gain", [P, D])
        stat = sb("stat", [P, 2, 4])
        wroute = sb("wroute", [P, 2, KD, NG + NE])
        broute = sb("broute", [P, 2, NG + NE])
        ps = top.enter_context(nc.psum_tensor("ps", [P, 8, 512], F32))

        raw_loaded = [sem(f"raw_loaded{i}") for i in range(3)]
        wh_ready, wl_ready, w_used = sem("wh_ready"), sem("wl_ready"), sem("w_used")
        dve_step, act_step = sem("dve_step"), sem("act_step")
        steps = {"dve": 0, "act": 0}

        def dve_link(v, ins):
            steps["dve"] += 1
            ins.then_inc(dve_step, 1)
            v.wait_ge(dve_step, steps["dve"])

        def act_link(a, ins):
            steps["act"] += 1
            ins.then_inc(act_step, 1)
            a.wait_ge(act_step, steps["act"])

        ms_ready, rms_ready = sem("ms_ready"), sem("rms_ready")
        roots = {"v": 0, "a": 0}

        def rms_inverse(v, ms, out, scale):
            steps["dve"] += 1
            nc.vector.tensor_scalar(out, ms, scale, EPS, ALU.mult, ALU.add).then_inc(ms_ready, 1)
            roots["v"] += 1
            v.wait_ge(rms_ready, roots["v"])
            nc.vector.reciprocal(out, out).then_inc(dve_step, 1)
            v.wait_ge(dve_step, steps["dve"])

        def root(a, x):
            roots["a"] += 1
            a.wait_ge(ms_ready, roots["a"])
            nc.scalar.activation(x, x, ACT.Sqrt).then_inc(rms_ready, 1)

        def inverse_rms(v, junk):
            for t in range(TILES):
                dve_link(v, nc.vector.tensor_tensor_reduce(junk, h[:, t], h[:, t], 1.0, 0.0, ALU.mult,
                                                           ALU.add, stat[:, 0, t:t + 1]))
            rms_inverse(v, stat[:, 0, 0:TILES], stat[:, 1, 0:TILES], 1.0 / D)

        def norm_rows(t, out):
            return nc.vector.scalar_tensor_tensor(out, h[:, t], stat[:, 1, t:t + 1], gain[:], ALU.mult, ALU.mult)

        def split_product(pe, m, outs, xh, xl, wh, wl, nk, halves, start=True, stop=True):
            pe.wait_ge(wh_ready, m + 1)
            for t, out in enumerate(outs):
                for k in range(nk):
                    for x in (xh, xl):
                        for c in range(halves):
                            nc.tensor.matmul(out[c], x(t, k), wh[:, k, c * 512:c * 512 + 512],
                                             start=start and k == 0 and x is xh, stop=False)
            pe.wait_ge(wl_ready, m + 1)
            for t, out in enumerate(outs):
                for k in range(nk):
                    for c in range(halves):
                        last = nc.tensor.matmul(out[c], xh(t, k), wl[:, k, c * 512:c * 512 + 512],
                                                start=False, stop=stop and k == nk - 1)
            return last

        gm = ExitStack()
        split_gm = [[sb(f"gm_w{p}{i}", [P, WCOL], F32R, gm) for p in "hl"] for i in range(2)]
        fx = sb("gm_fx", [P, 2 * KD * TOK], F32R, gm)
        xth = fx[:, 0:KD * TOK].rearrange("p (k t) -> p k t", k=KD)
        xtl = fx[:, KD * TOK:].rearrange("p (k t) -> p k t", k=KD)
        utl = fx[:, :].rearrange("p (k t) -> p k t", k=KG)
        u = sb("gm_u", [P, TILES, DG], F32, gm)
        gm_v = ExitStack()
        vv = sb("gm_v", [P, TILES, DG], F32, gm_v)
        gm_v.close()
        uth = sb("gm_uth", [P, KG, TOK], F32R, gm)
        gmst = sb("gm_stat", [P, 20], F32, gm)
        bs = sb("gm_bs", [P, 2, NSG], F32, gm)
        gm.close()
        wst = raw[:, 2, 0:2 * NSG * P].rearrange("p (a g i) -> p a g i", a=2, g=NSG)
        bin_c = raw[:, 2, 2048:3072].rearrange("p (a n) -> p a n", a=2)
        ln_c = raw[:, 2, 3072:4096].rearrange("p (a n) -> p a n", a=2)
        xn = [u[:, 0, i * D:(i + 1) * D] for i in range(2)]
        ws_raw = u[:, 1, 0:2 * NSG * P].rearrange("p (a g j) -> p a g j", a=2, g=NSG)

        ld_h, ld_const, ld_gain, ld_ws, ld_ws16, ld_bs, ld_route = map(
            sem, ["ld_h", "ld_const", "ld_gain", "ld_ws", "ld_ws16", "ld_bs", "ld_route"])
        ld_bin = [sem("ld_bin0"), sem("ld_bin1")]
        ld_ln, ld_bout = sem("ld_ln"), sem("ld_bout")
        ws_zeroed = sem("ws_zeroed")
        gm_xn, gm_xT, gm_xh, gm_xl = map(sem, ["gm_xn", "gm_xT", "gm_xh", "gm_xl"])
        gm_wsT, gm_wst = sem("gm_wsT"), sem("gm_wst")
        z_read, z_gelu = sem("z_read"), sem("z_gelu")
        v_sum, v_ready, ln_used = sem("v_sum"), sem("v_ready"), sem("ln_used")
        s_done, us_ready = sem("s_done"), sem("us_ready")
        uT_done, uth_ready, utl_ready = sem("uT_done"), sem("uth_ready"), sem("utl_ready")
        v_stored = sem("v_stored")

        IN_ORDER = [4, 5, 6, 7, 0, 1, 2, 3]

        def gm_dest(c):
            return (u, c * 512) if c < 4 else (vv, (c - 4) * 512)

        def in_weights(m):
            return A["gm_w_in"][0, :, IN_ORDER[m] * 512:IN_ORDER[m] * 512 + 512].rearrange("(k p) n -> p k n", p=P)

        def out_weights(j):
            return A["gm_w_out"][0, j * 512:(j + 1) * 512, :].rearrange("(k p) n -> p k n", p=P)

        def raw_in(s):
            return raw[:, s, :].rearrange("p (k n) -> p k n", k=KD)

        def raw_out(s):
            return raw[:, s, :].rearrange("p (k n) -> p k n", k=KE)

        def gm_sync(sp):
            sp.dma_start(h[:, 0:2, :], A["x_prompt"][0].rearrange("(t p) d -> p t d", p=P)).then_inc(ld_h, 16)
            sp.dma_start(h[:, 2, :], A["x_sample"].rearrange("b s d -> (b s) d")).then_inc(ld_h, 16)
            for m in range(N_IN + N_OUT):
                if m >= 2:
                    sp.wait_ge(wl_ready, m - 1)
                src = in_weights(m) if m < N_IN else out_weights(m - N_IN)
                dst = raw_in(m % 2) if m < N_IN else raw_out(m % 2)
                sp.dma_start(dst, src).then_inc(raw_loaded[m % 2], 16)

        def gm_pool(g):
            g.dma_start(const[:], A["const"]).then_inc(ld_const, 16)
            g.dma_start(gain[:], A["norm_mix"][0:1, :].partition_broadcast(P)).then_inc(ld_gain, 16)
            g.dma_start(ws_raw[:, 0], A["gm_w_s"][0].rearrange("g i j -> i g j")).then_inc(ld_ws, 16)
            g.wait_ge(ws_zeroed, 1)
            for b in range(DECB):
                g.dma_start(ws_raw[b * DECS:(b + 1) * DECS, 1, :, b * DECS:(b + 1) * DECS],
                            A["gm_w_s"][0, :, 0:DECS, 0:DECS].rearrange("g i j -> i g j")).then_inc(ld_ws16, 16)
            g.dma_start(bs[:, 0], A["gm_b_s"][0].rearrange("g i -> i g"),
                        allow_slow_non_contiguous=True).then_inc(ld_bs, 16)
            for b in range(DECB):
                g.dma_start(bs[b * DECS:(b + 1) * DECS, 1],
                            A["gm_b_s"][0, :, 0:DECS].rearrange("g i -> i g"),
                            allow_slow_non_contiguous=True).then_inc(ld_bs, 16)
            for l in range(2):
                g.dma_start(wroute[:, l, :, 0:NG], A["moe_w_group"][l].rearrange("(k p) n -> p k n", p=P)).then_inc(ld_route, 16)
                g.dma_start(wroute[:, l, :, NG:], A["moe_w_expert"][l].rearrange("(k p) n -> p k n", p=P)).then_inc(ld_route, 16)
                g.dma_start(broute[:, l, 0:NG], A["moe_b_group"][l:l + 1, :].partition_broadcast(P)).then_inc(ld_route, 16)
                g.dma_start(broute[:, l, NG:], A["moe_b_expert"][l:l + 1, :].partition_broadcast(P)).then_inc(ld_route, 16)
            for m in range(N_IN):
                if m == 6:
                    for c in range(4):
                        if c:
                            g.wait_ge(ln_used, c)
                        for i, name in enumerate(("gm_ln_g", "gm_ln_b")):
                            g.dma_start(ln_c[:, i], A[name][0:1, c * 512:c * 512 + 512].partition_broadcast(P)
                                        ).then_inc(ld_ln, 16)
                if m >= 2:
                    g.wait_ge(z_read, TILES * (m - 1))
                c = IN_ORDER[m]
                g.dma_start(bin_c[:, m % 2], A["gm_b_in"][0:1, c * 512:c * 512 + 512].partition_broadcast(P)
                            ).then_inc(ld_bin[m % 2], 16)
            g.wait_ge(v_ready, 1)
            g.dma_start(O[6].rearrange("n b s d -> (n b s) d"), vv[:, SAMPLE, :]).then_inc(v_stored, 16)
            g.dma_start(gain[:], A["gm_b_out"][0:1, :].partition_broadcast(P)).then_inc(ld_bout, 16)

        def split_h(a, m, src_slot, wh, raw_count, free):
            a.wait_ge(raw_loaded[src_slot], 16 * raw_count)
            if free is not None:
                a.wait_ge(w_used, free)
            nc.scalar.activation(wh[:], raw[:, src_slot, :], ACT.Copy).then_inc(wh_ready, 1)

        def split_l(v, m, src_slot, wh, wl):
            v.wait_ge(wh_ready, m + 1)
            nc.vector.tensor_tensor(wl[:], raw[:, src_slot, :], wh[:].bitcast(F32), ALU.subtract).then_inc(wl_ready, 1)

        def gm_split_h(a, m):
            split_h(a, m, m % 2, split_gm[m % 2][0], m // 2 + 1, m - 1 if m >= 2 else None)

        def gm_split_l(v, m):
            split_l(v, m, m % 2, *split_gm[m % 2])

        def gm_vector(v):
            nc.vector.memset(ws_raw[:, 1], 0.0).then_inc(ws_zeroed, 1)
            v.wait_ge(ld_h, 32)
            v.wait_ge(ld_gain, 16)
            inverse_rms(v, u[:, 2, 0:D])
            for t in range(TILES):
                if t >= 2:
                    v.wait_ge(gm_xT, t - 1)
                norm_rows(t, xn[t % 2]).then_inc(gm_xn, 1)
                if t >= 1:
                    gm_xl_part(v, t - 1)
                else:
                    gm_split_l(v, 0)
            gm_xl_part(v, TILES - 1)
            gm_split_l(v, 1)
            for a in range(2):
                v.wait_ge(gm_wsT, a + 1)
                dve_link(v, nc.vector.tensor_copy(wst[:, a], ps[:, 2 * a:2 * a + 2].rearrange("p b (g i) -> p (b g) i", i=P)))
            nc.vector.memset(wst[CHUNK:P, 0, :, 0:CHUNK], 0.0).then_inc(gm_wst, 1)
            for m in range(N_IN):
                c = IN_ORDER[m]
                dst, col = gm_dest(c)
                if m == 4:
                    gm_layer_norm(v)
                for t in range(TILES):
                    if t == 0:
                        v.wait_ge(ld_bin[m % 2], 16 * (m // 2 + 1))
                        v.wait_ge(w_used, m + 1)
                    nc.vector.tensor_tensor(dst[:, t, col:col + 512], ps[:, 3 * (m % 2) + t], bin_c[:, m % 2],
                                            ALU.add).then_inc(z_read, 1)
                gm_split_l(v, m + 2)
            for t in range(TILES):
                for gp in range(NSG // 2):
                    n = t * 4 + gp
                    v.wait_ge(s_done, n + 1)
                    if n == 0:
                        v.wait_ge(z_gelu, TILES * N_IN)
                        v.wait_ge(ld_bs, 16 * (1 + DECB))
                    for i in range(2):
                        g = 2 * gp + i
                        uu = u[:, t, g * SGW:(g + 1) * SGW]
                        nc.vector.scalar_tensor_tensor(uu, ps[:, n % 6, i * SGW:(i + 1) * SGW],
                                                       bs[:, 1 if t == SAMPLE else 0, g:g + 1], uu,
                                                       ALU.add, ALU.mult).then_inc(us_ready, 1)
            for n in range(TILES * 4):
                t, q = divmod(n, 4)
                v.wait_ge(uth_ready, n + 1)
                nc.vector.tensor_tensor(utl[:, 4 * q:4 * q + 4, t * P:(t + 1) * P],
                                        ps[:, 6 + n % 2].rearrange("p (k t) -> p k t", k=4),
                                        uth[:, 4 * q:4 * q + 4, t * P:(t + 1) * P].bitcast(F32),
                                        ALU.subtract).then_inc(utl_ready, 1)
            v.wait_ge(ld_bout, 16)
            for t in range(TILES):
                dve_link(v, nc.vector.tensor_tensor(h[:, t], h[:, t], gain[:], ALU.add))
            for m in range(N_IN + 2, N_IN + N_OUT):
                gm_split_l(v, m)
            v.wait_ge(w_used, N_IN + N_OUT)
            for t in range(TILES):
                dve_link(v, nc.vector.tensor_tensor(h[:, t].rearrange("p (c n) -> p c n", c=2),
                                                    h[:, t].rearrange("p (c n) -> p c n", c=2),
                                                    ps[:, 2 * t:2 * t + 2], ALU.add))

        def gm_xl_part(v, t):
            v.wait_ge(gm_xh, t + 1)
            nc.vector.tensor_tensor(xtl[:, :, t * P:(t + 1) * P], ps[:, 6:8].rearrange("p b (k t) -> p (b k) t", t=P),
                                    xth[:, :, t * P:(t + 1) * P].bitcast(F32), ALU.subtract).then_inc(gm_xl, 1)

        def gm_layer_norm(v):
            v.wait_ge(z_gelu, TILES * 4)
            mean, inv = gmst[:, 12:15], gmst[:, 15:18]
            dve_link(v, nc.vector.tensor_reduce(mean, gmst[:, 0:12].rearrange("p (t c) -> p t c", t=TILES), AX.X, ALU.add))
            dve_link(v, nc.vector.tensor_scalar(mean, mean, 1.0 / DG, None, ALU.mult))
            for t in range(TILES):
                dve_link(v, nc.vector.tensor_scalar(vv[:, t], vv[:, t], mean[:, t:t + 1], None, ALU.subtract))
                dve_link(v, nc.vector.tensor_tensor_reduce(u[:, 2], vv[:, t], vv[:, t], 1.0, 0.0, ALU.mult, ALU.add,
                                                           inv[:, t:t + 1]))
            rms_inverse(v, inv, inv, 1.0 / DG)
            for t in range(TILES):
                dve_link(v, nc.vector.tensor_scalar(vv[:, t], vv[:, t], inv[:, t:t + 1], None, ALU.mult))
            for c in range(4):
                v.wait_ge(ld_ln, 32 * (c + 1))
                cols = slice(c * 512, c * 512 + 512)
                for i, op in ((0, ALU.mult), (1, ALU.add)):
                    last = nc.vector.tensor_tensor(vv[:, :, cols], vv[:, :, cols],
                                                   ln_c[:, i:i + 1].to_broadcast([P, TILES, 512]), op)
                    if i == 0:
                        dve_link(v, last)
                last.then_inc(ln_used, 1)
            v.wait_ge(ln_used, 4)
            nc.vector.memset(gmst[:, 18:19], 0.0).then_inc(v_ready, 1)

        def gm_scalar(a):
            root(a, stat[:, 1, 0:TILES])
            gm_split_h(a, 0)
            gm_xh_part(a, 0)
            gm_split_h(a, 1)
            gm_xh_part(a, 1)
            gm_xh_part(a, 2)
            for m in range(N_IN):
                c = IN_ORDER[m]
                dst, col = gm_dest(c)
                if m == 4:
                    root(a, gmst[:, 15:18])
                for t in range(TILES):
                    a.wait_ge(z_read, m * TILES + t + 1)
                    z = dst[:, t, col:col + 512]
                    kw = {"accum_out": gmst[:, 4 * t + c - 4:4 * t + c - 3]} if c >= 4 else {}
                    nc.scalar.activation(z, z, ACT.Gelu_apprx_tanh, **kw).then_inc(z_gelu, 1)
                gm_split_h(a, m + 2)
            for n in range(TILES * 4):
                t, q = divmod(n, 4)
                a.wait_ge(uT_done, n + 1)
                if n == 0:
                    a.wait_ge(v_stored, 16)
                nc.scalar.activation(uth[:, 4 * q:4 * q + 4, t * P:(t + 1) * P],
                                     ps[:, 6 + n % 2].rearrange("p (k t) -> p k t", k=4), ACT.Copy).then_inc(uth_ready, 1)
            for m in range(N_IN + 2, N_IN + N_OUT):
                gm_split_h(a, m)

        def gm_xh_part(a, t):
            a.wait_ge(gm_xT, t + 1)
            nc.scalar.activation(xth[:, :, t * P:(t + 1) * P], ps[:, 6:8].rearrange("p b (k t) -> p (b k) t", t=P),
                                 ACT.Copy).then_inc(gm_xh, 1)

        def gm_tensor(pe):
            pe.wait_ge(ld_const, 16)
            for t in range(TILES):
                pe.wait_ge(gm_xn, t + 1)
                if t:
                    pe.wait_ge(gm_xl, t)
                for k in range(KD):
                    last = nc.tensor.transpose(ps[:, 6 + k // 4, (k % 4) * P:(k % 4 + 1) * P],
                                               xn[t % 2][:, k * P:(k + 1) * P], ident)
                last.then_inc(gm_xT, 1)
            for a, s, n in ((0, ld_ws, 16), (1, ld_ws16, 16 * DECB)):
                pe.wait_ge(s, n)
                for g in range(NSG):
                    last = nc.tensor.transpose(ps[:, 2 * a + g // 4, (g % 4) * P:(g % 4 + 1) * P], ws_raw[:, a, g], ident)
                last.then_inc(gm_wsT, 1)
            pe.wait_ge(gm_xl, TILES)
            pe.wait_ge(gm_wst, 1)
            for m in range(N_IN):
                if m >= 2:
                    pe.wait_ge(z_read, TILES * (m - 1))
                wh, wl = [w[:].rearrange("p (k n) -> p k n", k=KD) for w in split_gm[m % 2]]
                last = split_product(pe, m, [[ps[:, 3 * (m % 2) + t]] for t in range(TILES)],
                                     lambda t, k: xth[:, k, t * P:(t + 1) * P], lambda t, k: xtl[:, k, t * P:(t + 1) * P],
                                     wh, wl, KD, 1)
                last.then_inc(w_used, 1)
            pe.wait_ge(v_ready, 1)
            pe.wait_ge(z_read, TILES * N_IN)
            for t in range(TILES):
                for gp in range(NSG // 2):
                    n = t * 4 + gp
                    if n >= 6:
                        pe.wait_ge(us_ready, 2 * (n - 5))
                    for i in range(2):
                        g = 2 * gp + i
                        last = nc.tensor.matmul(ps[:, n % 6, i * SGW:(i + 1) * SGW], wst[:, 1 if t == SAMPLE else 0, g],
                                                vv[:, t, g * SGW:(g + 1) * SGW], start=True, stop=True)
                    last.then_inc(s_done, 1)
            for n in range(TILES * 4):
                t, q = divmod(n, 4)
                pe.wait_ge(us_ready, 8 * (t + 1))
                if n >= 2:
                    pe.wait_ge(utl_ready, n - 1)
                for j in range(4):
                    k = 4 * q + j
                    last = nc.tensor.transpose(ps[:, 6 + n % 2, j * P:(j + 1) * P], u[:, t, k * P:(k + 1) * P], ident)
                last.then_inc(uT_done, 1)
            pe.wait_ge(utl_ready, TILES * 4)
            for j in range(N_OUT):
                m = N_IN + j
                wh, wl = [w[:].rearrange("p (k n) -> p k n", k=KE) for w in split_gm[m % 2]]
                last = split_product(pe, m, [[ps[:, 2 * t], ps[:, 2 * t + 1]] for t in range(TILES)],
                                     lambda t, k: uth[:, 4 * j + k, t * P:(t + 1) * P],
                                     lambda t, k: utl[:, 4 * j + k, t * P:(t + 1) * P],
                                     wh, wl, KE, 2, start=j == 0, stop=j == N_OUT - 1)
                last.then_inc(w_used, 1)

        moe = ExitStack()
        split_moe = [[sb(f"moe_w{p}{i}", [P, WCOL], F32R, moe) for p in "hl"] for i in range(3)]
        rows = sb("moe_rows", [P, 4, D], F32, moe)
        xsplit = [[sb(f"moe_x{p}{i}", [P, KD, CAP], F32R, moe) for p in "hl"] for i in range(2)]
        sil = sb("moe_silu", [CAP, DE], F32, moe)
        hid = sb("moe_hidden", [CAP, DE], F32, moe)
        hth, htl = sb("moe_hTh", [P, KE, CAP], F32R, moe), sb("moe_hTl", [P, KE, CAP], F32R, moe)
        NT = NG + NE
        logit = sb("rt_logit", [P, TILES, NT], F32, moe)
        gsel = sb("rt_group", [P, TILES, NG], F32, moe)
        pen = sb("rt_penalty", [P, TILES, NG], F32, moe)
        lem = sb("rt_in_group", [P, TILES, NE], F32, moe)
        pick = [sb(f"rt_pick{i}", [P, TILES, NE], F32, moe) for i in range(2)]
        tmp = sb("rt_tmp", [P, TILES, NE], F32, moe)
        best = sb("rt_best", [P, 6, TILES], F32, moe)
        ex = sb("rt_exp", [P, TILES, NG + 1], F32, moe)
        wts = sb("rt_weight", [P, 2, TILES], F32, moe)
        picked = sb("rt_picked", [P, TILES, NE], F32, moe)
        rank = sb("rt_rank", [P, TILES + 1, NE], F32, moe)
        cat = sb("rt_counts", [P, 2 * NE], F32, moe)
        first = sb("rt_first", [P, 2 * NE], F32, moe)
        dst = sb("rt_dst", [P, TILES, 2], F32, moe)
        dst_i = sb("rt_dst_i", [P, TILES * 2], U32, moe)
        first_i = sb("rt_first_i", [P, NE], I32, moe)
        ov = sb("rt_over", [P, 4, NE], F32, moe)
        ovb = sb("rt_over_block", [P, EXTRA, NE], F32, moe)
        ovb2 = sb("rt_over_block2", [P, EXTRA, NE], F32, moe)
        ovt = sb("rt_over_table", [P, 16], F32, moe)
        ovt_i = sb("rt_over_table_i", [P, 16], I32, moe)
        moe.close()
        BX, BA, BB, BH, BY, BR = 0, 2, 3, 4, 5, 7

        ld_ffn, pad_written = sem("ld_ffn"), sem("pad_written")
        rt_xn, rt_xT, rt_xTc, rt_logits = sem("rt_xn"), sem("rt_xT"), sem("rt_xTc"), sem("rt_logits")
        rt_diff, rt_exp, rt_picked, rt_rank = sem("rt_diff"), sem("rt_expd"), sem("rt_pickd"), sem("rt_rankd")
        rt_dst, rt_table, scattered = sem("rt_dstd"), sem("rt_table"), sem("scattered")
        x_loaded = [sem("x_loaded0"), sem("x_loaded1")]
        xT_done, xh_ready, xl_ready = sem("xT_done"), sem("xh_ready"), sem("xl_ready")
        silu_done, hid_done = sem("silu_done"), sem("hid_done")
        hT_done, hh_ready, hl_ready = sem("hT_done"), sem("hh_ready"), sem("hl_ready")
        y_out, y_stored, y_final = sem("y_out"), sem("y_stored"), sem("y_final")
        y_back, combined = [sem("y_back0"), sem("y_back1")], sem("combined")
        over = [{k: sem(f"over{l}_{k}") for k in ("w", "x", "xT", "xTc", "ab", "silu", "hid", "hT", "hTc", "y",
                                                  "yc", "st")} for l in range(2)]

        def at_least(eng, s, n):
            if not isinstance(n, int) or n > 0:
                eng.wait_ge(s, n)

        RAW_BASE = [N_IN // 2 + N_OUT // 2] * 2 + [0]

        def raw_count(l, s, q):
            return RAW_BASE[s] + NE * l + q + 1

        def w_in_expert(l, name, e):
            w = A[name][l, bass.ds(e, 1)]
            return w.rearrange("o (k p) n -> p (o k) n", p=P)

        def moe_w_view(w, nk):
            return w.rearrange("p (k n) -> p k n", k=nk)

        def moe_sync(sp, l):
            m0, E0 = M_MOE[l], NE * l

            def load(name, e, j, slot):
                if isinstance(j, int) and j < 3:
                    if l == 0:
                        sp.wait_ge(wl_ready, m0)
                    else:
                        sp.wait_ge(at_weights_used, 1)
                else:
                    at_least(sp, wl_ready, m0 + j - 2)
                sp.dma_start(moe_w_view(raw[:, slot, :], KE if name == "moe_w2" else KD),
                             w_in_expert(l, name, e)).then_inc(raw_loaded[slot], 16)

            def load_x(e, par):
                row = sp.value_load(first_i[0:1, bass.ds(e, 1)], min_val=0, max_val=SLOTS)
                if not (isinstance(e, int) and e < 2):
                    at_least(sp, xT_done, E0 + e - 1)
                sp.dma_start(rows[0:CAP, par, :], xrows[bass.ds(row, CAP), :]).then_inc(x_loaded[par], 16)

            def store_y(e, par):
                row = sp.value_load(first_i[0:1, bass.ds(e, 1)], min_val=0, max_val=SLOTS)
                at_least(sp, y_stored, 16 * (E0 + e))
                if isinstance(e, int):
                    sp.wait_ge(y_out, E0 + e + 1)
                sp.dma_start(yrows[bass.ds(row, CAP), :], rows[0:CAP, 2 + par, :]).then_inc(y_stored, 16)

            load("moe_w1", 0, 0, 0)
            load("moe_w3", 0, 1, 1)
            load("moe_w1", 1, 2, 2)
            sp.wait_ge(scattered, 16 * 2 * TILES * (l + 1))
            sp.wait_ge(pad_written, 16)
            load_x(0, 0)
            load("moe_w3", 1, 3, 0)
            load("moe_w2", 0, 4, 1)
            load_x(1, 1)

            def of_expert(e, par):
                load("moe_w1", e, 3 * e - 1, 2)
                load_x(e, par)
                load("moe_w3", e, 3 * e, 0)
                if not (isinstance(e, int) and e < 4):
                    store_y(e - 4, par)
                load("moe_w2", e - 1, 3 * e + 1, 1)

            for e in range(2, 5):
                of_expert(e, e % 2)
            with sp.Fori(0, (NE - 6) // 2) as i:
                of_expert(2 * i + 5, 1)
                of_expert(2 * i + 6, 0)
            of_expert(NE - 1, 1)
            load("moe_w2", NE - 1, 3 * NE - 1, 2)
            for e in range(NE - 4, NE):
                store_y(e, e % 2)
            s = over[l]
            sp.wait_ge(y_stored, 16 * (E0 + NE))
            sp.wait_ge(wl_ready, m0 + 3 * NE)
            sp.wait_ge(rt_table, l + 1)
            n_over = sp.value_load(ovt_i[0:1, 7:8], min_val=0, max_val=EXTRA)
            sp.sem_inc(s["st"], 16)
            with sp.Fori(0, EXTRA) as i:
                with sp.If(n_over > i):
                    e = sp.value_load(ovt_i[0:1, bass.ds(i, 1)], min_val=0, max_val=NE - 1)
                    row = sp.value_load(ovt_i[0:1, bass.ds(i + 8, 1)], min_val=0, max_val=SLOTS)
                    at_least(sp, s["st"], 16 * i + 16)
                    sp.dma_start(rows[0:CAP, 0, :], xrows[bass.ds(row, CAP), :]).then_inc(s["x"], 16)
                    for slot, name in enumerate(("moe_w1", "moe_w3", "moe_w2")):
                        sp.dma_start(moe_w_view(raw[:, slot, :], KE if slot == 2 else KD),
                                     w_in_expert(l, name, e)).then_inc(s["w"], 16)
                    at_least(sp, s["yc"], i + 1)
                    sp.dma_start(yrows[bass.ds(row, CAP), :], rows[0:CAP, 2, :]).then_inc(s["st"], 16)
            at_least(sp, s["st"], 16 * n_over + 16)
            sp.sem_inc(y_final, 1)

        def experts(eng, step):
            for e in range(3):
                step(e, e % 2)
            with eng.Fori(0, (NE - 4) // 2) as i:
                step(2 * i + 3, 1)
                step(2 * i + 4, 0)
            step(NE - 1, 1)

        def is_first(e):
            return isinstance(e, int) and e == 0

        def is_last(e):
            return isinstance(e, int) and e == NE - 1

        def moe_pool(g, l):
            if l == 0:
                g.dma_start(xrows[SLOTS:ROWS], A["x_prompt"][0, 0:CAP, :]).then_inc(pad_written, 16)
                g.wait_ge(wl_ready, N_IN + N_OUT - 1)
            g.dma_start(gain[:], A["norm_ffn"][l:l + 1, :].partition_broadcast(P)).then_inc(ld_ffn, 16)
            g.wait_ge(rt_dst, l + 1)
            for t in range(TILES):
                for k in range(2):
                    g.indirect_dma_start(xrows[0:SLOTS], bass.IndirectOffsetOnAxis(ap=dst_i[:, 2 * t + k:2 * t + k + 1], axis=0),
                                         rows[:, t], None).then_inc(scattered, 16)
            g.wait_ge(y_final, l + 1)
            for t in range(TILES):
                if t == 2:
                    g.wait_ge(combined, TILES * l + 1)
                for k in range(2):
                    g.indirect_dma_start(rows[:, (2 * t + k) % 4], None, yrows[0:SLOTS],
                                         bass.IndirectOffsetOnAxis(ap=dst_i[:, 2 * t + k:2 * t + k + 1], axis=0)
                                         ).then_inc(y_back[t % 2], 16)

        def first_max(v, x, n, out, value, key):
            shape = [P, TILES, n]
            t_ = tmp[:, :, 0:n]
            w = const[:, C_RANKW:C_RANKW + n].unsqueeze(1).to_broadcast(shape)
            dve_link(v, nc.vector.tensor_reduce(value, x, AX.X, ALU.max))
            dve_link(v, nc.vector.tensor_tensor(t_, x, value.unsqueeze(2).to_broadcast(shape), ALU.is_equal))
            dve_link(v, nc.vector.tensor_tensor(t_, t_, w, ALU.mult))
            dve_link(v, nc.vector.tensor_reduce(key, t_, AX.X, ALU.max))
            dve_link(v, nc.vector.tensor_tensor(out, t_, key.unsqueeze(2).to_broadcast(shape), ALU.is_equal))

        def route_vector(v, l):
            v.wait_ge(ld_ffn, 16 * (l + 1))
            inverse_rms(v, rows[:, 3])
            for t in range(TILES):
                norm_rows(t, rows[:, t]).then_inc(rt_xn, 1)
            v.wait_ge(rt_logits, TILES * (l + 1))
            v.wait_ge(ld_route, 16 * 8)
            if l == 0:
                v.wait_ge(ld_const, 16)
            dve_link(v, nc.vector.tensor_tensor(logit[:], ps[:, BR, 0:96].rearrange("p (t c) -> p t c", t=TILES)[:, :, 0:NT],
                                                broute[:, l, :].unsqueeze(1).to_broadcast([P, TILES, NT]), ALU.add))
            lg, le = logit[:, :, 0:NG], logit[:, :, NG:NT]
            first_max(v, lg, NG, gsel[:], best[:, 0], best[:, 1])
            dve_link(v, nc.vector.tensor_tensor(ex[:, :, 0:NG], lg, best[:, 0].unsqueeze(2).to_broadcast([P, TILES, NG]),
                                                ALU.subtract))
            dve_link(v, nc.vector.tensor_scalar(pen[:], gsel[:], BIG, -BIG, ALU.mult, ALU.add))
            shape4 = [P, TILES, NG, EPG]
            lem4 = lem[:].rearrange("p t (g j) -> p t g j", g=NG)
            dve_link(v, nc.vector.tensor_tensor(lem4, le.rearrange("p t (g j) -> p t g j", g=NG),
                                                gsel[:].unsqueeze(3).to_broadcast(shape4), ALU.mult))
            dve_link(v, nc.vector.tensor_tensor(lem4, lem4, pen[:].unsqueeze(3).to_broadcast(shape4), ALU.add))
            first_max(v, lem[:], NE, pick[0][:], best[:, 2], best[:, 3])
            dve_link(v, nc.vector.scalar_tensor_tensor(lem[:], pick[0][:], -2 * BIG, lem[:], ALU.mult, ALU.add))
            first_max(v, lem[:], NE, pick[1][:], best[:, 4], best[:, 5])
            nc.vector.tensor_tensor(picked[:], pick[0][:], pick[1][:], ALU.add).then_inc(rt_picked, 1)
            nc.vector.tensor_tensor(ex[:, :, NG], best[:, 4], best[:, 2], ALU.subtract).then_inc(rt_diff, 1)
            v.wait_ge(rt_rank, l + 1)
            dve_link(v, nc.vector.tensor_copy(rank[:], ps[:, BR, 128:192].rearrange("p (t e) -> p t e", e=NE)))
            count = rank[:, TILES]
            dve_link(v, nc.vector.tensor_scalar(cat[:, 0:NE], count, float(CAP), None, ALU.min))
            dve_link(v, nc.vector.tensor_tensor(cat[:, NE:], count, cat[:, 0:NE], ALU.subtract))
            dve_link(v, nc.vector.tensor_tensor_scan(first[:], ones[:, 0:2 * NE], cat[:], 0.0, ALU.mult, ALU.add))
            dve_link(v, nc.vector.tensor_tensor(first[:], first[:], cat[:], ALU.subtract))
            shape = [P, TILES, NE]
            dve_link(v, nc.vector.tensor_tensor(ov[:, 0], first[:, NE:], first[:, 0:NE], ALU.subtract))
            dve_link(v, nc.vector.tensor_scalar(ov[:, 0], ov[:, 0], -float(CAP), None, ALU.add))
            dve_link(v, nc.vector.tensor_scalar(tmp[:], rank[:, 0:TILES], float(CAP), None, ALU.is_ge))
            dve_link(v, nc.vector.tensor_tensor(tmp[:], tmp[:], ov[:, 0:1].to_broadcast(shape), ALU.mult))
            dve_link(v, nc.vector.tensor_tensor(tmp[:], tmp[:], rank[:, 0:TILES], ALU.add))
            dve_link(v, nc.vector.tensor_tensor(tmp[:], tmp[:], first[:, 0:NE].unsqueeze(1).to_broadcast(shape), ALU.add))
            for k in range(2):
                dve_link(v, nc.vector.tensor_tensor(lem[:], pick[k][:], tmp[:], ALU.mult))
                dve_link(v, nc.vector.tensor_reduce(dst[:, :, k], lem[:], AX.X, ALU.add))
            dve_link(v, nc.vector.tensor_copy(first_i[:], first[:, 0:NE]))
            nc.vector.tensor_copy(dst_i[:], dst[:].rearrange("p t k -> p (t k)")).then_inc(rt_dst, 1)
            v.wait_ge(rt_exp, l + 1)
            dve_link(v, nc.vector.tensor_reduce(best[:, 0], ex[:, :, 0:NG], AX.X, ALU.add))
            dve_link(v, nc.vector.scalar_tensor_tensor(best[:, 1], ex[:, :, NG], 1.0, best[:, 0], ALU.add, ALU.mult))
            dve_link(v, nc.vector.reciprocal(wts[:, 0], best[:, 1]))
            dve_link(v, nc.vector.tensor_tensor(wts[:, 1], ex[:, :, NG], wts[:, 0], ALU.mult))
            o = ov[0:1]
            c0 = cat[0:1, NE:]
            dve_link(v, nc.vector.tensor_scalar(o[:, 1], c0, 0.0, None, ALU.is_gt))
            for n in range(1, (TOK - 1) // CAP):
                dve_link(v, nc.vector.tensor_scalar(o[:, 2], c0, float(n * CAP), None, ALU.is_gt))
                dve_link(v, nc.vector.tensor_tensor(o[:, 1], o[:, 1], o[:, 2], ALU.add))
            dve_link(v, nc.vector.tensor_tensor_scan(o[:, 2], ones[0:1, 0:NE], o[:, 1], 0.0, ALU.mult, ALU.add))
            dve_link(v, nc.vector.tensor_tensor(o[:, 1], o[:, 2], o[:, 1], ALU.subtract))
            bshape = [1, EXTRA, NE]
            it = const[0:1, C_IOTA:C_IOTA + EXTRA].unsqueeze(2).to_broadcast(bshape)
            nc.vector.tensor_copy(ovt[0:1, 7:8], o[:, 2, NE - 1:NE]).then_inc(dve_step, 1)
            steps["dve"] += 1
            dve_link(v, nc.vector.tensor_tensor(ovb[0:1], o[:, 1:2].to_broadcast(bshape), it, ALU.is_le))
            dve_link(v, nc.vector.tensor_tensor(ovb2[0:1], o[:, 2:3].to_broadcast(bshape), it, ALU.is_le))
            dve_link(v, nc.vector.tensor_tensor(ovb[0:1], ovb[0:1], ovb2[0:1], ALU.subtract))
            dve_link(v, nc.vector.tensor_tensor(ovb2[0:1], ovb[0:1], const[0:1, C_IOTA:C_IOTA + NE].unsqueeze(1).to_broadcast(bshape), ALU.mult))
            dve_link(v, nc.vector.tensor_reduce(ovt[0:1, 0:EXTRA], ovb2[0:1], AX.X, ALU.add))
            dve_link(v, nc.vector.scalar_tensor_tensor(o[:, 3], o[:, 1], -float(CAP), first[0:1, NE:], ALU.mult, ALU.add))
            dve_link(v, nc.vector.tensor_tensor(ovb2[0:1], ovb[0:1], o[:, 3:4].to_broadcast(bshape), ALU.mult))
            dve_link(v, nc.vector.tensor_reduce(ovt[0:1, 8:8 + EXTRA], ovb2[0:1], AX.X, ALU.add))
            dve_link(v, nc.vector.scalar_tensor_tensor(ovt[0:1, 8:8 + EXTRA], const[0:1, C_IOTA:C_IOTA + EXTRA], float(CAP),
                                                       ovt[0:1, 8:8 + EXTRA], ALU.mult, ALU.add))
            nc.vector.tensor_copy(ovt_i[0:1, 0:8 + EXTRA], ovt[0:1, 0:8 + EXTRA]).then_inc(rt_table, 1)

        def route_scalar(a, l):
            root(a, stat[:, 1, 0:TILES])
            for t in range(TILES):
                n = TILES * l + t
                a.wait_ge(rt_xT, n + 1)
                if t:
                    a.wait_ge(rt_logits, n)
                nc.scalar.activation(rows[:, 3].rearrange("p (b n) -> p b n", b=2), ps[:, BX:BX + 2], ACT.Copy
                                     ).then_inc(rt_xTc, 1)
            a.wait_ge(rt_diff, l + 1)
            nc.scalar.activation(ex[:], ex[:], ACT.Exp).then_inc(rt_exp, 1)

        def route_tensor(pe, l):
            if l == 0:
                pe.wait_ge(ld_route, 16 * 8)
            for t in range(TILES):
                n = TILES * l + t
                pe.wait_ge(rt_xn, n + 1)
                if t:
                    pe.wait_ge(rt_xTc, n)
                for k in range(KD):
                    last = nc.tensor.transpose(ps[:, BX + k // 4, (k % 4) * P:(k % 4 + 1) * P],
                                               rows[:, t, k * P:(k + 1) * P], ident)
                last.then_inc(rt_xT, 1)
                pe.wait_ge(rt_xTc, n + 1)
                for k in range(KD):
                    last = nc.tensor.matmul(ps[:, BR, 32 * t:32 * t + NT], rows[:, 3, k * P:(k + 1) * P],
                                            wroute[:, l, k, :], start=k == 0, stop=k == KD - 1)
                last.then_inc(rt_logits, 1)
            pe.wait_ge(rt_picked, l + 1)
            for t in range(TILES + 1):
                for s in range(min(t + 1, TILES)):
                    last = nc.tensor.matmul(ps[:, BR, 128 + t * NE:128 + (t + 1) * NE], upper if s == t else ones,
                                            picked[:, s], start=s == 0, stop=s == min(t, TILES - 1))
            last.then_inc(rt_rank, 1)

        def moe_split_h(a, l, j, slot, q):
            split_h(a, M_MOE[l] + j, slot, split_moe[slot][0], raw_count(l, slot, q),
                    M_MOE[l] + (0 if isinstance(j, int) and j < 3 else j - 2))

        def moe_split_l(v, l, j, slot):
            split_l(v, M_MOE[l] + j, slot, *split_moe[slot])

        def x_banks():
            return ps[:, BX:BX + 2, 0:4 * CAP].rearrange("p b (k t) -> p b k t", t=CAP)

        def x_part(x):
            return x[:].rearrange("p (b k) t -> p b k t", b=2)

        def moe_scalar(a, l):
            E0 = NE * l
            if l == 1:
                a.wait_ge(at_done, 1)
            for j in range(3):
                moe_split_h(a, l, j, j, 0)

            def x_high(e, par):
                a.wait_ge(xT_done, E0 + e + 1)
                nc.scalar.activation(x_part(xsplit[par][0]), x_banks(), ACT.Copy).then_inc(xh_ready, 1)

            def hidden_high(e):
                a.wait_ge(hT_done, E0 + e + 1)
                nc.scalar.activation(hth[:], ps[:, BH, 0:KE * CAP].rearrange("p (k t) -> p k t", t=CAP), ACT.Copy
                                     ).then_inc(hh_ready, 1)

            def y_copy(e, par):
                a.wait_ge(w_used, M_MOE[l] + (3 * NE if is_last(e) else 3 * e + 5))
                at_least(a, y_stored, 16 * (E0 + e - 1))
                nc.scalar.activation(rows[0:CAP, 2 + par].rearrange("p (b n) -> p b n", b=2), ps[0:CAP, BY:BY + 2],
                                     ACT.Copy).then_inc(y_out, 1)

            x_high(0, 0)

            def step(e, par):
                a.wait_ge(w_used, M_MOE[l] + (1 if is_first(e) else 3 * e))
                at_least(a, hid_done, E0 + e)
                nc.scalar.activation(sil[:], ps[0:CAP, BA], ACT.Silu).then_inc(silu_done, 1)
                if not is_first(e):
                    hidden_high(e - 1)
                if is_first(e):
                    moe_split_h(a, l, 3, 0, 1)
                else:
                    moe_split_h(a, l, 3 * e + 2, 2, e)
                if is_last(e):
                    y_copy(e - 1, 1 - par)
                    return
                x_high(e + 1, 1 - par)
                if is_first(e):
                    moe_split_h(a, l, 4, 1, 1)
                else:
                    moe_split_h(a, l, 3 * e + 3, 0, e + 1)
                    y_copy(e - 1, 1 - par)
                    moe_split_h(a, l, 3 * e + 4, 1, e + 1)

            experts(a, step)
            hidden_high(NE - 1)
            y_copy(NE - 1, 1)
            a.wait_ge(rt_table, l + 1)
            n_over = a.value_load(ovt_i[0:1, 7:8], min_val=0, max_val=EXTRA)
            s = over[l]
            with a.Fori(0, EXTRA) as i:
                with a.If(n_over > i):
                    a.wait_ge(s["xT"], i + 1)
                    nc.scalar.activation(rows[:, 1, 0:KD * CAP].rearrange("p (b k t) -> p b k t", b=2, t=CAP), x_banks(),
                                         ACT.Copy).then_inc(s["xTc"], 1)
                    a.wait_ge(s["ab"], i + 1)
                    nc.scalar.activation(sil[:], ps[0:CAP, BA], ACT.Silu).then_inc(s["silu"], 1)
                    a.wait_ge(s["hT"], i + 1)
                    nc.scalar.activation(rows[:, 3, 0:KE * CAP], ps[:, BH, 0:KE * CAP], ACT.Copy).then_inc(s["hTc"], 1)
                    a.wait_ge(s["y"], i + 1)
                    nc.scalar.activation(rows[0:CAP, 2].rearrange("p (b n) -> p b n", b=2), ps[0:CAP, BY:BY + 2],
                                         ACT.Copy).then_inc(s["yc"], 1)

        def moe_vector(v, l):
            E0 = NE * l
            for j in range(3):
                moe_split_l(v, l, j, j)

            def x_low(e, par):
                v.wait_ge(xh_ready, E0 + e + 1)
                nc.vector.tensor_tensor(x_part(xsplit[par][1]), x_banks(), x_part(xsplit[par][0]).bitcast(F32),
                                        ALU.subtract).then_inc(xl_ready, 1)

            def hidden_low(e):
                v.wait_ge(hh_ready, E0 + e + 1)
                nc.vector.tensor_tensor(htl[:], ps[:, BH, 0:KE * CAP].rearrange("p (k t) -> p k t", t=CAP),
                                        hth[:].bitcast(F32), ALU.subtract).then_inc(hl_ready, 1)

            x_low(0, 0)

            def step(e, par):
                if not is_first(e):
                    hidden_low(e - 1)
                moe_split_l(v, l, 3 if is_first(e) else 3 * e + 2, 0 if is_first(e) else 2)
                v.wait_ge(w_used, M_MOE[l] + (2 if is_first(e) else 3 * e + 1))
                v.wait_ge(silu_done, E0 + e + 1)
                nc.vector.tensor_tensor(hid[:], sil[:], ps[0:CAP, BB], ALU.mult).then_inc(hid_done, 1)
                if is_last(e):
                    return
                x_low(e + 1, 1 - par)
                if is_first(e):
                    moe_split_l(v, l, 4, 1)
                else:
                    moe_split_l(v, l, 3 * e + 3, 0)
                    moe_split_l(v, l, 3 * e + 4, 1)

            experts(v, step)
            hidden_low(NE - 1)
            n_over = v.value_load(ovt_i[0:1, 7:8], min_val=0, max_val=EXTRA)
            s = over[l]
            with v.Fori(0, EXTRA) as i:
                with v.If(n_over > i):
                    v.wait_ge(s["silu"], i + 1)
                    nc.vector.tensor_tensor(hid[:], sil[:], ps[0:CAP, BB], ALU.mult).then_inc(s["hid"], 1)
            for t in range(TILES):
                v.wait_ge(y_back[t % 2], 32 * ([2, 1][t % 2] * l + t // 2 + 1))
                dve_link(v, nc.vector.scalar_tensor_tensor(h[:, t], rows[:, (2 * t) % 4], wts[:, 0, t:t + 1], h[:, t],
                                                           ALU.mult, ALU.add))
                nc.vector.scalar_tensor_tensor(h[:, t], rows[:, (2 * t + 1) % 4], wts[:, 1, t:t + 1], h[:, t],
                                               ALU.mult, ALU.add).then_inc(combined, 1)
            v.wait_ge(combined, TILES * (l + 1))

        def moe_tensor(pe, l):
            E0, m0 = NE * l, M_MOE[l]

            def transpose_x(e, par):
                pe.wait_ge(x_loaded[par], 8 * (E0 + e - par) + 16)
                at_least(pe, xl_ready, E0 + e)
                for k in range(KD):
                    last = nc.tensor.transpose(ps[:, BX + k // 4, (k % 4) * CAP:(k % 4 + 1) * CAP],
                                               rows[0:CAP, par, k * P:(k + 1) * P], ident[0:CAP, 0:CAP])
                last.then_inc(xT_done, 1)

            def product_x(e, par, j, slot, bank):
                wh, wl = [moe_w_view(w[:], KD) for w in split_moe[slot]]
                xh, xl = xsplit[par]
                return split_product(pe, m0 + j, [[ps[0:CAP, bank]]], lambda t, k: xh[:, k], lambda t, k: xl[:, k],
                                     wh, wl, KD, 1)

            def transpose_hidden(e):
                pe.wait_ge(hid_done, E0 + e + 1)
                at_least(pe, hl_ready, E0 + e)
                for k in range(KE):
                    last = nc.tensor.transpose(ps[:, BH, k * CAP:(k + 1) * CAP], hid[:, k * P:(k + 1) * P],
                                               ident[0:CAP, 0:CAP])
                last.then_inc(hT_done, 1)

            def product_y(e, j, slot):
                pe.wait_ge(hl_ready, E0 + e + 1)
                at_least(pe, y_out, E0 + e)
                wh, wl = [moe_w_view(w[:], KE) for w in split_moe[slot]]
                split_product(pe, m0 + j, [[ps[0:CAP, BY], ps[0:CAP, BY + 1]]], lambda t, k: hth[:, k],
                              lambda t, k: htl[:, k], wh, wl, KE, 2).then_inc(w_used, 1)

            transpose_x(0, 0)

            def step(e, par):
                f = is_first(e)
                pe.wait_ge(xl_ready, E0 + e + 1)
                at_least(pe, silu_done, E0 + e)
                product_x(e, par, 0 if f else 3 * e - 1, 0 if f else 2, BA).then_inc(w_used, 1)
                if not f:
                    transpose_hidden(e - 1)
                at_least(pe, hid_done, E0 + e)
                product_x(e, par, 1 if f else 3 * e, 1 if f else 0, BB).then_inc(w_used, 1)
                if not is_last(e):
                    transpose_x(e + 1, 1 - par)
                if not f:
                    product_y(e - 1, 3 * e + 1, 1)

            experts(pe, step)
            transpose_hidden(NE - 1)
            product_y(NE - 1, 3 * NE - 1, 2)
            pe.wait_ge(rt_table, l + 1)
            n_over = pe.value_load(ovt_i[0:1, 7:8], min_val=0, max_val=EXTRA)
            s = over[l]
            with pe.Fori(0, EXTRA) as i:
                with pe.If(n_over > i):
                    pe.wait_ge(s["x"], 16 * i + 16)
                    pe.wait_ge(s["st"], 16 * i + 16)
                    for k in range(KD):
                        last = nc.tensor.transpose(ps[:, BX + k // 4, (k % 4) * CAP:(k % 4 + 1) * CAP],
                                                   rows[0:CAP, 0, k * P:(k + 1) * P], ident[0:CAP, 0:CAP])
                    last.then_inc(s["xT"], 1)
                    pe.wait_ge(s["xTc"], i + 1)
                    pe.wait_ge(s["w"], 48 * i + 48)
                    for bank, slot in ((BA, 0), (BB, 1)):
                        for k in range(KD):
                            last = nc.tensor.matmul(ps[0:CAP, bank], rows[:, 1, k * CAP:(k + 1) * CAP],
                                                    moe_w_view(raw[:, slot], KD)[:, k], start=k == 0, stop=k == KD - 1)
                    last.then_inc(s["ab"], 1)
                    pe.wait_ge(s["hid"], i + 1)
                    for k in range(KE):
                        last = nc.tensor.transpose(ps[:, BH, k * CAP:(k + 1) * CAP], hid[:, k * P:(k + 1) * P],
                                                   ident[0:CAP, 0:CAP])
                    last.then_inc(s["hT"], 1)
                    pe.wait_ge(s["hTc"], i + 1)
                    for c in range(2):
                        for k in range(KE):
                            last = nc.tensor.matmul(ps[0:CAP, BY + c], rows[:, 3, k * CAP:(k + 1) * CAP],
                                                    moe_w_view(raw[:, 2], KE)[:, k, c * 512:c * 512 + 512],
                                                    start=k == 0, stop=k == KE - 1)
                    last.then_inc(s["y"], 1)

        at = ExitStack()
        work = sb("at_work", [P, 4, D], F32, at)
        gain2 = sb("at_gain", [P, D], F32, at)
        c_sb = sb("at_c", [P, TILES, KVR + ROPE], F32, at)
        cq_sb = sb("at_cq", [P, TILES, QR], F32, at)
        q_sb = sb("at_q", [P, TILES, HEADS, QK], F32, at)
        kr = sb("at_krope", [P, TILES, ROPE], F32, at)
        rot = sb("at_rot", [P, 2, TILES * HEADS, ROPE // 2], F32, at)
        g_kva, g_kr = sb("at_g_kva", [P, KVR], F32, at), sb("at_g_kr", [P, ROPE], F32, at)
        g_qa, g_qr = sb("at_g_qa", [P, QR], F32, at), sb("at_g_qr", [P, ROPE], F32, at)
        g_qk = sb("at_g_qk", [QK, 2], F32, at)
        ast = sb("at_stat", [P, 64], F32, at)
        qT = sb("at_qT", [QK, TILES, HEADS, P], F32, at)
        cT = sb("at_cT", [P, 2, 2, P], F32, at)
        cqT = sb("at_cqT", [P, 3, P], F32, at)
        sq = sb("at_sq", [P, HEADS * NOPE], F32, at)
        kst = sb("at_kstat", [P, 2, HEADS], F32, at)
        kcat = sb("at_kcat", [P, 2, HEADS, QK], F32, at)
        cst = sb("at_cache_ckv", [P, 4, KVR], F32, at)
        ksr = sb("at_cache_krope", [P, 4, ROPE], F32, at)
        kTp, vp = sb("at_kTp", [QK, HEADS, SEQ], F32, at), sb("at_vp", [P, 2, HEADS * VD], F32, at)
        kT2, v2 = sb("at_kT2", [QK, HEADS, P], F32, at), sb("at_v2", [P, HEADS * VD], F32, at)
        KG_ = PAST + DECS
        kTg = sb("at_kTg", [QK, 2, HEADS, KG_], F32, at)
        vg = sb("at_vg", [P, 2, 2, HEADS * VD], F32, at)
        vnew = sb("at_vnew", [DECS, 2, HEADS * VD], F32, at)
        qz = sb("at_qz", [QK, 2, HEADS * (P + DECS)], F32, at)
        oT = sb("at_oT", [P, 4, TOK], F32, at)
        rmax = sb("at_rmax", [P, 2, HEADS], F32, at)
        rsum = sb("at_rsum", [P, 2, HEADS], F32, at)
        pTn = sb("at_pTn", [DECS, 2, P], F32, at)
        at.close()
        vscr = nc.dram_tensor("at_vnew_rows", (P, HEADS * VD), F32, kind="Internal").ap()
        p_sb = work[:, 0:2].rearrange("p a n -> p (a n)")
        pT = work[:, 2:4].rearrange("p a n -> p (a n)")
        w_dkv = raw[:, 0, 0:KD * 288].rearrange("p (k n) -> p k n", k=KD)
        w_dq = raw[:, 1, 0:KD * QR].rearrange("p (k n) -> p k n", k=KD)
        w_uv = raw[:, 1, KD * QR:].rearrange("p (k n) -> p k n", k=2)
        w_uq = raw[:, 2, 0:3 * 768].rearrange("p (k n) -> p k n", k=3)
        w_uk = raw[:, 2, 3 * 768:3 * 768 + 1024].rearrange("p (k n) -> p k n", k=2)
        w_o = raw[:, 0, :].rearrange("p (k n) -> p k n", k=4)

        ld_at, ld_atg, ld_kvg, ld_wo = sem("ld_at"), sem("ld_atg"), sem("ld_kvg"), sem("ld_wo")
        at_xn, at_xT, at_xc, at_proj, at_projc = map(sem, ["at_xn", "at_xTd", "at_xc", "at_proj", "at_projc"])
        at_lat, at_cqn, at_cqT, at_cqTc, at_qd, at_qc = map(
            sem, ["at_lat", "at_cqn", "at_cqTd", "at_cqTc", "at_qd", "at_qc"])
        at_qn, at_qT, at_qTc = sem("at_qn"), sem("at_qTd"), sem("at_qTc")
        at_T, at_cTc, at_kv, at_sq, at_red, at_ms, at_rt = map(
            sem, ["at_T", "at_cTc", "at_kv", "at_sqd", "at_red", "at_ms", "at_rt"])
        at_v, at_kcat, at_KT, at_kT = sem("at_v"), sem("at_kcatd"), sem("at_KT"), sem("at_kTd")
        at_qz, at_sc, at_p1, at_e, at_p2, at_PT, at_PTc, at_pv, at_o = map(
            sem, ["at_qzd", "at_sc", "at_p1", "at_e", "at_p2", "at_PT", "at_PTc", "at_pv", "at_o"])
        ld_c, ld_vn, vn_stored, lat_stored = sem("ld_c"), sem("ld_vn"), sem("vn_stored"), sem("lat_stored")
        at_y, at_done, at_weights_used = sem("at_y"), sem("at_done"), sem("at_weights_used")
        GROUPS = DECB // 2
        NEW = TILES
        QTILES = 2

        def at_sync(sp):
            sp.dma_start(w_dkv, A["w_dkv"].rearrange("(k p) n -> p k n", p=P)).then_inc(ld_at, 16)
            sp.dma_start(w_dq, A["w_dq"][0].rearrange("(k p) n -> p k n", p=P)).then_inc(ld_at, 16)
            sp.dma_start(w_uq, A["w_uq"][0].rearrange("(k p) h n -> p k (h n)", p=P)).then_inc(ld_at, 16)
            sp.dma_start(w_uk, A["w_uk"].rearrange("(k p) h n -> p k (h n)", p=P)).then_inc(ld_at, 16)
            sp.dma_start(w_uv, A["w_uv"].rearrange("(k p) h n -> p k (h n)", p=P)).then_inc(ld_at, 16)
            sp.wait_ge(at_proj, TILES)
            sp.dma_start(w_o, A["w_o"][0].rearrange("(k p) n -> p k n", p=P)).then_inc(ld_wo, 16)
            ckv_rows = A["cache_ckv"].rearrange("b (t p) r -> p (b t) r", p=P)
            kr_rows = A["cache_krope"].rearrange("b (t p) r -> p (b t) r", p=P)

            def load_cache(g):
                sp.dma_start(cst[:], ckv_rows[:, bass.ds(4 * g, 4), :]).then_inc(ld_c, 16)
                sp.dma_start(ksr[:], kr_rows[:, bass.ds(4 * g, 4), :]).then_inc(ld_c, 16)

            def load_vnew(g):
                sp.dma_start(vnew[:], vscr[bass.ds(2 * DECS * g, 2 * DECS), :].rearrange("(b q) n -> q b n", b=2)
                             ).then_inc(ld_vn, 16)

            load_cache(0)
            sp.wait_ge(vn_stored, 16)
            load_vnew(0)
            with sp.Fori(1, GROUPS) as g:
                sp.wait_ge(at_kcat, 2 * NEW + 8 * g)
                load_cache(g)
                sp.wait_ge(at_pv, QTILES + g)
                load_vnew(g)

        def at_pool(g):
            g.wait_ge(combined, TILES)
            g.dma_start(gain[:], A["kv_norm"].rearrange("(a n) -> a n", a=1).partition_broadcast(P)).then_inc(ld_kvg, 16)
            g.dma_start(gain2[:], A["norm_mix"][1:2, :].partition_broadcast(P)).then_inc(ld_kvg, 16)
            g.dma_start(g_kva[:], A["kv_a_norm"].rearrange("(a n) -> a n", a=1).partition_broadcast(P)).then_inc(ld_atg, 16)
            g.dma_start(g_kr[:], A["k_rope_norm"].rearrange("(a n) -> a n", a=1).partition_broadcast(P)).then_inc(ld_atg, 16)
            g.dma_start(g_qa[:], A["q_a_norm"].partition_broadcast(P)).then_inc(ld_atg, 16)
            g.dma_start(g_qr[:], A["q_rope_norm"].partition_broadcast(P)).then_inc(ld_atg, 16)
            g.dma_start(g_qk[0:NOPE, 0:1], A["q_nope_norm"][0].rearrange("(n a) -> n a", a=1),
                        allow_slow_non_contiguous=True).then_inc(ld_atg, 16)
            g.dma_start(g_qk[0:NOPE, 1:2], A["k_nope_norm"].rearrange("(n a) -> n a", a=1),
                        allow_slow_non_contiguous=True).then_inc(ld_atg, 16)
            g.wait_ge(at_lat, 1)
            for t in range(2):
                g.dma_start(O[2][0, t * P:(t + 1) * P, :], c_sb[:, t, 0:KVR]).then_inc(lat_stored, 16)
                g.dma_start(O[3][0, t * P:(t + 1) * P, :], kr[:, t, :]).then_inc(lat_stored, 16)
            g.dma_start(O[4].rearrange("b s r -> (b s) r"), c_sb[:, SAMPLE, 0:KVR]).then_inc(lat_stored, 16)
            g.dma_start(O[5].rearrange("b s r -> (b s) r"), kr[:, SAMPLE, :]).then_inc(lat_stored, 16)
            g.wait_ge(at_v, NEW)
            g.dma_start(vscr[:, :], v2[:]).then_inc(vn_stored, 16)

        def normalise(v, x, parts):
            for a, b, st in parts:
                n, w = x.shape[1], b - a
                s3 = [P, n, w]
                j = work[:, 0:4].rearrange("p a n -> p (a n)")[:, 0:n * w].rearrange("p (n w) -> p n w", n=n)
                dve_link(v, nc.vector.tensor_tensor(j, x[:, :, a:b], x[:, :, a:b], ALU.mult))
                dve_link(v, nc.vector.tensor_reduce(st, j, AX.X, ALU.add))
                dve_link(v, nc.vector.tensor_scalar(st, st, 1.0 / w, None, ALU.mult))

        def scale_rows(v, x, a, b, st, gain_row=None):
            shape = [P, x.shape[1], b - a]
            dve_link(v, nc.vector.tensor_tensor(x[:, :, a:b], x[:, :, a:b], st.unsqueeze(2).to_broadcast(shape), ALU.mult))
            if gain_row is not None:
                dve_link(v, nc.vector.tensor_tensor(x[:, :, a:b], x[:, :, a:b],
                                                    gain_row.unsqueeze(1).to_broadcast(shape), ALU.mult))

        def rotate(v, x, out, cos, sin, shape):
            half = ROPE // 2
            x1, x2 = x[..., 0:half], x[..., half:ROPE]
            n = 1
            for s in shape[1:-1]:
                n *= s
            r = [rot[:, i, 0:n] if len(shape) == 3 else rot[:, i, 0:n].rearrange("p (t h) c -> p t h c", h=HEADS)
                 for i in range(2)]
            dve_link(v, nc.vector.tensor_tensor(r[0], x1, sin, ALU.mult))
            dve_link(v, nc.vector.tensor_tensor(r[1], x2, sin, ALU.mult))
            dve_link(v, nc.vector.tensor_tensor(out[..., 0:half], x1, cos, ALU.mult))
            dve_link(v, nc.vector.tensor_tensor(out[..., half:ROPE], x2, cos, ALU.mult))
            dve_link(v, nc.vector.tensor_tensor(out[..., 0:half], out[..., 0:half], r[1], ALU.subtract))
            dve_link(v, nc.vector.tensor_tensor(out[..., half:ROPE], out[..., half:ROPE], r[0], ALU.add))

        def at_vector(v):
            v.wait_ge(ld_kvg, 32)
            inverse_rms(v, work[:, 0])
            for t in range(TILES):
                if t:
                    v.wait_ge(at_xT, 2 * t)
                norm_rows(t, work[:, 0]).then_inc(at_xn, 1)
                nc.vector.scalar_tensor_tensor(work[:, 1], h[:, t], stat[:, 1, t:t + 1], gain2[:], ALU.mult, ALU.mult
                                               ).then_inc(at_xn, 1)
            dve_link(v, nc.vector.memset(qz[:], 0.0))
            dve_link(v, nc.vector.memset(g_qk[NOPE:QK, :], 1.0))
            v.wait_ge(ld_atg, 96)
            v.wait_ge(at_projc, 2 * TILES)
            c_all, cq_all = c_sb[:], cq_sb[:]
            normalise(v, c_all, [(0, KVR, ast[:, 0:3]), (KVR, KVR + ROPE, ast[:, 3:6])])
            normalise(v, cq_all, [(0, QR, ast[:, 6:9])])
            rms_inverse(v, ast[:, 0:9], ast[:, 0:9], 1.0)
            scale_rows(v, cq_all, 0, QR, ast[:, 6:9], g_qa[:])
            nc.vector.memset(ast[:, 60:61], 0.0).then_inc(at_cqn, 1)
            scale_rows(v, c_all, 0, KVR, ast[:, 0:3], g_kva[:])
            scale_rows(v, c_all, KVR, KVR + ROPE, ast[:, 3:6], g_kr[:])
            cos3 = const[:, C_COS:C_COS + 48].rearrange("p (t c) -> p t c", t=TILES)
            sin3 = const[:, C_SIN:C_SIN + 48].rearrange("p (t c) -> p t c", t=TILES)
            rotate(v, c_sb[:, :, KVR:], kr[:], cos3, sin3, [P, TILES, 16])
            nc.vector.memset(ast[:, 61:62], 0.0).then_inc(at_lat, 1)
            for n in range(NEW):
                key_rows(v, n, n % 2, kr[:, n])
            v.wait_ge(at_qc, TILES)
            q24 = q_sb[:].rearrange("p t h n -> p (t h) n")
            normalise(v, q24, [(0, NOPE, ast[:, 10:34]), (NOPE, QK, ast[:, 34:58])])
            rms_inverse(v, ast[:, 10:58], ast[:, 10:58], 1.0)
            scale_rows(v, q24, 0, NOPE, ast[:, 10:34])
            scale_rows(v, q24, NOPE, QK, ast[:, 34:58], g_qr[:])
            shape = [P, TILES, HEADS, 16]
            qr_ = q_sb[:, :, :, NOPE:QK]
            tmpq = work[:, 0, 0:TILES * HEADS * ROPE].rearrange("p (t h c) -> p t h c", t=TILES, h=HEADS)
            rotate(v, qr_, tmpq, cos3.unsqueeze(2).to_broadcast(shape), sin3.unsqueeze(2).to_broadcast(shape), shape)
            nc.vector.tensor_copy(qr_, tmpq).then_inc(at_qn, 1)
            for t in range(2):
                prompt_softmax(v, t)
            with v.Fori(0, GROUPS) as g:
                for i in range(4):
                    if i == 0:
                        v.wait_ge(ld_c, 32 * g + 32)
                    key_rows(v, NEW + 4 * g + i, (i + 1) % 2, ksr[:, i])
                sample_softmax(v, g)
            v.wait_ge(at_y, 1)
            v.wait_ge(lat_stored, 96)
            for t in range(TILES):
                dve_link(v, nc.vector.tensor_tensor(h[:, t].rearrange("p (c n) -> p c n", c=2),
                                                    h[:, t].rearrange("p (c n) -> p c n", c=2),
                                                    ps[:, 2 * t:2 * t + 2], ALU.add))
            nc.vector.memset(stat[:, 0, 3:4], 0.0).then_inc(at_done, 1)

        def key_rows(v, n, par, rope_rows):
            k3 = ps[:, 1 + par].rearrange("p (h d) -> p h d", h=HEADS)
            v.wait_ge(at_sq, n + 1)
            nc.vector.tensor_reduce(kst[:, par], sq[:].rearrange("p (h d) -> p h d", h=HEADS), AX.X, ALU.add
                                    ).then_inc(at_red, 1)
            v.wait_ge(at_red, n + 1)
            nc.vector.tensor_scalar(kst[:, par], kst[:, par], 1.0 / NOPE, EPS, ALU.mult, ALU.add).then_inc(at_ms, 1)
            v.wait_ge(at_rt, 2 * n + 1)
            nc.vector.reciprocal(kst[:, par], kst[:, par]).then_inc(at_rt, 1)
            if not (isinstance(n, int) and n < 2):
                v.wait_ge(at_KT, n - 1)
            nc.vector.tensor_copy(kcat[:, par, :, NOPE:], rope_rows.unsqueeze(1).to_broadcast([P, HEADS, ROPE])
                                  ).then_inc(at_kcat, 1)
            v.wait_ge(at_rt, 2 * n + 2)
            nc.vector.tensor_tensor(kcat[:, par, :, 0:NOPE], k3, kst[:, par].unsqueeze(2).to_broadcast([P, HEADS, NOPE]),
                                    ALU.mult).then_inc(at_kcat, 1)

        def at_most_units(v, U, x, shape, n_max):
            hd = shape[1]
            m, s = rmax[:, 0, 0:hd], rsum[:, 0, 0:hd]
            nc.vector.tensor_reduce(m, x, AX.X, ALU.max).then_inc(at_p2x, 1)
            v.wait_ge(at_p2x, 3 * U + 1)
            nc.vector.tensor_tensor(x, x, m.unsqueeze(2).to_broadcast(shape), ALU.subtract).then_inc(at_p1, 1)
            v.wait_ge(at_e, U + 1)
            nc.vector.tensor_reduce(s, x, AX.X, ALU.add).then_inc(at_p2x, 1)
            v.wait_ge(at_p2x, 3 * U + 2)
            nc.vector.reciprocal(s, s).then_inc(at_p2x, 1)
            v.wait_ge(at_p2x, 3 * U + 3)
            nc.vector.tensor_tensor(x, x, s.unsqueeze(2).to_broadcast(shape), ALU.mult).then_inc(at_p2, 1)

        at_p2x, at_ps = sem("at_p2x"), sem("at_ps")

        def prompt_softmax(v, t):
            nk = (t + 1) * P
            p3 = p_sb.rearrange("p (h k) -> p h k", h=HEADS)
            s3 = ps[:, 0:4].rearrange("p b (h k) -> p (b h) k", h=2)
            v.wait_ge(at_sc, t + 1)
            if t:
                v.wait_ge(at_PT, t)
            else:
                v.wait_ge(at_qT, TILES)
            if t:
                nc.vector.tensor_scalar(p3[:, :, 0:P], s3[:, :, 0:P], SCALE, None, ALU.mult).then_inc(at_ps, 1)
            own = slice(t * P, (t + 1) * P)
            nc.vector.scalar_tensor_tensor(p3[:, :, own], s3[:, :, own], SCALE,
                                           const[:, C_MASK:C_MASK + P].unsqueeze(1).to_broadcast([P, HEADS, P]),
                                           ALU.mult, ALU.add).then_inc(at_ps, 1)
            v.wait_ge(at_ps, [1, 3][t])
            at_most_units(v, t, p3[:, :, 0:nk], [P, HEADS, nk], nk)
            v.wait_ge(at_pv, t + 1)
            o3 = ps[:, 6:8].rearrange("p b (h x q) -> p (b h) x q", h=2, x=2)
            nc.vector.tensor_copy(oT[0:VD, :, t * P:(t + 1) * P], o3[0:VD, :, 0]).then_inc(at_ox, 1)
            nc.vector.tensor_copy(oT[VD:P, :, t * P:(t + 1) * P], o3[VD:P, :, 1]).then_inc(at_ox, 1)
            v.wait_ge(at_ox, 2 * t + 2)
            nc.vector.memset(ast[:, 62:63], 0.0).then_inc(at_o, 1)

        at_ox = sem("at_ox")

        def sample_softmax(v, g):
            U = QTILES + g
            v.wait_ge(at_sc, U)
            for b in range(2):
                src = qT[:, SAMPLE, :, bass.ds(2 * DECS * g + DECS * b, DECS)]
                nc.vector.tensor_copy(qz[:, b].rearrange("p (h c) -> p h c", h=HEADS)[:, :, 0:DECS], src).then_inc(at_qz, 1)
                nc.vector.tensor_copy(kTg[:, b, :, PAST:], kT2[:, :, bass.ds(2 * DECS * g + DECS * b, DECS)]
                                      ).then_inc(at_qz, 1)
            v.wait_ge(at_sc, U + 1)
            p3 = p_sb[:, 0:2 * KG_].rearrange("p (b k) -> p b k", b=2)
            nc.vector.tensor_scalar(p3, ps[:, 6:8, 0:KG_], SCALE, None, ALU.mult).then_inc(at_ps, 1)
            v.wait_ge(at_ps, g + 4)
            at_most_units(v, U, p3, [P, 2, KG_], KG_)
            v.wait_ge(at_pv, U + 1)
            o4 = ps[:, 2, 0:256].rearrange("p (b h x q) -> p h b x q", b=2, h=4, x=2)
            for x in range(2):
                dst_o = oT[x * VD:(x + 1) * VD, :, bass.ds(SEQ + 2 * DECS * g, 2 * DECS)]
                nc.vector.tensor_copy(dst_o.rearrange("p h (b q) -> p h b q", b=2), o4[x * VD:(x + 1) * VD, :, :, x]
                                      ).then_inc(at_ox, 1)
            v.wait_ge(at_ox, 2 * U + 2)
            nc.vector.memset(ast[:, 62:63], 0.0).then_inc(at_o, 1)

        def at_scalar(a):
            root(a, stat[:, 1, 0:TILES])
            for t in range(TILES):
                for i in range(2):
                    a.wait_ge(at_xT, 2 * t + i + 1)
                    if t:
                        a.wait_ge(at_proj, t)
                    nc.scalar.activation(work[:, 2 + i].rearrange("p (b n) -> p b n", b=2), ps[:, 2 * i:2 * i + 2],
                                         ACT.Copy).then_inc(at_xc, 1)
                a.wait_ge(at_proj, t + 1)
                nc.scalar.activation(c_sb[:, t], ps[:, 4, 0:KVR + ROPE], ACT.Copy).then_inc(at_projc, 1)
                nc.scalar.activation(cq_sb[:, t], ps[:, 5, 0:QR], ACT.Copy).then_inc(at_projc, 1)
            root(a, ast[:, 0:9])
            for t in range(TILES):
                a.wait_ge(at_cqT, t + 1)
                if t:
                    a.wait_ge(at_qd, t)
                nc.scalar.activation(cqT[:], ps[:, 6, 0:QR].rearrange("p (k t) -> p k t", k=3), ACT.Copy).then_inc(at_cqTc, 1)
                a.wait_ge(at_qd, t + 1)
                nc.scalar.activation(q_sb[:, t].rearrange("p (b h) n -> p b (h n)", b=2), ps[:, 4:6, 0:QR], ACT.Copy
                                     ).then_inc(at_qc, 1)
            key_tiles(a, 0, list(range(NEW)), [n % 2 for n in range(NEW)],
                      [kTp[:, :, 0:P], kTp[:, :, P:SEQ], kT2[:]], [vp[:, 0], vp[:, 1], v2[:]])
            root(a, ast[:, 10:58])
            for t in range(TILES):
                a.wait_ge(at_qT, t + 1)
                nc.scalar.activation(qT[:, t].rearrange("p (b h) n -> p b (h n)", b=2), ps[0:QK, 0:2], ACT.Copy,
                                     scale=g_qk[:, 0:1]).then_inc(at_qTc, 1)
            for t in range(2):
                n = (t + 1) * P
                probabilities(a, t, p_sb.rearrange("p (h k) -> p h k", h=HEADS)[:, :, 0:n])
                for c in range(t + 1):
                    a.wait_ge(at_PTx, [0, 1][t] + c + 1)
                    nc.scalar.activation(pT.rearrange("p (c h q) -> p c h q", c=2, h=HEADS)[:, c].rearrange("p (b h) q -> p b (h q)", b=2),
                                         ps[:, 4:6], ACT.Copy).then_inc(at_PTc, 1)
            with a.Fori(0, GROUPS) as g:
                U = QTILES + g
                a.wait_ge(at_pv, U)
                a.nop()
                key_tiles(a, g, [NEW + 4 * g + i for i in range(4)], [(i + 1) % 2 for i in range(4)],
                          [kTg[:, i // 2, :, (i % 2) * P:(i % 2 + 1) * P] for i in range(4)],
                          [vg[:, i // 2, i % 2] for i in range(4)])
                probabilities(a, U, p_sb[:, 0:2 * KG_].rearrange("p (b k) -> p b k", b=2))
                a.wait_ge(at_PT, U + 1)
                nc.scalar.activation(pT[:, 0:512].rearrange("p (b n) -> p b n", b=2), ps[:, 0:2, 0:256], ACT.Copy
                                     ).then_inc(at_PTc, 1)
                nc.scalar.activation(pTn[:], ps[0:DECS, 0:2, 256:384], ACT.Copy).then_inc(at_PTc, 1)

        at_PTx = sem("at_PTx")

        def probabilities(a, U, x):
            a.wait_ge(at_p1, U + 1)
            nc.scalar.activation(x, x, ACT.Exp).then_inc(at_e, 1)

        def key_tiles(a, g, ns, pars, kdst, vdst):
            def c_copy(i):
                n, par = ns[i], pars[i]
                if not (isinstance(n, int) and n < 2):
                    a.wait_ge(at_kv, n - 1)
                a.wait_ge(at_T, n + 1)
                nc.scalar.activation(cT[:, par], ps[:, 0, 0:256].rearrange("p (k t) -> p k t", k=2), ACT.Copy
                                     ).then_inc(at_cTc, 1)

            def kT_copy(i):
                a.wait_ge(at_KT, ns[i] + 1)
                d = kdst[i].rearrange("p (b h) n -> p b h n", b=2)
                nc.scalar.activation(d, ps[0:QK, 4:6].rearrange("p b (h n) -> p b h n", h=4), ACT.Copy,
                                     scale=g_qk[:, 1:2]).then_inc(at_kT, 1)

            c_copy(0)
            for i, n in enumerate(ns):
                par = pars[i]
                if i + 1 < len(ns):
                    c_copy(i + 1)
                a.wait_ge(at_kv, n + 1)
                nc.scalar.activation(vdst[i], ps[:, 3], ACT.Copy).then_inc(at_v, 1)
                at_least(a, at_red, n)
                nc.scalar.activation(sq[:], ps[:, 1 + par], ACT.Square).then_inc(at_sq, 1)
                if i:
                    kT_copy(i - 1)
                a.wait_ge(at_ms, n + 1)
                nc.scalar.activation(kst[:, par], kst[:, par], ACT.Sqrt).then_inc(at_rt, 1)
            kT_copy(len(ns) - 1)

        def at_tensor(pe):
            pe.wait_ge(ld_at, 80)
            for t in range(TILES):
                for i in range(2):
                    pe.wait_ge(at_xn, 2 * t + i + 1)
                    if t:
                        pe.wait_ge(at_xc, 2 * t)
                    for k in range(KD):
                        last = nc.tensor.transpose(ps[:, 2 * i + k // 4, (k % 4) * P:(k % 4 + 1) * P],
                                                   work[:, i, k * P:(k + 1) * P], ident)
                    last.then_inc(at_xT, 1)
                at_least(pe, at_projc, 2 * t)
                pe.wait_ge(at_xc, 2 * t + 2)
                for i, (w, n) in enumerate(((w_dkv, KVR + ROPE), (w_dq, QR))):
                    for k in range(KD):
                        last = nc.tensor.matmul(ps[:, 4 + i, 0:n], work[:, 2 + i, k * P:(k + 1) * P], w[:, k],
                                                start=k == 0, stop=k == KD - 1)
                last.then_inc(at_proj, 1)
            pe.wait_ge(at_cqn, 1)
            pe.wait_ge(at_projc, 2 * TILES)
            for t in range(TILES):
                if t:
                    pe.wait_ge(at_cqTc, t)
                for k in range(3):
                    last = nc.tensor.transpose(ps[:, 6, k * P:(k + 1) * P], cq_sb[:, t, k * P:(k + 1) * P], ident)
                last.then_inc(at_cqT, 1)
                pe.wait_ge(at_cqTc, t + 1)
                if t:
                    pe.wait_ge(at_qc, t)
                for c in range(2):
                    for k in range(3):
                        last = nc.tensor.matmul(ps[:, 4 + c, 0:QR], cqT[:, k], w_uq[:, k, c * QR:(c + 1) * QR],
                                                start=k == 0, stop=k == 2)
                last.then_inc(at_qd, 1)
            pe.wait_ge(at_lat, 1)
            pe.wait_ge(at_qc, TILES)
            expand(pe, list(range(NEW)), [n % 2 for n in range(NEW)], [c_sb[:, n, 0:KVR] for n in range(NEW)])
            pe.wait_ge(at_qn, 1)
            for t in range(TILES):
                at_least(pe, at_qTc, t)
                for hh in range(HEADS):
                    last = nc.tensor.transpose(ps[0:QK, hh // 4, (hh % 4) * P:(hh % 4 + 1) * P], q_sb[:, t, hh], ident)
                last.then_inc(at_qT, 1)
            pe.wait_ge(at_qTc, TILES)
            pe.wait_ge(at_kT, NEW)
            for t in range(2):
                for hh in range(HEADS):
                    last = nc.tensor.matmul(ps[:, hh // 2, (hh % 2) * SEQ:(hh % 2) * SEQ + (t + 1) * P],
                                            qT[:, t, hh], kTp[:, hh, 0:(t + 1) * P], start=True, stop=True)
                last.then_inc(at_sc, 1)
                pe.wait_ge(at_p2, t + 1)
                for c in range(t + 1):
                    if c or t:
                        pe.wait_ge(at_PTc, [0, 1][t] + c)
                    for hh in range(HEADS):
                        last = nc.tensor.transpose(ps[:, 4 + hh // 4, (hh % 4) * P:(hh % 4 + 1) * P],
                                                   p_sb[:, hh * SEQ + c * P:hh * SEQ + (c + 1) * P], ident)
                    last.then_inc(at_PTx, 1)
                pe.wait_ge(at_PTc, [1, 3][t])
                at_least(pe, at_o, t)
                pe.nop().then_inc(at_PT, 1)
                for hp in range(HEADS // 2):
                    for c in range(t + 1):
                        last = nc.tensor.matmul(ps[:, 6 + hp // 2, (hp % 2) * 256:(hp % 2) * 256 + 256],
                                                vp[:, c, hp * P:(hp + 1) * P],
                                                pT[:, c * D + hp * 256:c * D + hp * 256 + 256], start=c == 0, stop=c == t)
                last.then_inc(at_pv, 1)
            pe.wait_ge(ld_wo, 16)
            with pe.Fori(0, GROUPS) as g:
                U = QTILES + g
                pe.wait_ge(ld_c, 32 * g + 32)
                pe.wait_ge(at_o, U)
                expand(pe, [NEW + 4 * g + i for i in range(4)], [(i + 1) % 2 for i in range(4)],
                       [cst[:, i] for i in range(4)])
                pe.wait_ge(at_kT, NEW + 4 * g + 4)
                pe.wait_ge(at_qz, 4 * g + 4)
                for b in range(2):
                    for hh in range(HEADS):
                        last = nc.tensor.matmul(ps[:, 6 + b, 0:KG_], qz[:, b, hh * P:(hh + 1) * P], kTg[:, b, hh],
                                                start=hh == 0, stop=hh == HEADS - 1)
                last.then_inc(at_sc, 1)
                pe.wait_ge(at_p2, U + 1)
                for b in range(2):
                    for c in range(3):
                        n = DECS if c == 2 else P
                        last = nc.tensor.transpose(ps[0:n, b, c * P:(c + 1) * P],
                                                   p_sb[:, b * KG_ + c * P:b * KG_ + c * P + n], ident)
                last.then_inc(at_PT, 1)
                pe.wait_ge(at_PTc, 2 * g + 5)
                pe.wait_ge(ld_vn, 16 * g + 16)
                for b in range(2):
                    for hp in range(HEADS // 2):
                        out = ps[:, 2, (b * 4 + hp) * 32:(b * 4 + hp) * 32 + 32]
                        for c in range(3):
                            vv_ = vnew[:, b, hp * P:(hp + 1) * P] if c == 2 else vg[:, b, c, hp * P:(hp + 1) * P]
                            pp = pTn[:, b, hp * 32:hp * 32 + 32] if c == 2 else pT[:, b * 256 + c * P + hp * 32:b * 256 + c * P + hp * 32 + 32]
                            last = nc.tensor.matmul(out, vv_, pp, start=c == 0, stop=c == 2)
                last.then_inc(at_pv, 1)
            pe.wait_ge(at_o, QTILES + GROUPS)
            for t in range(TILES):
                for c in range(2):
                    for k in range(4):
                        last = nc.tensor.matmul(ps[:, 2 * t + c], oT[:, k, t * P:(t + 1) * P],
                                                w_o[:, k, c * 512:c * 512 + 512], start=k == 0, stop=k == 3)
            last.then_inc(at_y, 1)
            pe.wait_ge(at_y, 1)
            pe.nop().then_inc(at_weights_used, 1)

        def expand(pe, ns, pars, src):
            def turn(i):
                at_least(pe, at_cTc, ns[i])
                for k in range(2):
                    last = nc.tensor.transpose(ps[:, 0, k * P:(k + 1) * P], src[i][:, k * P:(k + 1) * P], ident)
                last.then_inc(at_T, 1)

            def turn_keys(i):
                n = ns[i]
                pe.wait_ge(at_kcat, 2 * n + 2)
                at_least(pe, at_kT, n)
                for hh in range(HEADS):
                    last = nc.tensor.transpose(ps[0:QK, 4 + hh // 4, (hh % 4) * P:(hh % 4 + 1) * P],
                                               kcat[:, pars[i], hh], ident)
                last.then_inc(at_KT, 1)

            turn(0)
            for i, n in enumerate(ns):
                if i + 1 < len(ns):
                    turn(i + 1)
                pe.wait_ge(at_cTc, n + 1)
                at_least(pe, at_v, n)
                if not (isinstance(n, int) and n < 2):
                    pe.wait_ge(at_kcat, 2 * n - 2)
                for k in range(2):
                    nc.tensor.matmul(ps[:, 1 + pars[i]], cT[:, pars[i], k], w_uk[:, k], start=k == 0, stop=k == 1)
                for k in range(2):
                    last = nc.tensor.matmul(ps[:, 3], cT[:, pars[i], k], w_uv[:, k], start=k == 0, stop=k == 1)
                last.then_inc(at_kv, 1)
                if i:
                    turn_keys(i - 1)
            turn_keys(len(ns) - 1)

        out_stored = sem("out_stored")
        block = top.enter_context(nc.Block())

        @block.sync
        def _(sp):
            gm_sync(sp)
            moe_sync(sp, 0)
            at_sync(sp)
            moe_sync(sp, 1)
            sp.wait_ge(combined, 2 * TILES)
            sp.dma_start(O[0][0].rearrange("(t p) d -> p t d", p=P), h[:, 0:2]).then_inc(out_stored, 16)
            sp.dma_start(O[1].rearrange("b s d -> (b s) d"), h[:, SAMPLE]).then_inc(out_stored, 16)
            sp.wait_ge(out_stored, 32)
            sp.wait_ge(v_stored, 16)
            sp.wait_ge(lat_stored, 96)

        @block.gpsimd
        def _(g):
            gm_pool(g)
            moe_pool(g, 0)
            at_pool(g)
            moe_pool(g, 1)

        @block.scalar
        def _(a):
            gm_scalar(a)
            route_scalar(a, 0)
            moe_scalar(a, 0)
            at_scalar(a)
            route_scalar(a, 1)
            moe_scalar(a, 1)

        @block.vector
        def _(v):
            gm_vector(v)
            route_vector(v, 0)
            moe_vector(v, 0)
            at_vector(v)
            route_vector(v, 1)
            moe_vector(v, 1)

        @block.tensor
        def _(pe):
            gm_tensor(pe)
            route_tensor(pe, 0)
            moe_tensor(pe, 0)
            at_tensor(pe)
            route_tensor(pe, 1)
            moe_tensor(pe, 1)


_INS = ['x_prompt', 'x_sample', 'cache_ckv', 'cache_krope', 'norm_mix', 'norm_ffn', 'gm_w_in', 'gm_b_in', 'gm_ln_g',
        'gm_ln_b', 'gm_w_s', 'gm_b_s', 'gm_w_out', 'gm_b_out', 'kv_norm', 'w_dkv', 'kv_a_norm', 'k_rope_norm', 'w_uk',
        'w_uv', 'k_nope_norm', 'w_dq', 'q_a_norm', 'w_uq', 'q_nope_norm', 'q_rope_norm', 'w_o', 'moe_w_group',
        'moe_b_group', 'moe_w_expert', 'moe_b_expert', 'moe_w1', 'moe_w3', 'moe_w2']
_OUTS = [((1, SEQ, D), 'float32'), ((DECB, DECS, D), 'float32'), ((1, SEQ, KVR), 'float32'),
         ((1, SEQ, ROPE), 'float32'), ((DECB, DECS, KVR), 'float32'), ((DECB, DECS, ROPE), 'float32'),
         ((1, DECB, DECS, DG), 'float32')]


def kernel(**inputs):
    import numpy as _np
    import concourse.bacc as _bacc
    from concourse import mybir as _mybir
    from concourse.bass_utils import run_bass_kernel_spmd as _run

    nc = _bacc.Bacc("TRN2", target_bir_lowering=False, num_devices=1)
    arrays, ins, outs = {}, {}, []
    for name in _INS:
        a = _np.ascontiguousarray(inputs[name])
        arrays[f"in_{name}_dram"] = a
        ins[name] = nc.dram_tensor(f"in_{name}_dram", a.shape, _mybir.dt.from_np(a.dtype), kind="ExternalInput").ap()
    arrays["in_const_dram"] = constants()
    ins["const"] = nc.dram_tensor("in_const_dram", (P, CONST_W), _mybir.dt.float32, kind="ExternalInput").ap()
    for i, (shape, dtype) in enumerate(_OUTS):
        dt = _mybir.dt.from_np(_np.dtype(dtype))
        outs.append(nc.dram_tensor(f"out_{i}_dram", shape, dt, kind="ExternalOutput").ap())
    build(nc, ins, outs)
    r = _run(nc, [arrays], core_ids=[0])
    return tuple(r.results[0][f"out_{i}_dram"] for i in range(len(_OUTS)))
```

```python
from contextlib import ExitStack

import numpy as np

import concourse.bass as bass
from concourse import mybir

ALU = mybir.AluOpType
ACT = mybir.ActivationFunctionType
AX = mybir.AxisListType
F32 = mybir.dt.float32
F32R = mybir.dt.float32r
I32 = mybir.dt.int32
U32 = mybir.dt.uint32

P = 128
TILES = 3
SAMPLE = 2
TOK = TILES * P
D = 1024
KD = D // P
DG = 2048
NSG = 8
SGW = DG // NSG
KG = DG // P
SEQ, DECB, DECS, PAST = 256, 8, 16, 256
CHUNK = 64
HEADS, NOPE, ROPE, VD = 8, 64, 32, 64
QK = NOPE + ROPE
QR, KVR = 384, 256
SCALE = QK ** -0.5
NG, EPG = 4, 4
NE = NG * EPG
DE = 512
KE = DE // P
EPS = 1e-6
BIG = 1e30
NEG = -1e30
SLOTS = 2 * TOK
CAP = 80
EXTRA = SLOTS // (CAP + 1)
ROWS = SLOTS + CAP
WCOL = 4096
N_IN, N_OUT = 8, 4
M_MOE = [N_IN + N_OUT, N_IN + N_OUT + 3 * NE]

C_ID, C_UP, C_ONE = 0, 128, 256
C_COS, C_SIN = 384, 384 + TILES * 16
C_MASK = C_SIN + TILES * 16
C_RANKW = C_MASK + 128
C_IOTA = C_RANKW + 16
C_HEADS = C_IOTA + 16
C_OWN = C_HEADS + 224
C_EPS = C_OWN + 240
CONST_W = C_EPS + 1


def constants():
    c = np.zeros((P, CONST_W), np.float32)
    c[:, C_ID:C_ID + P] = np.eye(P)
    c[:, C_UP:C_UP + P] = np.triu(np.ones((P, P)), 1)
    c[:, C_ONE:C_ONE + P] = 1.0
    half = ROPE // 2
    inv = (np.float32(10000.0) ** (-np.arange(half, dtype=np.float32) / np.float32(half))).astype(np.float32)
    for t in range(TILES):
        pos = np.arange(P) + t * P if t < SAMPLE else PAST + np.arange(P) % DECS
        ang = pos.astype(np.float32)[:, None] * inv[None]
        c[:, C_COS + 16 * t:C_COS + 16 * t + 16] = np.cos(ang)
        c[:, C_SIN + 16 * t:C_SIN + 16 * t + 16] = np.sin(ang)
    c[:CHUNK, C_MASK + CHUNK:C_MASK + P] = NEG
    c[:, C_RANKW:C_RANKW + 16] = 32 - np.arange(16)
    c[:, C_IOTA:C_IOTA + 16] = np.arange(16)
    for x in range(2):
        c[NOPE * x:NOPE * (x + 1), C_HEADS + 96 + DECS * x:C_HEADS + 96 + DECS * (x + 1)] = 1.0
    c[:, C_OWN:C_EPS] = NEG
    c[:, C_EPS] = EPS
    c[:, C_OWN + P - DECS:C_OWN + P] = 0.0
    return c


def build(nc, A, O):
    top = ExitStack()
    with top:
        def sem(name):
            return top.enter_context(nc.semaphore(name))

        def sb(name, shape, dt=F32, scope=top):
            return scope.enter_context(nc.sbuf_tensor(name, shape, dt))

        xrows = nc.dram_tensor("moe_xrows", (ROWS, D), F32, kind="Internal").ap()
        yrows = nc.dram_tensor("moe_yrows", (ROWS, D), F32, kind="Internal").ap()

        h = sb("h", [P, TILES, D])
        const = sb("const", [P, CONST_W])
        ident, upper, ones = const[:, C_ID:C_ID + P], const[:, C_UP:C_UP + P], const[:, C_ONE:C_ONE + P]
        raw = sb("raw", [P, 3, WCOL])
        gain = sb("gain", [P, D])
        stat = sb("stat", [P, 2, 4])
        wroute = sb("wroute", [P, 2, KD, NG + NE])
        broute = sb("broute", [P, 2, NG + NE])
        ps = top.enter_context(nc.psum_tensor("ps", [P, 8, 512], F32))

        raw_loaded = [sem(f"raw_loaded{i}") for i in range(3)]
        wh_ready, wl_ready, w_used = sem("wh_ready"), sem("wl_ready"), sem("w_used")
        dve_step, act_step = sem("dve_step"), sem("act_step")
        steps = {"dve": 0, "act": 0}

        def dve_link(v, ins):
            steps["dve"] += 1
            ins.then_inc(dve_step, 1)
            v.wait_ge(dve_step, steps["dve"])

        def act_link(a, ins):
            steps["act"] += 1
            ins.then_inc(act_step, 1)
            a.wait_ge(act_step, steps["act"])

        ms_ready, rms_ready = sem("ms_ready"), sem("rms_ready")
        roots = {"ms_a": 0, "rms": 0}

        def rms_inverse(v, ms, out, scale):
            steps["dve"] += 1
            nc.vector.tensor_scalar(out, ms, scale, EPS, ALU.mult, ALU.add).then_inc(ms_ready, 1)
            roots["rms"] += 1
            v.wait_ge(rms_ready, roots["rms"])
            nc.vector.reciprocal(out, out).then_inc(dve_step, 1)
            v.wait_ge(dve_step, steps["dve"])

        def root(a, x):
            roots["ms_a"] += 1
            a.wait_ge(ms_ready, roots["ms_a"])
            nc.scalar.activation(x, x, ACT.Sqrt).then_inc(rms_ready, 1)

        def inverse_rms(v, junk):
            for t in range(TILES):
                dve_link(v, nc.vector.tensor_tensor_reduce(junk, h[:, t], h[:, t], 1.0, 0.0, ALU.mult,
                                                           ALU.add, stat[:, 0, t:t + 1]))
            rms_inverse(v, stat[:, 0, 0:TILES], stat[:, 1, 0:TILES], 1.0 / D)

        def row_roots(a, junk, ready):
            for t in range(TILES):
                ready(t)
                act_link(a, nc.scalar.activation(junk, h[:, t], ACT.Square, accum_out=stat[:, 0, t:t + 1]))
            nc.scalar.activation(stat[:, 1, 0:TILES], stat[:, 0, 0:TILES], ACT.Sqrt, bias=const[:, C_EPS:C_EPS + 1],
                                 scale=1.0 / D).then_inc(rms_ready, 1)

        def inverse_of_roots(v):
            roots["rms"] += 1
            v.wait_ge(rms_ready, roots["rms"])
            dve_link(v, nc.vector.reciprocal(stat[:, 1, 0:TILES], stat[:, 1, 0:TILES]))

        def norm_rows(t, out):
            return nc.vector.scalar_tensor_tensor(out, h[:, t], stat[:, 1, t:t + 1], gain[:], ALU.mult, ALU.mult)

        def split_product(pe, m, outs, xh, xl, wh, wl, nk, halves, start=True, stop=True):
            pe.wait_ge(wh_ready, m + 1)
            for t, out in enumerate(outs):
                for k in range(nk):
                    for x in (xh, xl):
                        for c in range(halves):
                            nc.tensor.matmul(out[c], x(t, k), wh[:, k, c * 512:c * 512 + 512],
                                             start=start and k == 0 and x is xh, stop=False)
            pe.wait_ge(wl_ready, m + 1)
            for t, out in enumerate(outs):
                for k in range(nk):
                    for c in range(halves):
                        last = nc.tensor.matmul(out[c], xh(t, k), wl[:, k, c * 512:c * 512 + 512],
                                                start=False, stop=stop and k == nk - 1)
            return last

        gm = ExitStack()
        split_gm = [[sb(f"gm_w{p}{i}", [P, WCOL], F32R, gm) for p in "hl"] for i in range(2)]
        fx = sb("gm_fx", [P, 2 * KD * TOK], F32R, gm)
        xth = fx[:, 0:KD * TOK].rearrange("p (k t) -> p k t", k=KD)
        xtl = fx[:, KD * TOK:].rearrange("p (k t) -> p k t", k=KD)
        utl = fx[:, :].rearrange("p (k t) -> p k t", k=KG)
        u = sb("gm_u", [P, TILES, DG], F32, gm)
        gm_v = ExitStack()
        vv = sb("gm_v", [P, TILES, DG], F32, gm_v)
        gm_v.close()
        uth = sb("gm_uth", [P, KG, TOK], F32R, gm)
        gmst = sb("gm_stat", [P, 20], F32, gm)
        bs = sb("gm_bs", [P, 2, NSG], F32, gm)
        gm.close()
        wst = raw[:, 2, 0:2 * NSG * P].rearrange("p (a g i) -> p a g i", a=2, g=NSG)
        bin_c = raw[:, 2, 2048:3072].rearrange("p (a n) -> p a n", a=2)
        ln_c = u[:, 0:2]
        xn = [u[:, 0, i * D:(i + 1) * D] for i in range(2)]
        ws_raw = u[:, 1, 0:2 * NSG * P].rearrange("p (a g j) -> p a g j", a=2, g=NSG)

        ld_h, ld_const, ld_gain, ld_ws, ld_ws16, ld_bs, ld_route = map(
            sem, ["ld_h", "ld_const", "ld_gain", "ld_ws", "ld_ws16", "ld_bs", "ld_route"])
        ld_bin = [sem("ld_bin0"), sem("ld_bin1")]
        ld_ln, ld_bout = sem("ld_ln"), sem("ld_bout")
        ws_zeroed = sem("ws_zeroed")
        gm_xn, gm_xT, gm_xh, gm_xl = map(sem, ["gm_xn", "gm_xT", "gm_xh", "gm_xl"])
        gm_wsT, gm_wst = sem("gm_wsT"), sem("gm_wst")
        z_read, z_gelu = sem("z_read"), sem("z_gelu")
        v_mean, v_square, v_ready, h_mixed = map(sem, ["v_mean", "v_square", "v_ready", "h_mixed"])
        s_done, us_ready = sem("s_done"), sem("us_ready")
        uT_done, uth_ready, utl_ready = sem("uT_done"), sem("uth_ready"), sem("utl_ready")
        v_stored = sem("v_stored")

        IN_ORDER = [4, 5, 6, 7, 0, 1, 2, 3]

        def gm_dest(c):
            return (u, c * 512) if c < 4 else (vv, (c - 4) * 512)

        def in_weights(m):
            return A["gm_w_in"][0, :, IN_ORDER[m] * 512:IN_ORDER[m] * 512 + 512].rearrange("(k p) n -> p k n", p=P)

        def out_weights(j):
            return A["gm_w_out"][0, j * 512:(j + 1) * 512, :].rearrange("(k p) n -> p k n", p=P)

        def raw_in(s):
            return raw[:, s, :].rearrange("p (k n) -> p k n", k=KD)

        def raw_out(s):
            return raw[:, s, :].rearrange("p (k n) -> p k n", k=KE)

        def gm_sync(sp):
            sp.dma_start(h[:, 0:2, :], A["x_prompt"][0].rearrange("(t p) d -> p t d", p=P)).then_inc(ld_h, 16)
            sp.dma_start(h[:, 2, :], A["x_sample"].rearrange("b s d -> (b s) d")).then_inc(ld_h, 16)
            sp.wait_ge(ld_const, 16)
            sp.wait_ge(ld_gain, 16)
            for m in range(N_IN + N_OUT):
                if m >= 2:
                    sp.wait_ge(wl_ready, m - 1)
                src = in_weights(m) if m < N_IN else out_weights(m - N_IN)
                dst = raw_in(m % 2) if m < N_IN else raw_out(m % 2)
                sp.dma_start(dst, src).then_inc(raw_loaded[m % 2], 16)

        def gm_pool(g):
            g.dma_start(const[:], A["const"]).then_inc(ld_const, 16)
            g.dma_start(gain[:], A["norm_mix"][0:1, :].partition_broadcast(P)).then_inc(ld_gain, 16)
            g.dma_start(ws_raw[:, 0], A["gm_w_s"][0].rearrange("g i j -> i g j")).then_inc(ld_ws, 16)
            g.wait_ge(ws_zeroed, 1)
            for b in range(DECB):
                g.dma_start(ws_raw[b * DECS:(b + 1) * DECS, 1, :, b * DECS:(b + 1) * DECS],
                            A["gm_w_s"][0, :, 0:DECS, 0:DECS].rearrange("g i j -> i g j")).then_inc(ld_ws16, 16)
            g.dma_start(bs[:, 0], A["gm_b_s"][0].rearrange("g i -> i g"),
                        allow_slow_non_contiguous=True).then_inc(ld_bs, 16)
            for b in range(DECB):
                g.dma_start(bs[b * DECS:(b + 1) * DECS, 1],
                            A["gm_b_s"][0, :, 0:DECS].rearrange("g i -> i g"),
                            allow_slow_non_contiguous=True).then_inc(ld_bs, 16)
            for l in range(2):
                g.dma_start(wroute[:, l, :, 0:NG], A["moe_w_group"][l].rearrange("(k p) n -> p k n", p=P)).then_inc(ld_route, 16)
                g.dma_start(wroute[:, l, :, NG:], A["moe_w_expert"][l].rearrange("(k p) n -> p k n", p=P)).then_inc(ld_route, 16)
                g.dma_start(broute[:, l, 0:NG], A["moe_b_group"][l:l + 1, :].partition_broadcast(P)).then_inc(ld_route, 16)
                g.dma_start(broute[:, l, NG:], A["moe_b_expert"][l:l + 1, :].partition_broadcast(P)).then_inc(ld_route, 16)
            for m in range(N_IN):
                if m == 2:
                    g.wait_ge(gm_xT, TILES)
                    g.wait_ge(gm_wsT, 2)
                    for i, name in enumerate(("gm_ln_g", "gm_ln_b")):
                        g.dma_start(ln_c[:, i], A[name].partition_broadcast(P)).then_inc(ld_ln, 16)
                if m >= 2:
                    g.wait_ge(z_read, TILES * (m - 1))
                c = IN_ORDER[m]
                g.dma_start(bin_c[:, m % 2], A["gm_b_in"][0:1, c * 512:c * 512 + 512].partition_broadcast(P)
                            ).then_inc(ld_bin[m % 2], 16)
            g.wait_ge(v_ready, TILES)
            g.dma_start(O[6].rearrange("n b s d -> (n b s) d"), vv[:, SAMPLE, :]).then_inc(v_stored, 16)
            g.dma_start(gain[:], A["gm_b_out"][0:1, :].partition_broadcast(P)).then_inc(ld_bout, 16)

        def split_h(a, m, src_slot, wh, raw_count, free):
            a.wait_ge(raw_loaded[src_slot], 16 * raw_count)
            if free is not None:
                a.wait_ge(w_used, free)
            nc.scalar.activation(wh[:], raw[:, src_slot, :], ACT.Copy).then_inc(wh_ready, 1)

        def split_l(v, m, src_slot, wh, wl):
            v.wait_ge(wh_ready, m + 1)
            nc.vector.tensor_tensor(wl[:], raw[:, src_slot, :], wh[:].bitcast(F32), ALU.subtract).then_inc(wl_ready, 1)

        def gm_split_h(a, m):
            split_h(a, m, m % 2, split_gm[m % 2][0], m // 2 + 1, m - 1 if m >= 2 else None)

        def gm_split_l(v, m):
            split_l(v, m, m % 2, *split_gm[m % 2])

        def gm_vector(v):
            nc.vector.memset(ws_raw[:, 1], 0.0).then_inc(ws_zeroed, 1)
            v.wait_ge(ld_h, 32)
            v.wait_ge(ld_gain, 16)
            inverse_of_roots(v)
            for t in range(TILES):
                if t >= 2:
                    v.wait_ge(gm_xT, t - 1)
                norm_rows(t, xn[t % 2]).then_inc(gm_xn, 1)
                if t >= 1:
                    gm_xl_part(v, t - 1)
            gm_xl_part(v, TILES - 1)
            gm_split_l(v, 0)
            for a in range(2):
                v.wait_ge(gm_wsT, a + 1)
                dve_link(v, nc.vector.tensor_copy(wst[:, a], ps[:, 3 + 2 * a:5 + 2 * a].rearrange("p b (g i) -> p (b g) i", i=P)))
            nc.vector.memset(wst[CHUNK:P, 0, :, 0:CHUNK], 0.0).then_inc(gm_wst, 1)
            gm_split_l(v, 1)
            for m in range(N_IN):
                c = IN_ORDER[m]
                dst, col = gm_dest(c)
                if m == 4:
                    gm_layer_norm(v)
                for t in range(TILES):
                    if t == 0:
                        v.wait_ge(ld_bin[m % 2], 16 * (m // 2 + 1))
                        v.wait_ge(w_used, m + 1)
                    nc.vector.tensor_tensor(dst[:, t, col:col + 512], ps[:, 3 * (m % 2) + t], bin_c[:, m % 2],
                                            ALU.add).then_inc(z_read, 1)
                gm_split_l(v, m + 2)
            for t in range(TILES):
                for gp in range(NSG // 2):
                    n = t * 4 + gp
                    v.wait_ge(s_done, n + 1)
                    if n == 0:
                        v.wait_ge(z_gelu, TILES * N_IN)
                        v.wait_ge(ld_bs, 16 * (1 + DECB))
                    for i in range(2):
                        g = 2 * gp + i
                        uu = u[:, t, g * SGW:(g + 1) * SGW]
                        nc.vector.scalar_tensor_tensor(uu, ps[:, n % 6, i * SGW:(i + 1) * SGW],
                                                       bs[:, 1 if t == SAMPLE else 0, g:g + 1], uu,
                                                       ALU.add, ALU.mult).then_inc(us_ready, 1)
            for n in range(TILES * 4):
                t, q = divmod(n, 4)
                v.wait_ge(uth_ready, n + 1)
                nc.vector.tensor_tensor(utl[:, 4 * q:4 * q + 4, t * P:(t + 1) * P],
                                        ps[:, 6 + n % 2].rearrange("p (k t) -> p k t", k=4),
                                        uth[:, 4 * q:4 * q + 4, t * P:(t + 1) * P].bitcast(F32),
                                        ALU.subtract).then_inc(utl_ready, 1)
            v.wait_ge(ld_bout, 16)
            for t in range(TILES):
                dve_link(v, nc.vector.tensor_tensor(h[:, t], h[:, t], gain[:], ALU.add))
            for m in range(N_IN + 2, N_IN + N_OUT):
                gm_split_l(v, m)
            v.wait_ge(w_used, N_IN + N_OUT)
            for t in range(TILES):
                nc.vector.tensor_tensor(h[:, t].rearrange("p (c n) -> p c n", c=2), h[:, t].rearrange("p (c n) -> p c n", c=2),
                                        ps[:, 2 * t:2 * t + 2], ALU.add).then_inc(h_mixed, 1)
            v.wait_ge(h_mixed, TILES)

        def gm_xl_part(v, t):
            v.wait_ge(gm_xh, t + 1)
            nc.vector.tensor_tensor(xtl[:, :, t * P:(t + 1) * P], ps[:, 6:8].rearrange("p b (k t) -> p (b k) t", t=P),
                                    xth[:, :, t * P:(t + 1) * P].bitcast(F32), ALU.subtract).then_inc(gm_xl, 1)

        def gm_layer_norm(v):
            v.wait_ge(z_gelu, TILES * 4)
            mean, inv = gmst[:, 12:15], gmst[:, 15:18]
            dve_link(v, nc.vector.tensor_reduce(mean, gmst[:, 0:12].rearrange("p (t c) -> p t c", t=TILES), AX.X, ALU.add))
            nc.vector.tensor_scalar(mean, mean, -1.0 / DG, None, ALU.mult).then_inc(v_mean, 1)
            v.wait_ge(v_mean, 1)
            v.wait_ge(ld_ln, 32)
            for t in range(TILES):
                v.wait_ge(v_square, t + 1)
                dve_link(v, nc.vector.scalar_tensor_tensor(vv[:, t], vv[:, t], mean[:, t:t + 1], ln_c[:, 0], ALU.add, ALU.mult))
            roots["rms"] += 1
            v.wait_ge(rms_ready, roots["rms"])
            dve_link(v, nc.vector.reciprocal(inv, inv))
            for t in range(TILES):
                nc.vector.scalar_tensor_tensor(vv[:, t], vv[:, t], inv[:, t:t + 1], ln_c[:, 1], ALU.mult, ALU.add
                                               ).then_inc(v_ready, 1)
            v.wait_ge(v_ready, TILES)

        def gm_scalar(a):
            a.wait_ge(ld_h, 32)
            a.wait_ge(ld_const, 16)
            row_roots(a, u[:, 2, 0:D], lambda t: None)
            gm_xh_part(a, 0)
            gm_xh_part(a, 1)
            gm_split_h(a, 0)
            gm_xh_part(a, 2)
            gm_split_h(a, 1)
            for m in range(N_IN):
                c = IN_ORDER[m]
                dst, col = gm_dest(c)
                if m == 4:
                    a.wait_ge(v_mean, 1)
                    for t in range(TILES):
                        nc.scalar.activation(u[:, 2], vv[:, t], ACT.Square, bias=gmst[:, 12 + t:13 + t],
                                             accum_out=gmst[:, 15 + t:16 + t]).then_inc(v_square, 1)
                        a.wait_ge(v_square, t + 1)
                    nc.scalar.activation(gmst[:, 15:18], gmst[:, 15:18], ACT.Sqrt, bias=const[:, C_EPS:C_EPS + 1],
                                         scale=1.0 / DG).then_inc(rms_ready, 1)
                for t in range(TILES):
                    a.wait_ge(z_read, m * TILES + t + 1)
                    z = dst[:, t, col:col + 512]
                    kw = {"accum_out": gmst[:, 4 * t + c - 4:4 * t + c - 3]} if c >= 4 else {}
                    nc.scalar.activation(z, z, ACT.Gelu_apprx_tanh, **kw).then_inc(z_gelu, 1)
                gm_split_h(a, m + 2)
            for n in range(TILES * 4):
                t, q = divmod(n, 4)
                a.wait_ge(uT_done, n + 1)
                if n == 0:
                    a.wait_ge(v_stored, 16)
                nc.scalar.activation(uth[:, 4 * q:4 * q + 4, t * P:(t + 1) * P],
                                     ps[:, 6 + n % 2].rearrange("p (k t) -> p k t", k=4), ACT.Copy).then_inc(uth_ready, 1)
            for m in range(N_IN + 2, N_IN + N_OUT):
                gm_split_h(a, m)

        def gm_xh_part(a, t):
            a.wait_ge(gm_xT, t + 1)
            nc.scalar.activation(xth[:, :, t * P:(t + 1) * P], ps[:, 6:8].rearrange("p b (k t) -> p (b k) t", t=P),
                                 ACT.Copy).then_inc(gm_xh, 1)

        def gm_tensor(pe):
            pe.wait_ge(ld_const, 16)
            for t in range(TILES):
                pe.wait_ge(gm_xn, t + 1)
                if t:
                    pe.wait_ge(gm_xl, t)
                for k in range(KD):
                    last = nc.tensor.transpose(ps[:, 6 + k // 4, (k % 4) * P:(k % 4 + 1) * P],
                                               xn[t % 2][:, k * P:(k + 1) * P], ident)
                last.then_inc(gm_xT, 1)
            for a, s, n in ((0, ld_ws, 16), (1, ld_ws16, 16 * DECB)):
                pe.wait_ge(s, n)
                if a:
                    pe.wait_ge(gm_xl, TILES)
                for g in range(NSG):
                    last = nc.tensor.transpose(ps[:, 3 + 2 * a + g // 4, (g % 4) * P:(g % 4 + 1) * P], ws_raw[:, a, g], ident)
                last.then_inc(gm_wsT, 1)
            pe.wait_ge(gm_xl, TILES)
            for m in range(N_IN):
                if m == 1:
                    pe.wait_ge(gm_wst, 1)
                if m >= 2:
                    pe.wait_ge(z_read, TILES * (m - 1))
                wh, wl = [w[:].rearrange("p (k n) -> p k n", k=KD) for w in split_gm[m % 2]]
                last = split_product(pe, m, [[ps[:, 3 * (m % 2) + t]] for t in range(TILES)],
                                     lambda t, k: xth[:, k, t * P:(t + 1) * P], lambda t, k: xtl[:, k, t * P:(t + 1) * P],
                                     wh, wl, KD, 1)
                last.then_inc(w_used, 1)
            pe.wait_ge(v_ready, TILES)
            pe.wait_ge(z_read, TILES * N_IN)
            for t in range(TILES):
                for gp in range(NSG // 2):
                    n = t * 4 + gp
                    if n >= 6:
                        pe.wait_ge(us_ready, 2 * (n - 5))
                    for i in range(2):
                        g = 2 * gp + i
                        last = nc.tensor.matmul(ps[:, n % 6, i * SGW:(i + 1) * SGW], wst[:, 1 if t == SAMPLE else 0, g],
                                                vv[:, t, g * SGW:(g + 1) * SGW], start=True, stop=True)
                    last.then_inc(s_done, 1)
            for n in range(TILES * 4):
                t, q = divmod(n, 4)
                pe.wait_ge(us_ready, 8 * (t + 1))
                if n >= 2:
                    pe.wait_ge(utl_ready, n - 1)
                for j in range(4):
                    k = 4 * q + j
                    last = nc.tensor.transpose(ps[:, 6 + n % 2, j * P:(j + 1) * P], u[:, t, k * P:(k + 1) * P], ident)
                last.then_inc(uT_done, 1)
            pe.wait_ge(utl_ready, TILES * 4)
            for j in range(N_OUT):
                m = N_IN + j
                wh, wl = [w[:].rearrange("p (k n) -> p k n", k=KE) for w in split_gm[m % 2]]
                last = split_product(pe, m, [[ps[:, 2 * t], ps[:, 2 * t + 1]] for t in range(TILES)],
                                     lambda t, k: uth[:, 4 * j + k, t * P:(t + 1) * P],
                                     lambda t, k: utl[:, 4 * j + k, t * P:(t + 1) * P],
                                     wh, wl, KE, 2, start=j == 0, stop=j == N_OUT - 1)
                last.then_inc(w_used, 1)

        moe = ExitStack()
        split_moe = [[sb(f"moe_w{p}{i}", [P, WCOL], F32R, moe) for p in "hl"] for i in range(3)]
        rows = sb("moe_rows", [P, 4, D], F32, moe)
        xsplit = [[sb(f"moe_x{p}{i}", [P, KD, CAP], F32R, moe) for p in "hl"] for i in range(2)]
        sil = sb("moe_silu", [CAP, DE], F32, moe)
        hid = sb("moe_hidden", [CAP, DE], F32, moe)
        hth, htl = sb("moe_hTh", [P, KE, CAP], F32R, moe), sb("moe_hTl", [P, KE, CAP], F32R, moe)
        NT = NG + NE
        logit = sb("rt_logit", [P, TILES, NT], F32, moe)
        gsel = sb("rt_group", [P, TILES, NG], F32, moe)
        pen = sb("rt_penalty", [P, TILES, NG], F32, moe)
        lem = sb("rt_in_group", [P, TILES, NE], F32, moe)
        pick = [sb(f"rt_pick{i}", [P, TILES, NE], F32, moe) for i in range(2)]
        tmp = sb("rt_tmp", [P, TILES, NE], F32, moe)
        best = sb("rt_best", [P, 6, TILES], F32, moe)
        ex = sb("rt_exp", [P, TILES, NG + 1], F32, moe)
        wts = sb("rt_weight", [P, 2, TILES], F32, moe)
        picked = sb("rt_picked", [P, TILES, NE], F32, moe)
        rank = sb("rt_rank", [P, TILES + 1, NE], F32, moe)
        cat = sb("rt_counts", [P, 2 * NE], F32, moe)
        first = sb("rt_first", [P, 2 * NE], F32, moe)
        dst = sb("rt_dst", [P, TILES, 2], F32, moe)
        dst_i = sb("rt_dst_i", [P, TILES * 2], U32, moe)
        first_i = sb("rt_first_i", [P, NE], I32, moe)
        ov = sb("rt_over", [P, 4, NE], F32, moe)
        ovb = sb("rt_over_block", [P, EXTRA, NE], F32, moe)
        ovb2 = sb("rt_over_block2", [P, EXTRA, NE], F32, moe)
        ovt = sb("rt_over_table", [P, 2 * EXTRA + 1], F32, moe)
        ovt_i = sb("rt_over_table_i", [P, 2 * EXTRA + 1], I32, moe)
        moe.close()
        y_rows = [rows[:, i] for i in range(4)] + [split_moe[2][1][:, i * D:(i + 1) * D].bitcast(F32) for i in range(2)]
        BX, BA, BB, BH, BY, BR = 0, 2, 3, 4, 5, 7

        ld_ffn, pad_written = sem("ld_ffn"), sem("pad_written")
        rt_xn, rt_xT, rt_xTc, rt_logits = sem("rt_xn"), sem("rt_xT"), sem("rt_xTc"), sem("rt_logits")
        rt_exp, rt_picked, rt_rank = sem("rt_expd"), sem("rt_pickd"), sem("rt_rankd")
        rt_dst, rt_table, scattered = sem("rt_dstd"), sem("rt_table"), sem("scattered")
        x_loaded = [sem("x_loaded0"), sem("x_loaded1")]
        xT_done, xh_ready, xl_ready = sem("xT_done"), sem("xh_ready"), sem("xl_ready")
        silu_done, hid_done = sem("silu_done"), sem("hid_done")
        hT_done, hh_ready, hl_ready = sem("hT_done"), sem("hh_ready"), sem("hl_ready")
        y_out, y_stored, y_final = sem("y_out"), sem("y_stored"), sem("y_final")
        y_back, combined = [sem(f"y_back{t}") for t in range(TILES)], sem("combined")
        over = [{k: sem(f"over{l}_{k}") for k in ("w", "x", "pe", "act", "hid", "st")} for l in range(2)]

        def at_least(eng, s, n):
            if not isinstance(n, int) or n > 0:
                eng.wait_ge(s, n)

        RAW_BASE = [N_IN // 2 + N_OUT // 2] * 2 + [0]

        def raw_count(l, s, q):
            return RAW_BASE[s] + NE * l + q + 1

        def w_in_expert(l, name, e):
            w = A[name][l, bass.ds(e, 1)]
            return w.rearrange("o (k p) n -> p (o k) n", p=P)

        def moe_w_view(w, nk):
            return w.rearrange("p (k n) -> p k n", k=nk)

        def moe_sync(sp, l):
            m0, E0 = M_MOE[l], NE * l

            def load(name, e, j, slot):
                if isinstance(j, int) and j < 3:
                    if l == 0:
                        sp.wait_ge(wl_ready, m0)
                    else:
                        sp.wait_ge(*[(at_proj, TILES), (sm_o, 1), (at_y, 1)][slot])
                else:
                    at_least(sp, wl_ready, m0 + j - 2)
                sp.dma_start(moe_w_view(raw[:, slot, :], KE if name == "moe_w2" else KD),
                             w_in_expert(l, name, e)).then_inc(raw_loaded[slot], 16)

            def load_x(e, par):
                row = sp.value_load(first_i[0:1, bass.ds(e, 1)], min_val=0, max_val=SLOTS)
                if not (isinstance(e, int) and e < 2):
                    at_least(sp, xT_done, E0 + e - 1)
                sp.dma_start(rows[0:CAP, par, :], xrows[bass.ds(row, CAP), :]).then_inc(x_loaded[par], 16)

            def store_y(e, par):
                row = sp.value_load(first_i[0:1, bass.ds(e, 1)], min_val=0, max_val=SLOTS)
                at_least(sp, y_stored, 16 * (E0 + e))
                if isinstance(e, int):
                    sp.wait_ge(y_out, E0 + e + 1)
                sp.dma_start(yrows[bass.ds(row, CAP), :], rows[0:CAP, 2 + par, :]).then_inc(y_stored, 16)

            load("moe_w1", 0, 0, 0)
            load("moe_w3", 0, 1, 1)
            load("moe_w1", 1, 2, 2)
            load("moe_w3", 1, 3, 0)
            load("moe_w2", 0, 4, 1)
            load("moe_w1", 2, 5, 2)
            sp.wait_ge(scattered, 16 * 2 * TILES * (l + 1))
            sp.wait_ge(pad_written, 16)
            load_x(0, 0)
            load_x(1, 1)

            def of_expert(e, par):
                if not (isinstance(e, int) and e == 2):
                    load("moe_w1", e, 3 * e - 1, 2)
                load_x(e, par)
                load("moe_w3", e, 3 * e, 0)
                if not (isinstance(e, int) and e < 4):
                    store_y(e - 4, par)
                load("moe_w2", e - 1, 3 * e + 1, 1)

            for e in range(2, 5):
                of_expert(e, e % 2)
            with sp.Fori(0, (NE - 6) // 2) as i:
                of_expert(2 * i + 5, 1)
                of_expert(2 * i + 6, 0)
            of_expert(NE - 1, 1)
            load("moe_w2", NE - 1, 3 * NE - 1, 2)
            for e in range(NE - 4, NE):
                store_y(e, e % 2)
            if l == 0:
                load_cache(sp)
            s = over[l]
            sp.wait_ge(y_stored, 16 * (E0 + NE))
            sp.wait_ge(wl_ready, m0 + 3 * NE)
            sp.wait_ge(rt_table, l + 1)
            n_over = sp.value_load(ovt_i[0:1, 2 * EXTRA:2 * EXTRA + 1], min_val=0, max_val=EXTRA)
            sp.sem_inc(s["st"], 16)
            with sp.Fori(0, EXTRA) as i:
                with sp.If(n_over > i):
                    e = sp.value_load(ovt_i[0:1, bass.ds(i, 1)], min_val=0, max_val=NE - 1)
                    row = sp.value_load(ovt_i[0:1, bass.ds(i + EXTRA, 1)], min_val=0, max_val=SLOTS)
                    at_least(sp, s["st"], 16 * i + 16)
                    sp.dma_start(rows[0:CAP, 0, :], xrows[bass.ds(row, CAP), :]).then_inc(s["x"], 16)
                    for slot, name in enumerate(("moe_w1", "moe_w3", "moe_w2")):
                        sp.dma_start(moe_w_view(raw[:, slot, :], KE if slot == 2 else KD),
                                     w_in_expert(l, name, e)).then_inc(s["w"], 16)
                    at_least(sp, s["act"], 4 * i + 4)
                    sp.dma_start(yrows[bass.ds(row, CAP), :], rows[0:CAP, 2, :]).then_inc(s["st"], 16)
            at_least(sp, s["st"], 16 * n_over + 16)
            sp.sem_inc(y_final, 1)

        def experts(eng, step):
            for e in range(3):
                step(e, e % 2)
            with eng.Fori(0, (NE - 4) // 2) as i:
                step(2 * i + 3, 1)
                step(2 * i + 4, 0)
            step(NE - 1, 1)

        def is_first(e):
            return isinstance(e, int) and e == 0

        def is_last(e):
            return isinstance(e, int) and e == NE - 1

        def moe_pool(g, l):
            if l == 0:
                g.dma_start(xrows[SLOTS:ROWS], A["x_prompt"][0, 0:CAP, :]).then_inc(pad_written, 16)
                g.wait_ge(wl_ready, N_IN + N_OUT - 1)
            g.dma_start(gain[:], A["norm_ffn"][l:l + 1, :].partition_broadcast(P)).then_inc(ld_ffn, 16)
            if l == 0:
                g.wait_ge(rt_xn, TILES)
                g.dma_start(gain[:], A["kv_norm"].rearrange("(a n) -> a n", a=1).partition_broadcast(P)).then_inc(ld_kvg, 16)
            g.wait_ge(rt_dst, l + 1)
            for t in range(TILES):
                for k in range(2):
                    g.indirect_dma_start(xrows[0:SLOTS], bass.IndirectOffsetOnAxis(ap=dst_i[:, 2 * t + k:2 * t + k + 1], axis=0),
                                         rows[:, t], None).then_inc(scattered, 16)
            g.wait_ge(y_final, l + 1)
            for t in range(TILES):
                for k in range(2):
                    g.indirect_dma_start(y_rows[2 * t + k], None, yrows[0:SLOTS],
                                         bass.IndirectOffsetOnAxis(ap=dst_i[:, 2 * t + k:2 * t + k + 1], axis=0)
                                         ).then_inc(y_back[t], 16)

        def first_max(v, x, n, out, value, key):
            shape = [P, TILES, n]
            t_ = tmp[:, :, 0:n]
            w = const[:, C_RANKW:C_RANKW + n].unsqueeze(1).to_broadcast(shape)
            dve_link(v, nc.vector.tensor_reduce(value, x, AX.X, ALU.max))
            dve_link(v, nc.vector.tensor_tensor(t_, x, value.unsqueeze(2).to_broadcast(shape), ALU.is_equal))
            dve_link(v, nc.vector.tensor_tensor(t_, t_, w, ALU.mult))
            dve_link(v, nc.vector.tensor_reduce(key, t_, AX.X, ALU.max))
            dve_link(v, nc.vector.tensor_tensor(out, t_, key.unsqueeze(2).to_broadcast(shape), ALU.is_equal))

        def route_vector(v, l):
            v.wait_ge(ld_ffn, 16 * (l + 1))
            inverse_of_roots(v)
            for t in range(TILES):
                norm_rows(t, rows[:, t]).then_inc(rt_xn, 1)
            for j in range(3):
                moe_split_l(v, l, j, j)
            v.wait_ge(rt_logits, TILES * (l + 1))
            v.wait_ge(ld_route, 16 * 8)
            if l == 0:
                v.wait_ge(ld_const, 16)
            dve_link(v, nc.vector.tensor_tensor(logit[:], ps[:, BR, 0:96].rearrange("p (t c) -> p t c", t=TILES)[:, :, 0:NT],
                                                broute[:, l, :].unsqueeze(1).to_broadcast([P, TILES, NT]), ALU.add))
            lg, le = logit[:, :, 0:NG], logit[:, :, NG:NT]
            first_max(v, lg, NG, gsel[:], best[:, 0], best[:, 1])
            dve_link(v, nc.vector.tensor_tensor(ex[:, :, 0:NG], lg, best[:, 0].unsqueeze(2).to_broadcast([P, TILES, NG]),
                                                ALU.subtract))
            dve_link(v, nc.vector.tensor_scalar(pen[:], gsel[:], BIG, -BIG, ALU.mult, ALU.add))
            shape4 = [P, TILES, NG, EPG]
            lem4 = lem[:].rearrange("p t (g j) -> p t g j", g=NG)
            dve_link(v, nc.vector.tensor_tensor(lem4, le.rearrange("p t (g j) -> p t g j", g=NG),
                                                gsel[:].unsqueeze(3).to_broadcast(shape4), ALU.mult))
            dve_link(v, nc.vector.tensor_tensor(lem4, lem4, pen[:].unsqueeze(3).to_broadcast(shape4), ALU.add))
            first_max(v, lem[:], NE, pick[0][:], best[:, 2], best[:, 3])
            dve_link(v, nc.vector.scalar_tensor_tensor(lem[:], pick[0][:], -2 * BIG, lem[:], ALU.mult, ALU.add))
            first_max(v, lem[:], NE, pick[1][:], best[:, 4], best[:, 5])
            nc.vector.tensor_tensor(picked[:], pick[0][:], pick[1][:], ALU.add).then_inc(rt_picked, 1)
            nc.vector.tensor_tensor(ex[:, :, NG], best[:, 4], best[:, 2], ALU.subtract).then_inc(rt_picked, 1)
            v.wait_ge(rt_rank, l + 1)
            dve_link(v, nc.vector.tensor_copy(rank[:], ps[:, BR, 128:192].rearrange("p (t e) -> p t e", e=NE)))
            count = rank[:, TILES]
            dve_link(v, nc.vector.tensor_scalar(cat[:, 0:NE], count, float(CAP), None, ALU.min))
            dve_link(v, nc.vector.tensor_tensor(cat[:, NE:], count, cat[:, 0:NE], ALU.subtract))
            dve_link(v, nc.vector.tensor_tensor_scan(first[:], ones[:, 0:2 * NE], cat[:], 0.0, ALU.mult, ALU.add))
            dve_link(v, nc.vector.tensor_tensor(first[:], first[:], cat[:], ALU.subtract))
            shape = [P, TILES, NE]
            dve_link(v, nc.vector.tensor_tensor(ov[:, 0], first[:, NE:], first[:, 0:NE], ALU.subtract))
            dve_link(v, nc.vector.tensor_scalar(ov[:, 0], ov[:, 0], -float(CAP), None, ALU.add))
            dve_link(v, nc.vector.tensor_scalar(tmp[:], rank[:, 0:TILES], float(CAP), None, ALU.is_ge))
            dve_link(v, nc.vector.tensor_tensor(tmp[:], tmp[:], ov[:, 0:1].to_broadcast(shape), ALU.mult))
            dve_link(v, nc.vector.tensor_tensor(tmp[:], tmp[:], rank[:, 0:TILES], ALU.add))
            dve_link(v, nc.vector.tensor_tensor(tmp[:], tmp[:], first[:, 0:NE].unsqueeze(1).to_broadcast(shape), ALU.add))
            for k in range(2):
                dve_link(v, nc.vector.tensor_tensor(lem[:], pick[k][:], tmp[:], ALU.mult))
                dve_link(v, nc.vector.tensor_reduce(dst[:, :, k], lem[:], AX.X, ALU.add))
            dve_link(v, nc.vector.tensor_copy(first_i[:], first[:, 0:NE]))
            nc.vector.tensor_copy(dst_i[:], dst[:].rearrange("p t k -> p (t k)")).then_inc(rt_dst, 1)
            v.wait_ge(rt_exp, l + 1)
            dve_link(v, nc.vector.tensor_reduce(best[:, 0], ex[:, :, 0:NG], AX.X, ALU.add))
            dve_link(v, nc.vector.scalar_tensor_tensor(best[:, 1], ex[:, :, NG], 1.0, best[:, 0], ALU.add, ALU.mult))
            dve_link(v, nc.vector.reciprocal(wts[:, 0], best[:, 1]))
            dve_link(v, nc.vector.tensor_tensor(wts[:, 1], ex[:, :, NG], wts[:, 0], ALU.mult))

        def table_vector(v):
            o = ov[0:1]
            c0 = cat[0:1, NE:]
            dve_link(v, nc.vector.tensor_scalar(o[:, 1], c0, 0.0, None, ALU.is_gt))
            for n in range(1, (TOK - 1) // CAP):
                dve_link(v, nc.vector.tensor_scalar(o[:, 2], c0, float(n * CAP), None, ALU.is_gt))
                dve_link(v, nc.vector.tensor_tensor(o[:, 1], o[:, 1], o[:, 2], ALU.add))
            dve_link(v, nc.vector.tensor_tensor_scan(o[:, 2], ones[0:1, 0:NE], o[:, 1], 0.0, ALU.mult, ALU.add))
            dve_link(v, nc.vector.tensor_tensor(o[:, 1], o[:, 2], o[:, 1], ALU.subtract))
            bshape = [1, EXTRA, NE]
            it = const[0:1, C_IOTA:C_IOTA + EXTRA].unsqueeze(2).to_broadcast(bshape)
            nc.vector.tensor_copy(ovt[0:1, 2 * EXTRA:2 * EXTRA + 1], o[:, 2, NE - 1:NE]).then_inc(dve_step, 1)
            steps["dve"] += 1
            dve_link(v, nc.vector.tensor_tensor(ovb[0:1], o[:, 1:2].to_broadcast(bshape), it, ALU.is_le))
            dve_link(v, nc.vector.tensor_tensor(ovb2[0:1], o[:, 2:3].to_broadcast(bshape), it, ALU.is_le))
            dve_link(v, nc.vector.tensor_tensor(ovb[0:1], ovb[0:1], ovb2[0:1], ALU.subtract))
            dve_link(v, nc.vector.tensor_tensor(ovb2[0:1], ovb[0:1], const[0:1, C_IOTA:C_IOTA + NE].unsqueeze(1).to_broadcast(bshape), ALU.mult))
            dve_link(v, nc.vector.tensor_reduce(ovt[0:1, 0:EXTRA], ovb2[0:1], AX.X, ALU.add))
            dve_link(v, nc.vector.scalar_tensor_tensor(o[:, 3], o[:, 1], -float(CAP), first[0:1, NE:], ALU.mult, ALU.add))
            dve_link(v, nc.vector.tensor_tensor(ovb2[0:1], ovb[0:1], o[:, 3:4].to_broadcast(bshape), ALU.mult))
            dve_link(v, nc.vector.tensor_reduce(ovt[0:1, EXTRA:2 * EXTRA], ovb2[0:1], AX.X, ALU.add))
            dve_link(v, nc.vector.scalar_tensor_tensor(ovt[0:1, EXTRA:2 * EXTRA], const[0:1, C_IOTA:C_IOTA + EXTRA], float(CAP),
                                                       ovt[0:1, EXTRA:2 * EXTRA], ALU.mult, ALU.add))
            nc.vector.tensor_copy(ovt_i[0:1, :], ovt[0:1, :]).then_inc(rt_table, 1)

        def route_scalar(a, l):
            row_roots(a, rows[:, 3], lambda t: a.wait_ge(h_mixed, TILES * l + t + 1))
            moe_split_h(a, l, 0, 0, 0)
            for t in range(TILES):
                n = TILES * l + t
                a.wait_ge(rt_xT, n + 1)
                if t:
                    a.wait_ge(rt_logits, n)
                nc.scalar.activation(rows[:, 3].rearrange("p (b n) -> p b n", b=2), ps[:, BX:BX + 2], ACT.Copy
                                     ).then_inc(rt_xTc, 1)
                if t + 1 < TILES:
                    moe_split_h(a, l, t + 1, t + 1, 0)
            a.wait_ge(rt_picked, 2 * l + 2)
            nc.scalar.activation(ex[:], ex[:], ACT.Exp).then_inc(rt_exp, 1)

        def route_tensor(pe, l):
            if l == 0:
                pe.wait_ge(ld_route, 16 * 8)
            for t in range(TILES):
                n = TILES * l + t
                pe.wait_ge(rt_xn, n + 1)
                if t:
                    pe.wait_ge(rt_xTc, n)
                for k in range(KD):
                    last = nc.tensor.transpose(ps[:, BX + k // 4, (k % 4) * P:(k % 4 + 1) * P],
                                               rows[:, t, k * P:(k + 1) * P], ident)
                last.then_inc(rt_xT, 1)
                pe.wait_ge(rt_xTc, n + 1)
                for k in range(KD):
                    last = nc.tensor.matmul(ps[:, BR, 32 * t:32 * t + NT], rows[:, 3, k * P:(k + 1) * P],
                                            wroute[:, l, k, :], start=k == 0, stop=k == KD - 1)
                last.then_inc(rt_logits, 1)
            pe.wait_ge(rt_picked, 2 * l + 1)
            for t in range(TILES + 1):
                for s in range(min(t + 1, TILES)):
                    last = nc.tensor.matmul(ps[:, BR, 128 + t * NE:128 + (t + 1) * NE], upper if s == t else ones,
                                            picked[:, s], start=s == 0, stop=s == min(t, TILES - 1))
            last.then_inc(rt_rank, 1)

        def moe_split_h(a, l, j, slot, q):
            split_h(a, M_MOE[l] + j, slot, split_moe[slot][0], raw_count(l, slot, q),
                    M_MOE[l] + (0 if isinstance(j, int) and j < 3 else j - 2))

        def moe_split_l(v, l, j, slot):
            split_l(v, M_MOE[l] + j, slot, *split_moe[slot])

        def x_banks():
            return ps[:, BX:BX + 2, 0:4 * CAP].rearrange("p b (k t) -> p b k t", t=CAP)

        def x_part(x):
            return x[:].rearrange("p (b k) t -> p b k t", b=2)

        def moe_scalar(a, l):
            E0 = NE * l
            def x_high(e, par):
                a.wait_ge(xT_done, E0 + e + 1)
                nc.scalar.activation(x_part(xsplit[par][0]), x_banks(), ACT.Copy).then_inc(xh_ready, 1)

            def hidden_high(e):
                a.wait_ge(hT_done, E0 + e + 1)
                nc.scalar.activation(hth[:], ps[:, BH, 0:KE * CAP].rearrange("p (k t) -> p k t", t=CAP), ACT.Copy
                                     ).then_inc(hh_ready, 1)

            def y_copy(e, par):
                a.wait_ge(w_used, M_MOE[l] + (3 * NE if is_last(e) else 3 * e + 5))
                at_least(a, y_stored, 16 * (E0 + e - 1))
                nc.scalar.activation(rows[0:CAP, 2 + par].rearrange("p (b n) -> p b n", b=2), ps[0:CAP, BY:BY + 2],
                                     ACT.Copy).then_inc(y_out, 1)

            x_high(0, 0)

            def step(e, par):
                a.wait_ge(w_used, M_MOE[l] + (1 if is_first(e) else 3 * e))
                at_least(a, hid_done, E0 + e)
                nc.scalar.activation(sil[:], ps[0:CAP, BA], ACT.Silu).then_inc(silu_done, 1)
                if not is_first(e):
                    hidden_high(e - 1)
                if is_first(e):
                    moe_split_h(a, l, 3, 0, 1)
                else:
                    moe_split_h(a, l, 3 * e + 2, 2, e)
                if is_last(e):
                    y_copy(e - 1, 1 - par)
                    return
                x_high(e + 1, 1 - par)
                if is_first(e):
                    moe_split_h(a, l, 4, 1, 1)
                else:
                    moe_split_h(a, l, 3 * e + 3, 0, e + 1)
                    y_copy(e - 1, 1 - par)
                    moe_split_h(a, l, 3 * e + 4, 1, e + 1)

            experts(a, step)
            hidden_high(NE - 1)
            y_copy(NE - 1, 1)
            a.wait_ge(rt_table, l + 1)
            n_over = a.value_load(ovt_i[0:1, 2 * EXTRA:2 * EXTRA + 1], min_val=0, max_val=EXTRA)
            s = over[l]
            with a.Fori(0, EXTRA) as i:
                with a.If(n_over > i):
                    a.wait_ge(s["pe"], 4 * i + 1)
                    nc.scalar.activation(rows[:, 1, 0:KD * CAP].rearrange("p (b k t) -> p b k t", b=2, t=CAP), x_banks(),
                                         ACT.Copy).then_inc(s["act"], 1)
                    a.wait_ge(s["pe"], 4 * i + 2)
                    nc.scalar.activation(sil[:], ps[0:CAP, BA], ACT.Silu).then_inc(s["act"], 1)
                    a.wait_ge(s["pe"], 4 * i + 3)
                    nc.scalar.activation(rows[:, 3, 0:KE * CAP], ps[:, BH, 0:KE * CAP], ACT.Copy).then_inc(s["act"], 1)
                    a.wait_ge(s["pe"], 4 * i + 4)
                    nc.scalar.activation(rows[0:CAP, 2].rearrange("p (b n) -> p b n", b=2), ps[0:CAP, BY:BY + 2],
                                         ACT.Copy).then_inc(s["act"], 1)

        def moe_vector(v, l):
            E0 = NE * l

            def x_low(e, par):
                v.wait_ge(xh_ready, E0 + e + 1)
                nc.vector.tensor_tensor(x_part(xsplit[par][1]), x_banks(), x_part(xsplit[par][0]).bitcast(F32),
                                        ALU.subtract).then_inc(xl_ready, 1)

            def hidden_low(e):
                v.wait_ge(hh_ready, E0 + e + 1)
                nc.vector.tensor_tensor(htl[:], ps[:, BH, 0:KE * CAP].rearrange("p (k t) -> p k t", t=CAP),
                                        hth[:].bitcast(F32), ALU.subtract).then_inc(hl_ready, 1)

            x_low(0, 0)
            table_vector(v)

            def step(e, par):
                if not is_first(e):
                    hidden_low(e - 1)
                moe_split_l(v, l, 3 if is_first(e) else 3 * e + 2, 0 if is_first(e) else 2)
                v.wait_ge(w_used, M_MOE[l] + (2 if is_first(e) else 3 * e + 1))
                v.wait_ge(silu_done, E0 + e + 1)
                nc.vector.tensor_tensor(hid[:], sil[:], ps[0:CAP, BB], ALU.mult).then_inc(hid_done, 1)
                if is_last(e):
                    return
                x_low(e + 1, 1 - par)
                if is_first(e):
                    moe_split_l(v, l, 4, 1)
                else:
                    moe_split_l(v, l, 3 * e + 3, 0)
                    moe_split_l(v, l, 3 * e + 4, 1)

            experts(v, step)
            hidden_low(NE - 1)
            n_over = v.value_load(ovt_i[0:1, 2 * EXTRA:2 * EXTRA + 1], min_val=0, max_val=EXTRA)
            s = over[l]
            with v.Fori(0, EXTRA) as i:
                with v.If(n_over > i):
                    v.wait_ge(s["act"], 4 * i + 2)
                    nc.vector.tensor_tensor(hid[:], sil[:], ps[0:CAP, BB], ALU.mult).then_inc(s["hid"], 1)
            for t in range(TILES):
                v.wait_ge(y_back[t], 32 * (l + 1))
                dve_link(v, nc.vector.scalar_tensor_tensor(h[:, t], y_rows[2 * t], wts[:, 0, t:t + 1], h[:, t],
                                                           ALU.mult, ALU.add))
                nc.vector.scalar_tensor_tensor(h[:, t], y_rows[2 * t + 1], wts[:, 1, t:t + 1], h[:, t],
                                               ALU.mult, ALU.add).then_inc(combined, 1)
            v.wait_ge(combined, TILES * (l + 1))

        def moe_tensor(pe, l):
            E0, m0 = NE * l, M_MOE[l]

            def transpose_x(e, par):
                pe.wait_ge(x_loaded[par], 8 * (E0 + e - par) + 16)
                at_least(pe, xl_ready, E0 + e)
                for k in range(KD):
                    last = nc.tensor.transpose(ps[:, BX + k // 4, (k % 4) * CAP:(k % 4 + 1) * CAP],
                                               rows[0:CAP, par, k * P:(k + 1) * P], ident[0:CAP, 0:CAP])
                last.then_inc(xT_done, 1)

            def product_x(e, par, j, slot, bank):
                wh, wl = [moe_w_view(w[:], KD) for w in split_moe[slot]]
                xh, xl = xsplit[par]
                return split_product(pe, m0 + j, [[ps[0:CAP, bank]]], lambda t, k: xh[:, k], lambda t, k: xl[:, k],
                                     wh, wl, KD, 1)

            def transpose_hidden(e):
                pe.wait_ge(hid_done, E0 + e + 1)
                at_least(pe, hl_ready, E0 + e)
                for k in range(KE):
                    last = nc.tensor.transpose(ps[:, BH, k * CAP:(k + 1) * CAP], hid[:, k * P:(k + 1) * P],
                                               ident[0:CAP, 0:CAP])
                last.then_inc(hT_done, 1)

            def product_y(e, j, slot):
                pe.wait_ge(hl_ready, E0 + e + 1)
                at_least(pe, y_out, E0 + e)
                wh, wl = [moe_w_view(w[:], KE) for w in split_moe[slot]]
                split_product(pe, m0 + j, [[ps[0:CAP, BY], ps[0:CAP, BY + 1]]], lambda t, k: hth[:, k],
                              lambda t, k: htl[:, k], wh, wl, KE, 2).then_inc(w_used, 1)

            transpose_x(0, 0)

            def step(e, par):
                f = is_first(e)
                pe.wait_ge(xl_ready, E0 + e + 1)
                at_least(pe, silu_done, E0 + e)
                product_x(e, par, 0 if f else 3 * e - 1, 0 if f else 2, BA).then_inc(w_used, 1)
                if not f:
                    transpose_hidden(e - 1)
                at_least(pe, hid_done, E0 + e)
                product_x(e, par, 1 if f else 3 * e, 1 if f else 0, BB).then_inc(w_used, 1)
                if not is_last(e):
                    transpose_x(e + 1, 1 - par)
                if not f:
                    product_y(e - 1, 3 * e + 1, 1)

            experts(pe, step)
            transpose_hidden(NE - 1)
            product_y(NE - 1, 3 * NE - 1, 2)
            pe.wait_ge(rt_table, l + 1)
            n_over = pe.value_load(ovt_i[0:1, 2 * EXTRA:2 * EXTRA + 1], min_val=0, max_val=EXTRA)
            s = over[l]
            with pe.Fori(0, EXTRA) as i:
                with pe.If(n_over > i):
                    pe.wait_ge(s["x"], 16 * i + 16)
                    pe.wait_ge(s["st"], 16 * i + 16)
                    for k in range(KD):
                        last = nc.tensor.transpose(ps[:, BX + k // 4, (k % 4) * CAP:(k % 4 + 1) * CAP],
                                                   rows[0:CAP, 0, k * P:(k + 1) * P], ident[0:CAP, 0:CAP])
                    last.then_inc(s["pe"], 1)
                    pe.wait_ge(s["act"], 4 * i + 1)
                    pe.wait_ge(s["w"], 48 * i + 48)
                    for bank, slot in ((BA, 0), (BB, 1)):
                        for k in range(KD):
                            last = nc.tensor.matmul(ps[0:CAP, bank], rows[:, 1, k * CAP:(k + 1) * CAP],
                                                    moe_w_view(raw[:, slot], KD)[:, k], start=k == 0, stop=k == KD - 1)
                    last.then_inc(s["pe"], 1)
                    pe.wait_ge(s["hid"], i + 1)
                    for k in range(KE):
                        last = nc.tensor.transpose(ps[:, BH, k * CAP:(k + 1) * CAP], hid[:, k * P:(k + 1) * P],
                                                   ident[0:CAP, 0:CAP])
                    last.then_inc(s["pe"], 1)
                    pe.wait_ge(s["act"], 4 * i + 3)
                    for c in range(2):
                        for k in range(KE):
                            last = nc.tensor.matmul(ps[0:CAP, BY + c], rows[:, 3, k * CAP:(k + 1) * CAP],
                                                    moe_w_view(raw[:, 2], KE)[:, k, c * 512:c * 512 + 512],
                                                    start=k == 0, stop=k == KE - 1)
                    last.then_inc(s["pe"], 1)

        at = ExitStack()
        KC = 2 * P
        KALL = KC + P
        cst = sb("at_cache", [P, 2 * DECB, KVR + ROPE], F32, at)
        cTs = sb("at_cache_cT", [P, DECB, 2, KC], F32, at)
        w_uk = sb("at_w_uk", [P, 2, HEADS * NOPE], F32, at)
        krT = sb("at_krT", [QK, DECB + 1, KC], F32, at)
        rinv = sb("at_rinv", [P, DECB, KALL], F32, at)
        qa = sb("at_qa", [P, 2, DECB, HEADS * DECS], F32, at)
        sqT = qa[:].rearrange("p s b n -> p s (b n)")
        pcT = sb("at_pcT", [P, 2, HEADS, DECB, DECS], F32, at)
        wukT = pcT[0:QK].rearrange("p s h b q -> p (s h b q)").rearrange("p (h n) -> p h n", h=HEADS)
        gain2 = sb("at_gain", [P, D], F32, at)
        work = sb("at_work", [P, 4, D], F32, at)
        c_sb = sb("at_c", [P, TILES, KVR + ROPE], F32, at)
        q_sb = sb("at_q", [P, TILES, HEADS, QK], F32, at)
        kr = sb("at_krope", [P, TILES, ROPE], F32, at)
        rot = raw[:, 2, WCOL - 2 * 24 * 16:].rearrange("p (i n c) -> p i n c", i=2, c=ROPE // 2)
        g_kva, g_kr = sb("at_g_kva", [P, KVR], F32, at), sb("at_g_kr", [P, ROPE], F32, at)
        g_qa, g_qr = sb("at_g_qa", [P, QR], F32, at), sb("at_g_qr", [P, ROPE], F32, at)
        g_qk = sb("at_g_qk", [QK, 3], F32, at)
        ast = sb("at_stat", [P, 64], F32, at)
        qT = sb("at_qT", [QK, 2, HEADS, P], F32, at)
        qTs = gain2[0:QK].rearrange("p (b n) -> p b n", b=DECB)
        cqT = sb("at_cqT", [P, 3, P], F32, at)
        kst = sb("at_kstat", [P, 2, HEADS], F32, at)
        kcat = sb("at_kcat", [P, 2, HEADS, QK], F32, at)
        cq_sb = kcat[:].rearrange("p a h n -> p (a h n)")[:, 0:TILES * QR].rearrange("p (t n) -> p t n", t=TILES)
        kTp = raw[0:QK, 1, 0:HEADS * SEQ].rearrange("p (h k) -> p h k", h=HEADS)
        vp = raw[:, 1, HEADS * SEQ:HEADS * SEQ + 2 * HEADS * VD].rearrange("p (t n) -> p t n", t=2)
        new_rinv = sb("at_new_rinv", [P, P], F32, at)
        cTn = sb("at_cTn", [P, 2, P], F32, at)
        q_words = q_sb[:].rearrange("p t h n -> p (t h n)")
        s_sb = q_words[:, 0:2 * KALL].rearrange("p (a k) -> p a k", a=2)
        psT = q_words[:, 2 * KALL:4 * KALL].rearrange("p (a k) -> p a k", a=2)
        sst = sb("at_sample_stat", [P, 2, 3], F32, at)
        oT = sb("at_oT", [P, 4, TOK], F32, at)
        rmax = sb("at_rmax", [P, 2, HEADS], F32, at)
        rsum = sb("at_rsum", [P, 2, HEADS], F32, at)
        at.close()
        p_sb = work[:, 0:2].rearrange("p a n -> p (a n)")
        pT = work[:, 2:4].rearrange("p a n -> p (a n)")
        w_dkv = raw[:, 0, 0:KD * 288].rearrange("p (k n) -> p k n", k=KD)
        w_dq = raw[:, 1, 0:KD * QR].rearrange("p (k n) -> p k n", k=KD)
        w_uv = raw[:, 1, KD * QR:].rearrange("p (k n) -> p k n", k=2)
        w_uq = raw[:, 2, 0:3 * 768].rearrange("p (k n) -> p k n", k=3)
        cT = raw[:, 2, 3 * 768:3 * 768 + 512].rearrange("p (a s t) -> p a s t", a=2, s=2)
        sq = raw[:, 2, 3 * 768 + 512:3 * 768 + 1024]
        w_o = raw[:, 2, :].rearrange("p (k n) -> p k n", k=4)

        ld_at, ld_atg, ld_kvg, ld_wo = sem("ld_at"), sem("ld_atg"), sem("ld_kvg"), sem("ld_wo")
        ld_at2 = sem("ld_at2")
        lat_stored, ld_cache = sem("lat_stored"), [sem("ld_cache0"), sem("ld_cache1")]
        uk_T, uk_Tc, ch_T, ch_c, ch_K, ch_sq, ch_ssq, ch_rms, ch_rinv = map(
            sem, ["uk_T", "uk_Tc", "ch_T", "ch_cd", "ch_K", "ch_sqd", "ch_ssq", "ch_rmsd", "ch_rinvd"])
        nw_T, nw_Tc, nw_K, nw_sq, nw_ssq, nw_rinv, sq_ready = map(
            sem, ["nw_T", "nw_Tc", "nw_K", "nw_sqd", "nw_ssq", "nw_rinvd", "sq_readyd"])
        qa_done, qa_copied = sem("qa_done"), sem("qa_copied")
        sm_s, sm_step, sm_max, sm_exp, sm_rsum, sm_p, sm_pT, sm_pTc, sm_pc, sm_pcc = map(
            sem, ["sm_s", "sm_step", "sm_maxd", "sm_expd", "sm_rsum", "sm_p", "sm_pT", "sm_pTc", "sm_pc", "sm_pcc"])
        sm_o, pads_zeroed = sem("sm_o"), sem("pads_zeroed")
        at_xn, at_xT, at_xc, at_proj, at_projc = map(sem, ["at_xn", "at_xTd", "at_xc", "at_proj", "at_projc"])
        at_lat, at_cqn, at_cqT, at_cqTc, at_qd, at_qc = map(
            sem, ["at_lat", "at_cqn", "at_cqTd", "at_cqTc", "at_qd", "at_qc"])
        at_qn, at_qT, at_qTc = sem("at_qn"), sem("at_qTd"), sem("at_qTc")
        at_T, at_cTc, at_kv, at_sq, at_red, at_ms, at_rt = map(
            sem, ["at_T", "at_cTc", "at_kv", "at_sqd", "at_red", "at_ms", "at_rt"])
        at_v, at_kcat, at_KT, at_kT = sem("at_v"), sem("at_kcatd"), sem("at_KT"), sem("at_kTd")
        at_sc, at_p1, at_e, at_p2, at_PTc, at_pv, at_o = map(
            sem, ["at_sc", "at_p1", "at_e", "at_p2", "at_PTc", "at_pv", "at_o"])
        at_y = sem("at_y")
        NEW = 2

        def pairs_of(eng, step, n):
            step(0, 0)
            with eng.Fori(0, n // 2 - 1) as i:
                step(2 * i + 1, 1)
                step(2 * i + 2, 0)
            step(n - 1, 1)

        def load_cached(sp, half):
            n = slice(8 * half, 8 * half + 8)
            sp.dma_start(cst[:, n, 0:KVR], A["cache_ckv"].rearrange("b (t p) r -> p (b t) r", p=P)[:, n]
                         ).then_inc(ld_cache[half], 16)
            sp.dma_start(cst[:, n, KVR:], A["cache_krope"].rearrange("b (t p) r -> p (b t) r", p=P)[:, n]
                         ).then_inc(ld_cache[half], 16)

        def load_cache(sp):
            sp.dma_start(w_uk[:], A["w_uk"].rearrange("(k p) h n -> p k (h n)", p=P)).then_inc(ld_cache[0], 16)
            load_cached(sp, 0)

        def at_sync(sp):
            for t in range(TILES):
                sp.wait_ge(y_back[t], 32)
            sp.dma_start(w_dkv, A["w_dkv"].rearrange("(k p) n -> p k n", p=P)).then_inc(ld_at, 16)
            sp.dma_start(w_dq, A["w_dq"][0].rearrange("(k p) n -> p k n", p=P)).then_inc(ld_at, 16)
            load_cached(sp, 1)
            sp.dma_start(w_uq, A["w_uq"][0].rearrange("(k p) h n -> p k (h n)", p=P)).then_inc(ld_at2, 16)
            sp.dma_start(w_uv, A["w_uv"].rearrange("(k p) h n -> p k (h n)", p=P)).then_inc(ld_at2, 16)
            sp.wait_ge(at_qn, 1)
            sp.dma_start(w_o, A["w_o"][0].rearrange("(k p) n -> p k n", p=P)).then_inc(ld_wo, 16)

        def at_pool(g):
            g.dma_start(gain2[:], A["norm_mix"][1:2, :].partition_broadcast(P)).then_inc(ld_kvg, 16)
            g.wait_ge(combined, TILES)
            g.dma_start(g_kva[:], A["kv_a_norm"].rearrange("(a n) -> a n", a=1).partition_broadcast(P)).then_inc(ld_atg, 16)
            g.dma_start(g_kr[:], A["k_rope_norm"].rearrange("(a n) -> a n", a=1).partition_broadcast(P)).then_inc(ld_atg, 16)
            g.dma_start(g_qa[:], A["q_a_norm"].partition_broadcast(P)).then_inc(ld_atg, 16)
            g.dma_start(g_qr[:], A["q_rope_norm"].partition_broadcast(P)).then_inc(ld_atg, 16)
            g.dma_start(g_qk[0:NOPE, 0:1], A["q_nope_norm"][0].rearrange("(n a) -> n a", a=1),
                        allow_slow_non_contiguous=True).then_inc(ld_atg, 16)
            g.dma_start(g_qk[0:NOPE, 1:2], A["k_nope_norm"].rearrange("(n a) -> n a", a=1),
                        allow_slow_non_contiguous=True).then_inc(ld_atg, 16)
            g.wait_ge(at_lat, 1)
            for t in range(2):
                g.dma_start(O[2][0, t * P:(t + 1) * P, :], c_sb[:, t, 0:KVR]).then_inc(lat_stored, 16)
                g.dma_start(O[3][0, t * P:(t + 1) * P, :], kr[:, t, :]).then_inc(lat_stored, 16)
            g.dma_start(O[4].rearrange("b s r -> (b s) r"), c_sb[:, SAMPLE, 0:KVR]).then_inc(lat_stored, 16)
            g.dma_start(O[5].rearrange("b s r -> (b s) r"), kr[:, SAMPLE, :]).then_inc(lat_stored, 16)

        def normalise(v, x, parts):
            for a, b, st in parts:
                n, w = x.shape[1], b - a
                s3 = [P, n, w]
                j = work[:, 0:4].rearrange("p a n -> p (a n)")[:, 0:n * w].rearrange("p (n w) -> p n w", n=n)
                dve_link(v, nc.vector.tensor_tensor(j, x[:, :, a:b], x[:, :, a:b], ALU.mult))
                dve_link(v, nc.vector.tensor_reduce(st, j, AX.X, ALU.add))
                dve_link(v, nc.vector.tensor_scalar(st, st, 1.0 / w, None, ALU.mult))

        def scale_rows(v, x, a, b, st, gain_row=None):
            shape = [P, x.shape[1], b - a]
            dve_link(v, nc.vector.tensor_tensor(x[:, :, a:b], x[:, :, a:b], st.unsqueeze(2).to_broadcast(shape), ALU.mult))
            if gain_row is not None:
                dve_link(v, nc.vector.tensor_tensor(x[:, :, a:b], x[:, :, a:b],
                                                    gain_row.unsqueeze(1).to_broadcast(shape), ALU.mult))

        def rotate(v, x, out, cos, sin, shape):
            half = ROPE // 2
            x1, x2 = x[..., 0:half], x[..., half:ROPE]
            n = 1
            for s in shape[1:-1]:
                n *= s
            r = [rot[:, i, 0:n] if len(shape) == 3 else rot[:, i, 0:n].rearrange("p (t h) c -> p t h c", h=HEADS)
                 for i in range(2)]
            dve_link(v, nc.vector.tensor_tensor(r[0], x1, sin, ALU.mult))
            dve_link(v, nc.vector.tensor_tensor(r[1], x2, sin, ALU.mult))
            dve_link(v, nc.vector.tensor_tensor(out[..., 0:half], x1, cos, ALU.mult))
            dve_link(v, nc.vector.tensor_tensor(out[..., half:ROPE], x2, cos, ALU.mult))
            dve_link(v, nc.vector.tensor_tensor(out[..., 0:half], out[..., 0:half], r[1], ALU.subtract))
            dve_link(v, nc.vector.tensor_tensor(out[..., half:ROPE], out[..., half:ROPE], r[0], ALU.add))

        def at_vector(v):
            inverse_rms(v, work[:, 0])
            v.wait_ge(ld_kvg, 32)
            for t in range(TILES):
                if t:
                    v.wait_ge(at_xT, 2 * t)
                norm_rows(t, work[:, 0]).then_inc(at_xn, 1)
                nc.vector.scalar_tensor_tensor(work[:, 1], h[:, t], stat[:, 1, t:t + 1], gain2[:], ALU.mult, ALU.mult
                                               ).then_inc(at_xn, 1)
                if t == 0:
                    mean_squares(v, 0)
            inverse_key_rms(v, 0)
            nc.vector.memset(krT[0:NOPE], 0.0).then_inc(pads_zeroed, 1)
            nc.vector.memset(wukT[NOPE:QK], 0.0).then_inc(pads_zeroed, 1)
            dve_link(v, nc.vector.memset(g_qk[NOPE:QK, :], 1.0))
            v.wait_ge(ld_atg, 96)
            v.wait_ge(at_projc, 2 * TILES)
            c_all, cq_all = c_sb[:], cq_sb
            normalise(v, c_all, [(0, KVR, ast[:, 0:3]), (KVR, KVR + ROPE, ast[:, 3:6])])
            normalise(v, cq_all, [(0, QR, ast[:, 6:9])])
            rms_inverse(v, ast[:, 0:9], ast[:, 0:9], 1.0)
            scale_rows(v, cq_all, 0, QR, ast[:, 6:9], g_qa[:])
            nc.vector.memset(ast[:, 60:61], 0.0).then_inc(at_cqn, 1)
            dve_link(v, nc.vector.tensor_tensor(g_qk[0:NOPE, 2:3], g_qk[0:NOPE, 0:1], g_qk[0:NOPE, 1:2], ALU.mult))
            scale_rows(v, c_all, 0, KVR, ast[:, 0:3], g_kva[:])
            scale_rows(v, c_all, KVR, KVR + ROPE, ast[:, 3:6], g_kr[:])
            cos3 = const[:, C_COS:C_COS + 48].rearrange("p (t c) -> p t c", t=TILES)
            sin3 = const[:, C_SIN:C_SIN + 48].rearrange("p (t c) -> p t c", t=TILES)
            rotate(v, c_sb[:, :, KVR:], kr[:], cos3, sin3, [P, TILES, 16])
            nc.vector.tensor_copy(c_sb[:, SAMPLE, KVR:], kr[:, SAMPLE]).then_inc(at_lat, 1)
            mean_squares(v, 1)
            inverse_key_rms(v, 1)
            for t in range(TILES):
                v.wait_ge(at_qc, t + 1)
                j = work[:, 0, 0:HEADS * QK].rearrange("p (h n) -> p h n", h=HEADS)
                dve_link(v, nc.vector.tensor_tensor(j, q_sb[:, t], q_sb[:, t], ALU.mult))
                for a_, b_, c_ in ((0, NOPE, 10), (NOPE, QK, 34)):
                    st = ast[:, c_ + HEADS * t:c_ + HEADS * (t + 1)]
                    dve_link(v, nc.vector.tensor_reduce(st, j[:, :, a_:b_], AX.X, ALU.add))
                    dve_link(v, nc.vector.tensor_scalar(st, st, 1.0 / (b_ - a_), None, ALU.mult))
            rms_inverse(v, ast[:, 10:58], ast[:, 10:58], 1.0)
            for n in range(NEW):
                key_rows(v, n, n % 2, kr[:, n])
            q24 = q_sb[:].rearrange("p t h n -> p (t h) n")
            scale_rows(v, q24, 0, NOPE, ast[:, 10:34])
            scale_rows(v, q24, NOPE, QK, ast[:, 34:58], g_qr[:])
            shape = [P, TILES, HEADS, 16]
            qr_ = q_sb[:, :, :, NOPE:QK]
            tmpq = work[:, 0, 0:TILES * HEADS * ROPE].rearrange("p (t h c) -> p t h c", t=TILES, h=HEADS)
            rotate(v, qr_, tmpq, cos3.unsqueeze(2).to_broadcast(shape), sin3.unsqueeze(2).to_broadcast(shape), shape)
            nc.vector.tensor_copy(qr_, tmpq).then_inc(at_qn, 1)
            v.wait_ge(nw_ssq, 1)
            nc.vector.tensor_scalar(new_rinv[:], ps[:, 7, 0:P], 1.0 / NOPE, EPS, ALU.mult, ALU.add).then_inc(nw_rinv, 1)
            for t in range(2):
                prompt_softmax(v, t)
            v.wait_ge(sq_ready, 1)
            dve_link(v, nc.vector.reciprocal(new_rinv[:], new_rinv[:]))
            dve_link(v, nc.vector.tensor_copy(rinv[:, :, KC:], new_rinv[:].unsqueeze(1).to_broadcast([P, DECB, P])))
            v.wait_ge(qa_done, 1)
            nc.vector.tensor_copy(qa[:, 1].rearrange("p b (h q) -> p h b q", h=HEADS),
                                  ps[:, 2:4].rearrange("p c (h b q) -> p (c h) b q", h=4, b=DECB)).then_inc(qa_copied, 1)
            scores(v, 0, 0)

            def step(b, par):
                v.wait_ge(sm_exp, b + 1)
                nc.vector.reciprocal(sst[:, par, 2:3], sst[:, par, 2:3]).then_inc(sm_rsum, 1)
                v.wait_ge(sm_rsum, b + 1)
                nc.vector.tensor_scalar(s_sb[:, par], s_sb[:, par], sst[:, par, 2:3], None, ALU.mult).then_inc(sm_p, 1)
                if not (isinstance(b, int) and b == DECB - 1):
                    scores(v, b + 1, 1 - par)

            pairs_of(v, step, DECB)
            v.wait_ge(sm_o, 1)
            o3 = ps[:, 0:2].rearrange("p b (h x q) -> p (b h) x q", h=2, x=2)
            nc.vector.tensor_copy(oT[0:VD, :, SEQ:], o3[0:VD, :, 0]).then_inc(at_o, 1)
            nc.vector.tensor_copy(oT[VD:P, :, SEQ:], o3[VD:P, :, 1]).then_inc(at_o, 1)
            v.wait_ge(at_y, 1)
            v.wait_ge(lat_stored, 96)
            for t in range(TILES):
                nc.vector.tensor_tensor(h[:, t].rearrange("p (c n) -> p c n", c=2), h[:, t].rearrange("p (c n) -> p c n", c=2),
                                        ps[:, 2 * t:2 * t + 2], ALU.add).then_inc(h_mixed, 1)
            v.wait_ge(h_mixed, 2 * TILES)

        def mean_squares(v, half):
            v.wait_ge(ch_ssq, 4 * half + 4)
            nc.vector.tensor_scalar(rinv[:, 4 * half:4 * half + 4, 0:KC], ps[:, 6:8].rearrange("p b (x k) -> p (b x) k", x=2),
                                    1.0 / NOPE, EPS, ALU.mult, ALU.add).then_inc(ch_rms, 1)

        def inverse_key_rms(v, half):
            v.wait_ge(ch_rinv, half + 1)
            x = rinv[:, 4 * half:4 * half + 4, 0:KC]
            dve_link(v, nc.vector.reciprocal(x, x))

        def scores(v, b, par):
            v.wait_ge(sm_s, b + 1)
            if not (isinstance(b, int) and b < 2):
                v.wait_ge(sm_pT, b - 1)
            x = s_sb[:, par]
            nc.vector.tensor_tensor(x, ps[:, par, 0:KALL], rinv[:, bass.ds(b, 1)].rearrange("p a k -> p (a k)"), ALU.mult
                                    ).then_inc(sm_step, 1)
            v.wait_ge(sm_step, 4 * b + 1)
            nc.vector.tensor_tensor(x, x, ps[:, 2 + par, 0:KALL], ALU.add).then_inc(sm_step, 1)
            v.wait_ge(sm_step, 4 * b + 2)
            own = const[:, bass.ds(C_OWN + P - DECS - DECS * b, P)]
            nc.vector.tensor_tensor(x[:, KC:], x[:, KC:], own, ALU.add).then_inc(sm_step, 1)
            v.wait_ge(sm_step, 4 * b + 3)
            nc.vector.tensor_reduce(sst[:, par, 0:1], x, AX.X, ALU.max).then_inc(sm_step, 1)
            v.wait_ge(sm_step, 4 * b + 4)
            nc.vector.tensor_scalar(sst[:, par, 1:2], sst[:, par, 0:1], -SCALE, None, ALU.mult).then_inc(sm_max, 1)

        def key_rows(v, n, par, rope_rows):
            k3 = ps[:, 1 + par].rearrange("p (h d) -> p h d", h=HEADS)
            v.wait_ge(at_sq, n + 1)
            nc.vector.tensor_reduce(kst[:, par], sq[:].rearrange("p (h d) -> p h d", h=HEADS), AX.X, ALU.add
                                    ).then_inc(at_red, 1)
            v.wait_ge(at_red, n + 1)
            nc.vector.tensor_scalar(kst[:, par], kst[:, par], 1.0 / NOPE, EPS, ALU.mult, ALU.add).then_inc(at_ms, 1)
            v.wait_ge(at_rt, 2 * n + 1)
            nc.vector.reciprocal(kst[:, par], kst[:, par]).then_inc(at_rt, 1)
            if not (isinstance(n, int) and n < 2):
                v.wait_ge(at_KT, n - 1)
            nc.vector.tensor_copy(kcat[:, par, :, NOPE:], rope_rows.unsqueeze(1).to_broadcast([P, HEADS, ROPE])
                                  ).then_inc(at_kcat, 1)
            v.wait_ge(at_rt, 2 * n + 2)
            nc.vector.tensor_tensor(kcat[:, par, :, 0:NOPE], k3, kst[:, par].unsqueeze(2).to_broadcast([P, HEADS, NOPE]),
                                    ALU.mult).then_inc(at_kcat, 1)

        def at_most_units(v, U, x, shape, n_max):
            hd = shape[1]
            m, s = rmax[:, 0, 0:hd], rsum[:, 0, 0:hd]
            nc.vector.tensor_reduce(m, x, AX.X, ALU.max).then_inc(at_p2x, 1)
            v.wait_ge(at_p2x, 3 * U + 1)
            nc.vector.tensor_tensor(x, x, m.unsqueeze(2).to_broadcast(shape), ALU.subtract).then_inc(at_p1, 1)
            v.wait_ge(at_e, U + 1)
            nc.vector.tensor_reduce(s, x, AX.X, ALU.add).then_inc(at_p2x, 1)
            v.wait_ge(at_p2x, 3 * U + 2)
            nc.vector.reciprocal(s, s).then_inc(at_p2x, 1)
            v.wait_ge(at_p2x, 3 * U + 3)
            nc.vector.tensor_tensor(x, x, s.unsqueeze(2).to_broadcast(shape), ALU.mult).then_inc(at_p2, 1)

        at_p2x, at_ps = sem("at_p2x"), sem("at_ps")

        def prompt_softmax(v, t):
            nk = (t + 1) * P
            p3 = p_sb.rearrange("p (h k) -> p h k", h=HEADS)
            s3 = ps[:, 0:4].rearrange("p b (h k) -> p (b h) k", h=2)
            v.wait_ge(at_sc, t + 1)
            if t:
                v.wait_ge(at_PTx, t)
            else:
                v.wait_ge(at_qT, TILES)
            if t:
                nc.vector.tensor_scalar(p3[:, :, 0:P], s3[:, :, 0:P], SCALE, None, ALU.mult).then_inc(at_ps, 1)
            own = slice(t * P, (t + 1) * P)
            nc.vector.scalar_tensor_tensor(p3[:, :, own], s3[:, :, own], SCALE,
                                           const[:, C_MASK:C_MASK + P].unsqueeze(1).to_broadcast([P, HEADS, P]),
                                           ALU.mult, ALU.add).then_inc(at_ps, 1)
            v.wait_ge(at_ps, [1, 3][t])
            at_most_units(v, t, p3[:, :, 0:nk], [P, HEADS, nk], nk)
            v.wait_ge(at_pv, t + 1)
            o3 = ps[:, 6:8].rearrange("p b (h x q) -> p (b h) x q", h=2, x=2)
            nc.vector.tensor_copy(oT[0:VD, :, t * P:(t + 1) * P], o3[0:VD, :, 0]).then_inc(at_o, 1)
            nc.vector.tensor_copy(oT[VD:P, :, t * P:(t + 1) * P], o3[VD:P, :, 1]).then_inc(at_o, 1)

        def at_scalar(a):
            a.wait_ge(uk_T, 1)
            nc.scalar.activation(wukT[0:NOPE].rearrange("p h n -> p (h n)"),
                                 ps[0:NOPE, 0:4].rearrange("p b n -> p (b n)"), ACT.Copy).then_inc(uk_Tc, 1)

            def cache_copies(b):
                a.wait_ge(ch_T, b + 1)
                nc.scalar.activation(cTs[:, bass.ds(b, 1)].rearrange("p a s k -> p (a s k)"), ps[:, 0], ACT.Copy
                                     ).then_inc(ch_c, 1)
                nc.scalar.activation(krT[NOPE:QK, bass.ds(b, 1)].rearrange("p a k -> p (a k)"), ps[NOPE:QK, 1, 0:KC],
                                     ACT.Copy).then_inc(ch_c, 1)

            def squares(b):
                if b % 4 == 0:
                    cache_copies(b)
                if b % 4 < 3:
                    cache_copies(b + 1)
                for i in range(2):
                    a.wait_ge(ch_K, 2 * b + i + 1)
                    if i == 0 and b >= 2:
                        a.wait_ge(ch_ssq, b - 1)
                    nc.scalar.activation(sqT[:, b % 2, i * 512:i * 512 + 512], ps[:, 2 + i], ACT.Square).then_inc(ch_sq, 1)

            for b in range(4):
                squares(b)
            root(a, stat[:, 1, 0:TILES])
            for t in range(TILES):
                if t == 1:
                    roots_of_keys(a, 0)
                for i in range(2):
                    a.wait_ge(at_xT, 2 * t + i + 1)
                    if t:
                        a.wait_ge(at_proj, t)
                    nc.scalar.activation(work[:, 2 + i].rearrange("p (b n) -> p b n", b=2), ps[:, 2 * i:2 * i + 2],
                                         ACT.Copy).then_inc(at_xc, 1)
                a.wait_ge(at_proj, t + 1)
                nc.scalar.activation(c_sb[:, t], ps[:, 4, 0:KVR + ROPE], ACT.Copy).then_inc(at_projc, 1)
                nc.scalar.activation(cq_sb[:, t], ps[:, 5, 0:QR], ACT.Copy).then_inc(at_projc, 1)
            squares(4)
            root(a, ast[:, 0:9])
            for b in range(5, DECB):
                squares(b)
            roots_of_keys(a, 1)
            for t in range(TILES):
                a.wait_ge(at_cqT, t + 1)
                if t:
                    a.wait_ge(at_qd, t)
                nc.scalar.activation(cqT[:], ps[:, 6, 0:QR].rearrange("p (k t) -> p k t", k=3), ACT.Copy).then_inc(at_cqTc, 1)
                a.wait_ge(at_qd, t + 1)
                nc.scalar.activation(q_sb[:, t].rearrange("p (b h) n -> p b (h n)", b=2), ps[:, 4:6, 0:QR], ACT.Copy
                                     ).then_inc(at_qc, 1)
            root(a, ast[:, 10:58])
            key_tiles(a, 0, list(range(NEW)), [n % 2 for n in range(NEW)],
                      [kTp[:, :, 0:P], kTp[:, :, P:SEQ]], [vp[:, 0], vp[:, 1]])
            a.wait_ge(nw_T, 1)
            nc.scalar.activation(cTn[:].rearrange("p s k -> p (s k)"), ps[:, 6, 0:2 * P], ACT.Copy).then_inc(nw_Tc, 1)
            nc.scalar.activation(krT[NOPE:QK, DECB, 0:P], ps[NOPE:QK, 6, 2 * P:3 * P], ACT.Copy).then_inc(nw_Tc, 1)
            a.wait_ge(nw_K, 1)
            nc.scalar.activation(sqT[:, 0, 0:512], ps[:, 3], ACT.Square).then_inc(nw_sq, 1)
            for t in range(TILES):
                a.wait_ge(at_qT, t + 1)
                src = ps[0:QK, 0:2].rearrange("p c n -> p (c n)")
                if t < SAMPLE:
                    nc.scalar.activation(qT[:, t].rearrange("p h n -> p (h n)"), src, ACT.Copy,
                                         scale=g_qk[:, 0:1]).then_inc(at_qTc, 1)
                else:
                    nc.scalar.activation(qTs.rearrange("p b (h q) -> p h b q", h=HEADS),
                                         src.rearrange("p (h b q) -> p h b q", h=HEADS, b=DECB), ACT.Copy,
                                         scale=g_qk[:, 2:3]).then_inc(at_qTc, 1)
            a.wait_ge(nw_rinv, 1)
            nc.scalar.activation(new_rinv[:], new_rinv[:], ACT.Sqrt).then_inc(sq_ready, 1)
            for t in range(2):
                n = (t + 1) * P
                probabilities(a, t, p_sb.rearrange("p (h k) -> p h k", h=HEADS)[:, :, 0:n])
                for c in range(t + 1):
                    a.wait_ge(at_PTx, [0, 1][t] + c + 1)
                    nc.scalar.activation(pT.rearrange("p (c h q) -> p c h q", c=2, h=HEADS)[:, c].rearrange("p (b h) q -> p b (h q)", b=2),
                                         ps[:, 4:6], ACT.Copy).then_inc(at_PTc, 1)
            a.wait_ge(qa_done, 1)
            nc.scalar.activation(qa[:, 0].rearrange("p b (h q) -> p h b q", h=HEADS),
                                 ps[:, 0:2].rearrange("p c (h b q) -> p (c h) b q", h=4, b=DECB), ACT.Copy).then_inc(qa_copied, 1)

            def step(b, par):
                a.wait_ge(sm_max, b + 1)
                nc.scalar.activation(s_sb[:, par], s_sb[:, par], ACT.Exp, bias=sst[:, par, 1:2], scale=SCALE,
                                     accum_out=sst[:, par, 2:3]).then_inc(sm_exp, 1)
                a.wait_ge(sm_pT, b + 1)
                nc.scalar.activation(psT[:, par], ps[:, 4 + par, 0:KALL], ACT.Copy).then_inc(sm_pTc, 1)
                a.wait_ge(sm_pc, b + 1)
                nc.scalar.activation(pcT[:, :, :, bass.ds(b, 1), :].rearrange("p s h a q -> p s h (a q)"),
                                     ps[:, 6 + par, 0:2 * P].rearrange("p (s h q) -> p s h q", s=2, h=HEADS),
                                     ACT.Copy).then_inc(sm_pcc, 1)

            pairs_of(a, step, DECB)

        at_PTx = sem("at_PTx")

        def roots_of_keys(a, half):
            a.wait_ge(ch_rms, half + 1)
            x = rinv[:, 4 * half:4 * half + 4, 0:KC]
            nc.scalar.activation(x, x, ACT.Sqrt).then_inc(ch_rinv, 1)

        def probabilities(a, U, x):
            a.wait_ge(at_p1, U + 1)
            nc.scalar.activation(x, x, ACT.Exp).then_inc(at_e, 1)

        def key_tiles(a, g, ns, pars, kdst, vdst):
            def c_copy(i):
                n, par = ns[i], pars[i]
                if not (isinstance(n, int) and n < 2):
                    a.wait_ge(at_kv, n - 1)
                a.wait_ge(at_T, n + 1)
                nc.scalar.activation(cT[:, par], ps[:, 0, 0:256].rearrange("p (k t) -> p k t", k=2), ACT.Copy
                                     ).then_inc(at_cTc, 1)

            def kT_copy(i):
                a.wait_ge(at_KT, ns[i] + 1)
                d = kdst[i].rearrange("p (b h) n -> p b h n", b=2)
                nc.scalar.activation(d, ps[0:QK, 4:6].rearrange("p b (h n) -> p b h n", h=4), ACT.Copy,
                                     scale=g_qk[:, 1:2]).then_inc(at_kT, 1)

            c_copy(0)
            for i, n in enumerate(ns):
                par = pars[i]
                if i + 1 < len(ns):
                    c_copy(i + 1)
                a.wait_ge(at_kv, n + 1)
                nc.scalar.activation(vdst[i], ps[:, 3], ACT.Copy).then_inc(at_v, 1)
                at_least(a, at_red, n)
                nc.scalar.activation(sq[:], ps[:, 1 + par], ACT.Square).then_inc(at_sq, 1)
                if i:
                    kT_copy(i - 1)
                a.wait_ge(at_ms, n + 1)
                nc.scalar.activation(kst[:, par], kst[:, par], ACT.Sqrt).then_inc(at_rt, 1)
            kT_copy(len(ns) - 1)

        def at_tensor(pe):
            pe.wait_ge(ld_cache[0], 48)
            for s in range(2):
                for hh in range(HEADS):
                    last = nc.tensor.transpose(ps[0:NOPE, hh // 2, (hh % 2) * KVR + s * P:(hh % 2) * KVR + (s + 1) * P],
                                               w_uk[:, s, hh * NOPE:(hh + 1) * NOPE], ident)
            last.then_inc(uk_T, 1)
            pe.wait_ge(uk_Tc, 1)

            def turn_cache(b):
                if b:
                    pe.wait_ge(ch_c, 2 * b)
                for i in range(2):
                    row = cst[:, 2 * b + i]
                    for s in range(2):
                        nc.tensor.transpose(ps[:, 0, s * KC + i * P:s * KC + (i + 1) * P], row[:, s * P:(s + 1) * P], ident)
                    last = nc.tensor.transpose(ps[0:QK, 1, i * P:(i + 1) * P], row[:, KVR - NOPE:], ident)
                last.then_inc(ch_T, 1)

            def sum_squares(b, par):
                pe.wait_ge(ch_sq, 2 * b + 2)
                out = ps[:, 6 + b % 4 // 2, (b % 2) * KC:(b % 2 + 1) * KC]
                for hp in range(4):
                    last = nc.tensor.matmul(out, head_sums(hp), sqT[:, par, hp * KC:(hp + 1) * KC], start=hp == 0, stop=hp == 3)
                last.then_inc(ch_ssq, 1)

            def head_sums(hp):
                return const[:, C_HEADS + 96 - 32 * hp:C_HEADS + 96 - 32 * hp + P]

            def prepare(b, par):
                if b % 4 == 0:
                    pe.wait_ge(ld_cache[b // 4], 48 - 16 * (b // 4))
                    turn_cache(b)
                if b % 4 < 3:
                    turn_cache(b + 1)
                pe.wait_ge(ch_c, 2 * b + 1)
                for hp in range(4):
                    if hp % 2 == 0 and b:
                        pe.wait_ge(ch_sq, 2 * b + hp // 2 - 1)
                    for s in range(2):
                        last = nc.tensor.matmul(ps[:, 2 + hp // 2, (hp % 2) * KC:(hp % 2 + 1) * KC],
                                                w_uk[:, s, hp * P:(hp + 1) * P],
                                                cTs[:, b, s],
                                                start=s == 0, stop=s == 1)
                    if hp % 2:
                        last.then_inc(ch_K, 1)
                if b % 4:
                    sum_squares(b - 1, 1 - par)

            for b in range(4):
                prepare(b, b % 2)
            sum_squares(3, 1)
            pe.wait_ge(ld_at, 32)
            for t in range(TILES):
                for i in range(2):
                    pe.wait_ge(at_xn, 2 * t + i + 1)
                    if t:
                        pe.wait_ge(at_xc, 2 * t)
                    for k in range(KD):
                        last = nc.tensor.transpose(ps[:, 2 * i + k // 4, (k % 4) * P:(k % 4 + 1) * P],
                                                   work[:, i, k * P:(k + 1) * P], ident)
                    last.then_inc(at_xT, 1)
                at_least(pe, at_projc, 2 * t)
                pe.wait_ge(at_xc, 2 * t + 2)
                for i, (w, n) in enumerate(((w_dkv, KVR + ROPE), (w_dq, QR))):
                    for k in range(KD):
                        last = nc.tensor.matmul(ps[:, 4 + i, 0:n], work[:, 2 + i, k * P:(k + 1) * P], w[:, k],
                                                start=k == 0, stop=k == KD - 1)
                last.then_inc(at_proj, 1)
            pe.wait_ge(ch_rms, 1)
            for b in range(4, DECB):
                prepare(b, b % 2)
            sum_squares(DECB - 1, 1)
            pe.wait_ge(ld_at2, 32)
            pe.wait_ge(at_cqn, 1)
            pe.wait_ge(at_projc, 2 * TILES)
            pe.wait_ge(ch_rms, 2)
            for t in range(TILES):
                if t:
                    pe.wait_ge(at_cqTc, t)
                for k in range(3):
                    last = nc.tensor.transpose(ps[:, 6, k * P:(k + 1) * P], cq_sb[:, t, k * P:(k + 1) * P], ident)
                last.then_inc(at_cqT, 1)
                pe.wait_ge(at_cqTc, t + 1)
                if t:
                    pe.wait_ge(at_qc, t)
                for c in range(2):
                    for k in range(3):
                        last = nc.tensor.matmul(ps[:, 4 + c, 0:QR], cqT[:, k], w_uq[:, k, c * QR:(c + 1) * QR],
                                                start=k == 0, stop=k == 2)
                last.then_inc(at_qd, 1)
            pe.wait_ge(at_lat, 1)
            pe.wait_ge(at_qc, TILES)
            expand(pe, list(range(NEW)), [n % 2 for n in range(NEW)], [c_sb[:, n, 0:KVR] for n in range(NEW)])
            for s in range(2):
                nc.tensor.transpose(ps[:, 6, s * P:(s + 1) * P], c_sb[:, SAMPLE, s * P:(s + 1) * P], ident)
            nc.tensor.transpose(ps[0:QK, 6, 2 * P:3 * P], c_sb[:, SAMPLE, KVR - NOPE:], ident).then_inc(nw_T, 1)
            pe.wait_ge(nw_Tc, 2)
            pe.wait_ge(at_v, NEW)
            for hp in range(4):
                for s in range(2):
                    last = nc.tensor.matmul(ps[:, 3, hp * P:(hp + 1) * P], w_uk[:, s, hp * P:(hp + 1) * P], cTn[:, s],
                                            start=s == 0, stop=s == 1)
            last.then_inc(nw_K, 1)
            pe.wait_ge(nw_sq, 1)
            for hp in range(4):
                last = nc.tensor.matmul(ps[:, 7, 0:P], head_sums(hp), sqT[:, 0, hp * P:(hp + 1) * P], start=hp == 0, stop=hp == 3)
            last.then_inc(nw_ssq, 1)
            pe.wait_ge(at_qn, 1)
            for t in range(TILES):
                at_least(pe, at_qTc, t)
                for hh in range(HEADS):
                    last = nc.tensor.transpose(ps[0:QK, hh // 4, (hh % 4) * P:(hh % 4 + 1) * P], q_sb[:, t, hh], ident)
                last.then_inc(at_qT, 1)
            pe.wait_ge(at_qTc, TILES)
            pe.wait_ge(at_kT, NEW)
            for t in range(2):
                for hh in range(HEADS):
                    last = nc.tensor.matmul(ps[:, hh // 2, (hh % 2) * SEQ:(hh % 2) * SEQ + (t + 1) * P],
                                            qT[:, t, hh], kTp[:, hh, 0:(t + 1) * P], start=True, stop=True)
                last.then_inc(at_sc, 1)
                pe.wait_ge(at_p2, t + 1)
                for c in range(t + 1):
                    if c or t:
                        pe.wait_ge(at_PTc, [0, 1][t] + c)
                    for hh in range(HEADS):
                        last = nc.tensor.transpose(ps[:, 4 + hh // 4, (hh % 4) * P:(hh % 4 + 1) * P],
                                                   p_sb[:, hh * SEQ + c * P:hh * SEQ + (c + 1) * P], ident)
                    last.then_inc(at_PTx, 1)
                pe.wait_ge(at_PTc, [1, 3][t])
                at_least(pe, at_o, 2 * t)
                for hp in range(HEADS // 2):
                    for c in range(t + 1):
                        last = nc.tensor.matmul(ps[:, 6 + hp // 2, (hp % 2) * 256:(hp % 2) * 256 + 256],
                                                vp[:, c, hp * P:(hp + 1) * P],
                                                pT[:, c * D + hp * 256:c * D + hp * 256 + 256], start=c == 0, stop=c == t)
                last.then_inc(at_pv, 1)
            pe.wait_ge(at_p1, 2)
            pe.wait_ge(pads_zeroed, 2)
            for hh in range(HEADS):
                for s in range(2):
                    last = nc.tensor.matmul(ps[:, 2 * s + hh // 4, (hh % 4) * P:(hh % 4 + 1) * P], wukT[:, hh, s * P:(s + 1) * P],
                                            qTs[:, :, hh * DECS:(hh + 1) * DECS], start=True, stop=True)
            last.then_inc(qa_done, 1)
            pe.wait_ge(qa_copied, 2)
            pe.wait_ge(at_o, 4)

            def sample_scores(b, par):
                if b >= 2:
                    pe.wait_ge(sm_max, b - 1)
                for cols, keys in ((slice(0, KC), cTs[:, b]), (slice(KC, KALL), cTn)):
                    for s in range(2):
                        nc.tensor.matmul(ps[:, par, cols], qa[:, s, b], keys[:, s], start=s == 0, stop=s == 1)
                nc.tensor.matmul(ps[:, 2 + par, 0:KC], qTs[:, b], krT[:, b],
                                 start=True, stop=True)
                nc.tensor.matmul(ps[:, 2 + par, KC:KALL], qTs[:, b], krT[:, DECB, 0:P], start=True, stop=True).then_inc(sm_s, 1)

            sample_scores(0, 0)

            def step(b, par):
                if b < DECB - 1:
                    sample_scores(b + 1, 1 - par)
                pe.wait_ge(sm_p, b + 1)
                for c in range(3):
                    last = nc.tensor.transpose(ps[:, 4 + par, c * P:(c + 1) * P], s_sb[:, par, c * P:(c + 1) * P], ident)
                last.then_inc(sm_pT, 1)
                if b >= 2:
                    pe.wait_ge(sm_pcc, b - 1)
                pe.wait_ge(sm_pTc, b + 1)
                for s in range(2):
                    for c in range(3):
                        rows_ = c_sb[:, SAMPLE] if c == 2 else cst[:, 2 * b + c]
                        last = nc.tensor.matmul(ps[:, 6 + par, s * P:(s + 1) * P], rows_[:, s * P:(s + 1) * P],
                                                psT[:, par, c * P:(c + 1) * P], start=c == 0, stop=c == 2)
                last.then_inc(sm_pc, 1)

            for b in range(DECB):
                step(b, b % 2)
            pe.wait_ge(sm_pcc, DECB)
            for hh in range(HEADS):
                for s in range(2):
                    last = nc.tensor.matmul(ps[:, hh // 4, (hh % 4) * P:(hh % 4 + 1) * P],
                                            w_uv[:, s, (hh // 2) * P:(hh // 2 + 1) * P],
                                            pcT[:, s, hh].rearrange("p b q -> p (b q)"), start=s == 0, stop=s == 1)
            last.then_inc(sm_o, 1)
            pe.wait_ge(ld_wo, 16)
            pe.wait_ge(at_o, 6)
            for t in range(TILES):
                for c in range(2):
                    for k in range(4):
                        last = nc.tensor.matmul(ps[:, 2 * t + c], oT[:, k, t * P:(t + 1) * P],
                                                w_o[:, k, c * 512:c * 512 + 512], start=k == 0, stop=k == 3)
            last.then_inc(at_y, 1)

        def expand(pe, ns, pars, src):
            def turn(i):
                at_least(pe, at_cTc, ns[i])
                for k in range(2):
                    last = nc.tensor.transpose(ps[:, 0, k * P:(k + 1) * P], src[i][:, k * P:(k + 1) * P], ident)
                last.then_inc(at_T, 1)

            def turn_keys(i):
                n = ns[i]
                pe.wait_ge(at_kcat, 2 * n + 2)
                at_least(pe, at_kT, n)
                for hh in range(HEADS):
                    last = nc.tensor.transpose(ps[0:QK, 4 + hh // 4, (hh % 4) * P:(hh % 4 + 1) * P],
                                               kcat[:, pars[i], hh], ident)
                last.then_inc(at_KT, 1)

            turn(0)
            for i, n in enumerate(ns):
                if i + 1 < len(ns):
                    turn(i + 1)
                pe.wait_ge(at_cTc, n + 1)
                at_least(pe, at_v, n)
                if not (isinstance(n, int) and n < 2):
                    pe.wait_ge(at_kcat, 2 * n - 2)
                for k in range(2):
                    nc.tensor.matmul(ps[:, 1 + pars[i]], cT[:, pars[i], k], w_uk[:, k], start=k == 0, stop=k == 1)
                for k in range(2):
                    last = nc.tensor.matmul(ps[:, 3], cT[:, pars[i], k], w_uv[:, k], start=k == 0, stop=k == 1)
                last.then_inc(at_kv, 1)
                if i:
                    turn_keys(i - 1)
            turn_keys(len(ns) - 1)

        out_stored = sem("out_stored")
        block = top.enter_context(nc.Block())

        @block.sync
        def _(sp):
            gm_sync(sp)
            moe_sync(sp, 0)
            at_sync(sp)
            moe_sync(sp, 1)
            for t in range(TILES):
                sp.wait_ge(combined, TILES + t + 1)
                out = O[0][0, t * P:(t + 1) * P, :] if t < SAMPLE else O[1].rearrange("b s d -> (b s) d")
                sp.dma_start(out, h[:, t]).then_inc(out_stored, 16)
            sp.wait_ge(out_stored, 16 * TILES)
            sp.wait_ge(v_stored, 16)
            sp.wait_ge(lat_stored, 96)

        @block.gpsimd
        def _(g):
            gm_pool(g)
            moe_pool(g, 0)
            at_pool(g)
            moe_pool(g, 1)

        @block.scalar
        def _(a):
            gm_scalar(a)
            route_scalar(a, 0)
            moe_scalar(a, 0)
            at_scalar(a)
            route_scalar(a, 1)
            moe_scalar(a, 1)

        @block.vector
        def _(v):
            gm_vector(v)
            route_vector(v, 0)
            moe_vector(v, 0)
            at_vector(v)
            route_vector(v, 1)
            moe_vector(v, 1)

        @block.tensor
        def _(pe):
            gm_tensor(pe)
            route_tensor(pe, 0)
            moe_tensor(pe, 0)
            at_tensor(pe)
            route_tensor(pe, 1)
            moe_tensor(pe, 1)


_INS = ['x_prompt', 'x_sample', 'cache_ckv', 'cache_krope', 'norm_mix', 'norm_ffn', 'gm_w_in', 'gm_b_in', 'gm_ln_g',
        'gm_ln_b', 'gm_w_s', 'gm_b_s', 'gm_w_out', 'gm_b_out', 'kv_norm', 'w_dkv', 'kv_a_norm', 'k_rope_norm', 'w_uk',
        'w_uv', 'k_nope_norm', 'w_dq', 'q_a_norm', 'w_uq', 'q_nope_norm', 'q_rope_norm', 'w_o', 'moe_w_group',
        'moe_b_group', 'moe_w_expert', 'moe_b_expert', 'moe_w1', 'moe_w3', 'moe_w2']
_OUTS = [((1, SEQ, D), 'float32'), ((DECB, DECS, D), 'float32'), ((1, SEQ, KVR), 'float32'),
         ((1, SEQ, ROPE), 'float32'), ((DECB, DECS, KVR), 'float32'), ((DECB, DECS, ROPE), 'float32'),
         ((1, DECB, DECS, DG), 'float32')]


def kernel(**inputs):
    import numpy as _np
    import concourse.bacc as _bacc
    from concourse import mybir as _mybir
    from concourse.bass_utils import run_bass_kernel_spmd as _run

    nc = _bacc.Bacc("TRN2", target_bir_lowering=False, num_devices=1)
    arrays, ins, outs = {}, {}, []
    for name in _INS:
        a = _np.ascontiguousarray(inputs[name])
        arrays[f"in_{name}_dram"] = a
        ins[name] = nc.dram_tensor(f"in_{name}_dram", a.shape, _mybir.dt.from_np(a.dtype), kind="ExternalInput").ap()
    arrays["in_const_dram"] = constants()
    ins["const"] = nc.dram_tensor("in_const_dram", (P, CONST_W), _mybir.dt.float32, kind="ExternalInput").ap()
    for i, (shape, dtype) in enumerate(_OUTS):
        dt = _mybir.dt.from_np(_np.dtype(dtype))
        outs.append(nc.dram_tensor(f"out_{i}_dram", shape, dt, kind="ExternalOutput").ap())
    build(nc, ins, outs)
    r = _run(nc, [arrays], core_ids=[0])
    return tuple(r.results[0][f"out_{i}_dram"] for i in range(len(_OUTS)))
```

```python
from contextlib import ExitStack

import numpy as np

import concourse.bass as bass
from concourse import mybir

ALU = mybir.AluOpType
ACT = mybir.ActivationFunctionType
AX = mybir.AxisListType
F32 = mybir.dt.float32
F32R = mybir.dt.float32r
I32 = mybir.dt.int32
U32 = mybir.dt.uint32

P = 128
TILES = 3
SAMPLE = 2
TOK = TILES * P
D = 1024
KD = D // P
DG = 2048
NSG = 8
SGW = DG // NSG
KG = DG // P
SEQ, DECB, DECS, PAST = 256, 8, 16, 256
CHUNK = 64
HEADS, NOPE, ROPE, VD = 8, 64, 32, 64
QK = NOPE + ROPE
QR, KVR = 384, 256
SCALE = QK ** -0.5
NG, EPG = 4, 4
NE = NG * EPG
DE = 512
KE = DE // P
EPS = 1e-6
BIG = 1e30
NEG = -1e30
SLOTS = 2 * TOK
CAP = 72
EXTRA = SLOTS // (CAP + 1)
ROWS = SLOTS + CAP
WCOL = 4096
N_IN, N_OUT = 8, 4
M_MOE = [N_IN + N_OUT, N_IN + N_OUT + 3 * NE]

C_ID, C_UP, C_ONE = 0, 128, 256
C_COS, C_SIN = 384, 384 + TILES * 16
C_MASK = C_SIN + TILES * 16
C_RANKW = C_MASK + 128
C_IOTA = C_RANKW + 16
C_HEADS = C_IOTA + 16
C_OWN = C_HEADS + 224
C_EPS = C_OWN + 240
CONST_W = C_EPS + 1


def constants():
    c = np.zeros((P, CONST_W), np.float32)
    c[:, C_ID:C_ID + P] = np.eye(P)
    c[:, C_UP:C_UP + P] = np.triu(np.ones((P, P)), 1)
    c[:, C_ONE:C_ONE + P] = 1.0
    half = ROPE // 2
    inv = (np.float32(10000.0) ** (-np.arange(half, dtype=np.float32) / np.float32(half))).astype(np.float32)
    for t in range(TILES):
        pos = np.arange(P) + t * P if t < SAMPLE else PAST + np.arange(P) % DECS
        ang = pos.astype(np.float32)[:, None] * inv[None]
        c[:, C_COS + 16 * t:C_COS + 16 * t + 16] = np.cos(ang)
        c[:, C_SIN + 16 * t:C_SIN + 16 * t + 16] = np.sin(ang)
    c[:CHUNK, C_MASK + CHUNK:C_MASK + P] = NEG
    c[:, C_RANKW:C_RANKW + 16] = 32 - np.arange(16)
    c[:, C_IOTA:C_IOTA + 16] = np.arange(16)
    for x in range(2):
        c[NOPE * x:NOPE * (x + 1), C_HEADS + 96 + DECS * x:C_HEADS + 96 + DECS * (x + 1)] = 1.0
    c[:, C_OWN:C_EPS] = NEG
    c[:, C_EPS] = EPS
    c[:, C_OWN + P - DECS:C_OWN + P] = 0.0
    return c


def build(nc, A, O):
    top = ExitStack()
    with top:
        def sem(name):
            return top.enter_context(nc.semaphore(name))

        def sb(name, shape, dt=F32, scope=top):
            return scope.enter_context(nc.sbuf_tensor(name, shape, dt))

        xrows = nc.dram_tensor("moe_xrows", (ROWS, D), F32, kind="Internal").ap()
        yrows = nc.dram_tensor("moe_yrows", (ROWS, D), F32, kind="Internal").ap()

        h = sb("h", [P, TILES, D])
        const = sb("const", [P, CONST_W])
        ident, upper, ones = const[:, C_ID:C_ID + P], const[:, C_UP:C_UP + P], const[:, C_ONE:C_ONE + P]
        raw = sb("raw", [P, 3, WCOL])
        gain = sb("gain", [P, D])
        stat = sb("stat", [P, 2, 4])
        wroute = sb("wroute", [P, 2, KD, NG + NE])
        broute = sb("broute", [P, 2, NG + NE])
        ps = top.enter_context(nc.psum_tensor("ps", [P, 8, 512], F32))

        raw_loaded = [sem(f"raw_loaded{i}") for i in range(3)]
        wh_ready, wl_ready, w_used = sem("wh_ready"), sem("wl_ready"), sem("w_used")
        dve_step, act_step = sem("dve_step"), sem("act_step")
        steps = {"dve": 0, "act": 0}

        def dve_link(v, ins):
            steps["dve"] += 1
            ins.then_inc(dve_step, 1)
            v.wait_ge(dve_step, steps["dve"])

        def act_link(a, ins):
            steps["act"] += 1
            ins.then_inc(act_step, 1)
            a.wait_ge(act_step, steps["act"])

        ms_ready, rms_ready = sem("ms_ready"), sem("rms_ready")
        roots = {"ms_a": 0, "rms": 0}

        def rms_inverse(v, ms, out, scale):
            steps["dve"] += 1
            nc.vector.tensor_scalar(out, ms, scale, EPS, ALU.mult, ALU.add).then_inc(ms_ready, 1)
            roots["rms"] += 1
            v.wait_ge(rms_ready, roots["rms"])
            nc.vector.reciprocal(out, out).then_inc(dve_step, 1)
            v.wait_ge(dve_step, steps["dve"])

        def root(a, x):
            roots["ms_a"] += 1
            a.wait_ge(ms_ready, roots["ms_a"])
            nc.scalar.activation(x, x, ACT.Sqrt).then_inc(rms_ready, 1)

        def inverse_rms(v, junk):
            for t in range(TILES):
                dve_link(v, nc.vector.tensor_tensor_reduce(junk, h[:, t], h[:, t], 1.0, 0.0, ALU.mult,
                                                           ALU.add, stat[:, 0, t:t + 1]))
            rms_inverse(v, stat[:, 0, 0:TILES], stat[:, 1, 0:TILES], 1.0 / D)

        def row_roots(a, junk):
            for t in range(TILES):
                act_link(a, nc.scalar.activation(junk, h[:, t], ACT.Square, accum_out=stat[:, 0, t:t + 1]))
            nc.scalar.activation(stat[:, 1, 0:TILES], stat[:, 0, 0:TILES], ACT.Sqrt, bias=const[:, C_EPS:C_EPS + 1],
                                 scale=1.0 / D).then_inc(rms_ready, 1)

        def inverse_of_roots(v):
            roots["rms"] += 1
            v.wait_ge(rms_ready, roots["rms"])
            dve_link(v, nc.vector.reciprocal(stat[:, 1, 0:TILES], stat[:, 1, 0:TILES]))

        def norm_rows(t, out):
            return nc.vector.scalar_tensor_tensor(out, h[:, t], stat[:, 1, t:t + 1], gain[:], ALU.mult, ALU.mult)

        def split_product(pe, m, outs, xh, xl, wh, wl, nk, halves, start=True, stop=True):
            pe.wait_ge(wh_ready, m + 1)
            for t, out in enumerate(outs):
                for k in range(nk):
                    for x in (xh, xl):
                        for c in range(halves):
                            nc.tensor.matmul(out[c], x(t, k), wh[:, k, c * 512:c * 512 + 512],
                                             start=start and k == 0 and x is xh, stop=False)
            pe.wait_ge(wl_ready, m + 1)
            for t, out in enumerate(outs):
                for k in range(nk):
                    for c in range(halves):
                        last = nc.tensor.matmul(out[c], xh(t, k), wl[:, k, c * 512:c * 512 + 512],
                                                start=False, stop=stop and k == nk - 1)
            return last

        gm = ExitStack()
        split_gm = [[sb(f"gm_w{p}{i}", [P, WCOL], F32R, gm) for p in "hl"] for i in range(2)]
        fx = sb("gm_fx", [P, 2 * KD * TOK], F32R, gm)
        xth = fx[:, 0:KD * TOK].rearrange("p (k t) -> p k t", k=KD)
        xtl = fx[:, KD * TOK:].rearrange("p (k t) -> p k t", k=KD)
        utl = fx[:, :].rearrange("p (k t) -> p k t", k=KG)
        u = sb("gm_u", [P, TILES, DG], F32, gm)
        gm_v = ExitStack()
        vv = sb("gm_v", [P, TILES, DG], F32, gm_v)
        gm_v.close()
        uth = sb("gm_uth", [P, KG, TOK], F32R, gm)
        gmst = sb("gm_stat", [P, 20], F32, gm)
        bs = sb("gm_bs", [P, 2, NSG], F32, gm)
        gm.close()
        wst = raw[:, 2, 0:2 * NSG * P].rearrange("p (a g i) -> p a g i", a=2, g=NSG)
        bin_c = raw[:, 2, 2048:3072].rearrange("p (a n) -> p a n", a=2)
        ln_c = u[:, 0:2]
        xn = [u[:, 0, 0:D], u[:, 0, D:2 * D], u[:, 2, D:2 * D]]
        ws_raw = u[:, 1, 0:2 * NSG * P].rearrange("p (a g j) -> p a g j", a=2, g=NSG)

        ld_h2 = sem("ld_h2")
        ld_h, ld_const, ld_gain, ld_ws, ld_ws16, ld_bs, ld_route = map(
            sem, ["ld_h", "ld_const", "ld_gain", "ld_ws", "ld_ws16", "ld_bs", "ld_route"])
        ld_bin = [sem("ld_bin0"), sem("ld_bin1")]
        ld_ln, ld_bout = sem("ld_ln"), sem("ld_bout")
        ws_zeroed = sem("ws_zeroed")
        gm_xn, gm_xT, gm_xh, gm_xl = map(sem, ["gm_xn", "gm_xT", "gm_xh", "gm_xl"])
        gm_wsT, gm_wst = sem("gm_wsT"), sem("gm_wst")
        z_read, z_gelu = sem("z_read"), sem("z_gelu")
        v_mean, v_square, v_ready, h_mixed = map(sem, ["v_mean", "v_square", "v_ready", "h_mixed"])
        s_done, us_ready = sem("s_done"), sem("us_ready")
        uT_done, uth_ready, utl_ready = sem("uT_done"), sem("uth_ready"), sem("utl_ready")
        v_stored = sem("v_stored")

        IN_ORDER = [4, 5, 6, 7, 0, 1, 2, 3]

        def gm_dest(c):
            return (u, c * 512) if c < 4 else (vv, (c - 4) * 512)

        def in_weights(m):
            return A["gm_w_in"][0, :, IN_ORDER[m] * 512:IN_ORDER[m] * 512 + 512].rearrange("(k p) n -> p k n", p=P)

        def out_weights(j):
            return A["gm_w_out"][0, j * 512:(j + 1) * 512, :].rearrange("(k p) n -> p k n", p=P)

        def raw_in(s):
            return raw[:, s, :].rearrange("p (k n) -> p k n", k=KD)

        def raw_out(s):
            return raw[:, s, :].rearrange("p (k n) -> p k n", k=KE)

        def gm_sync(sp):
            sp.dma_start(h[:, 0:2, :], A["x_prompt"][0].rearrange("(t p) d -> p t d", p=P)).then_inc(ld_h, 16)
            sp.dma_start(const[:], A["const"]).then_inc(ld_const, 16)
            sp.dma_start(h[:, 2, :], A["x_sample"].rearrange("b s d -> (b s) d")).then_inc(ld_h2, 16)
            sp.wait_ge(ld_h, 16)
            for m in range(N_IN + N_OUT):
                if m >= 2:
                    sp.wait_ge(wl_ready, m - 1)
                src = in_weights(m) if m < N_IN else out_weights(m - N_IN)
                dst = raw_in(m % 2) if m < N_IN else raw_out(m % 2)
                sp.dma_start(dst, src).then_inc(raw_loaded[m % 2], 16)

        def gm_pool(g):
            g.dma_start(gain[:], A["norm_mix"][0:1, :].partition_broadcast(P)).then_inc(ld_gain, 16)
            g.dma_start(ws_raw[:, 0], A["gm_w_s"][0].rearrange("g i j -> i g j")).then_inc(ld_ws, 16)
            g.wait_ge(ws_zeroed, 1)
            for b in range(DECB):
                g.dma_start(ws_raw[b * DECS:(b + 1) * DECS, 1, :, b * DECS:(b + 1) * DECS],
                            A["gm_w_s"][0, :, 0:DECS, 0:DECS].rearrange("g i j -> i g j")).then_inc(ld_ws16, 16)
            g.dma_start(bs[:, 0], A["gm_b_s"][0].rearrange("g i -> i g"),
                        allow_slow_non_contiguous=True).then_inc(ld_bs, 16)
            for b in range(DECB):
                g.dma_start(bs[b * DECS:(b + 1) * DECS, 1],
                            A["gm_b_s"][0, :, 0:DECS].rearrange("g i -> i g"),
                            allow_slow_non_contiguous=True).then_inc(ld_bs, 16)
            for l in range(2):
                g.dma_start(wroute[:, l, :, 0:NG], A["moe_w_group"][l].rearrange("(k p) n -> p k n", p=P)).then_inc(ld_route, 16)
                g.dma_start(wroute[:, l, :, NG:], A["moe_w_expert"][l].rearrange("(k p) n -> p k n", p=P)).then_inc(ld_route, 16)
                g.dma_start(broute[:, l, 0:NG], A["moe_b_group"][l:l + 1, :].partition_broadcast(P)).then_inc(ld_route, 16)
                g.dma_start(broute[:, l, NG:], A["moe_b_expert"][l:l + 1, :].partition_broadcast(P)).then_inc(ld_route, 16)
            for m in range(N_IN):
                if m == 2:
                    g.wait_ge(gm_xT, TILES)
                    g.wait_ge(gm_wsT, 2)
                    for i, name in enumerate(("gm_ln_g", "gm_ln_b")):
                        g.dma_start(ln_c[:, i], A[name].partition_broadcast(P)).then_inc(ld_ln, 16)
                if m >= 2:
                    g.wait_ge(z_read, TILES * (m - 1))
                c = IN_ORDER[m]
                g.dma_start(bin_c[:, m % 2], A["gm_b_in"][0:1, c * 512:c * 512 + 512].partition_broadcast(P)
                            ).then_inc(ld_bin[m % 2], 16)
            g.wait_ge(v_ready, TILES)
            g.dma_start(O[6].rearrange("n b s d -> (n b s) d"), vv[:, SAMPLE, :]).then_inc(v_stored, 16)
            g.dma_start(gain[:], A["gm_b_out"][0:1, :].partition_broadcast(P)).then_inc(ld_bout, 16)

        def split_h(a, m, src_slot, wh, raw_count, free):
            a.wait_ge(raw_loaded[src_slot], 16 * raw_count)
            if free is not None:
                a.wait_ge(w_used, free)
            nc.scalar.activation(wh[:], raw[:, src_slot, :], ACT.Copy).then_inc(wh_ready, 1)

        def split_l(v, m, src_slot, wh, wl):
            v.wait_ge(wh_ready, m + 1)
            nc.vector.tensor_tensor(wl[:], raw[:, src_slot, :], wh[:].bitcast(F32), ALU.subtract).then_inc(wl_ready, 1)

        def gm_split_h(a, m):
            split_h(a, m, m % 2, split_gm[m % 2][0], m // 2 + 1, m - 1 if m >= 2 else None)

        def gm_split_l(v, m):
            split_l(v, m, m % 2, *split_gm[m % 2])

        def gm_vector(v):
            nc.vector.memset(ws_raw[:, 1], 0.0).then_inc(ws_zeroed, 1)
            v.wait_ge(ld_h, 16)
            v.wait_ge(ld_gain, 16)
            for t in range(TILES):
                if t == SAMPLE:
                    v.wait_ge(ld_h2, 16)
                nc.vector.tensor_tensor(xn[t], h[:, t], gain[:], ALU.mult).then_inc(gm_xn, 1)
            for t in range(TILES):
                gm_xl_part(v, t)
            gm_split_l(v, 0)
            for a in range(2):
                v.wait_ge(gm_wsT, a + 1)
                dve_link(v, nc.vector.tensor_copy(wst[:, a], ps[:, 6 - 3 * a:8 - 3 * a].rearrange("p b (g i) -> p (b g) i", i=P)))
            nc.vector.memset(wst[CHUNK:P, 0, :, 0:CHUNK], 0.0).then_inc(gm_wst, 1)
            gm_split_l(v, 1)
            inverse_of_roots(v)
            for m in range(N_IN):
                c = IN_ORDER[m]
                dst, col = gm_dest(c)
                if m == 4:
                    gm_layer_norm(v)
                for t in range(TILES):
                    if t == 0:
                        v.wait_ge(ld_bin[m % 2], 16 * (m // 2 + 1))
                        v.wait_ge(w_used, m + 1)
                    nc.vector.scalar_tensor_tensor(dst[:, t, col:col + 512], ps[:, 3 * (m % 2) + t], stat[:, 1, t:t + 1],
                                                   bin_c[:, m % 2], ALU.mult, ALU.add).then_inc(z_read, 1)
                gm_split_l(v, m + 2)
            for t in range(TILES):
                for gp in range(NSG // 2):
                    n = t * 4 + gp
                    v.wait_ge(s_done, n + 1)
                    if n == 0:
                        v.wait_ge(z_gelu, TILES * N_IN)
                        v.wait_ge(ld_bs, 16 * (1 + DECB))
                    for i in range(2):
                        g = 2 * gp + i
                        uu = u[:, t, g * SGW:(g + 1) * SGW]
                        nc.vector.scalar_tensor_tensor(uu, ps[:, n % 6, i * SGW:(i + 1) * SGW],
                                                       bs[:, 1 if t == SAMPLE else 0, g:g + 1], uu,
                                                       ALU.add, ALU.mult).then_inc(us_ready, 1)
            for n in range(TILES * 4):
                t, q = divmod(n, 4)
                v.wait_ge(uth_ready, n + 1)
                nc.vector.tensor_tensor(utl[:, 4 * q:4 * q + 4, t * P:(t + 1) * P],
                                        ps[:, 6 + n % 2].rearrange("p (k t) -> p k t", k=4),
                                        uth[:, 4 * q:4 * q + 4, t * P:(t + 1) * P].bitcast(F32),
                                        ALU.subtract).then_inc(utl_ready, 1)
            v.wait_ge(ld_bout, 16)
            for t in range(TILES):
                dve_link(v, nc.vector.tensor_tensor(h[:, t], h[:, t], gain[:], ALU.add))
            for m in range(N_IN + 2, N_IN + N_OUT):
                gm_split_l(v, m)
            moe_split_l(v, 0, 0, 0)
            v.wait_ge(w_used, N_IN + N_OUT)
            for t in range(TILES):
                nc.vector.tensor_tensor(h[:, t].rearrange("p (c n) -> p c n", c=2), h[:, t].rearrange("p (c n) -> p c n", c=2),
                                        ps[:, 2 * t:2 * t + 2], ALU.add).then_inc(h_mixed, 1)
                weigh_rows(v, 0, t)

        def gm_xl_part(v, t):
            v.wait_ge(gm_xh, t + 1)
            nc.vector.tensor_tensor(xtl[:, :, t * P:(t + 1) * P], ps[:, 2 * t:2 * t + 2].rearrange("p b (k t) -> p (b k) t", t=P),
                                    xth[:, :, t * P:(t + 1) * P].bitcast(F32), ALU.subtract).then_inc(gm_xl, 1)

        def gm_layer_norm(v):
            v.wait_ge(z_gelu, TILES * 4)
            mean, inv = gmst[:, 12:15], gmst[:, 15:18]
            dve_link(v, nc.vector.tensor_reduce(mean, gmst[:, 0:12].rearrange("p (t c) -> p t c", t=TILES), AX.X, ALU.add))
            nc.vector.tensor_scalar(mean, mean, -1.0 / DG, None, ALU.mult).then_inc(v_mean, 1)
            v.wait_ge(v_mean, 1)
            v.wait_ge(ld_ln, 32)
            for t in range(TILES):
                v.wait_ge(v_square, t + 1)
                dve_link(v, nc.vector.scalar_tensor_tensor(vv[:, t], vv[:, t], mean[:, t:t + 1], ln_c[:, 0], ALU.add, ALU.mult))
            roots["rms"] += 1
            v.wait_ge(rms_ready, roots["rms"])
            dve_link(v, nc.vector.reciprocal(inv, inv))
            for t in range(TILES):
                nc.vector.scalar_tensor_tensor(vv[:, t], vv[:, t], inv[:, t:t + 1], ln_c[:, 1], ALU.mult, ALU.add
                                               ).then_inc(v_ready, 1)
            v.wait_ge(v_ready, TILES)

        def gm_scalar(a):
            for t in range(TILES):
                gm_xh_part(a, t)
            gm_split_h(a, 0)
            gm_split_h(a, 1)
            a.wait_ge(ld_h, 16)
            a.wait_ge(ld_h2, 16)
            a.wait_ge(ld_const, 16)
            row_roots(a, u[:, 2, 0:D])
            for m in range(N_IN):
                c = IN_ORDER[m]
                dst, col = gm_dest(c)
                if m == 4:
                    a.wait_ge(v_mean, 1)
                    for t in range(TILES):
                        nc.scalar.activation(u[:, 2], vv[:, t], ACT.Square, bias=gmst[:, 12 + t:13 + t],
                                             accum_out=gmst[:, 15 + t:16 + t]).then_inc(v_square, 1)
                        a.wait_ge(v_square, t + 1)
                    nc.scalar.activation(gmst[:, 15:18], gmst[:, 15:18], ACT.Sqrt, bias=const[:, C_EPS:C_EPS + 1],
                                         scale=1.0 / DG).then_inc(rms_ready, 1)
                for t in range(TILES):
                    a.wait_ge(z_read, m * TILES + t + 1)
                    z = dst[:, t, col:col + 512]
                    kw = {"accum_out": gmst[:, 4 * t + c - 4:4 * t + c - 3]} if c >= 4 else {}
                    nc.scalar.activation(z, z, ACT.Gelu_apprx_tanh, **kw).then_inc(z_gelu, 1)
                gm_split_h(a, m + 2)
            for n in range(TILES * 4):
                t, q = divmod(n, 4)
                a.wait_ge(uT_done, n + 1)
                if n == 0:
                    a.wait_ge(v_stored, 16)
                nc.scalar.activation(uth[:, 4 * q:4 * q + 4, t * P:(t + 1) * P],
                                     ps[:, 6 + n % 2].rearrange("p (k t) -> p k t", k=4), ACT.Copy).then_inc(uth_ready, 1)
            for m in range(N_IN + 2, N_IN + N_OUT):
                gm_split_h(a, m)
            moe_split_h(a, 0, 0, 0, 0)

        def gm_xh_part(a, t):
            a.wait_ge(gm_xT, t + 1)
            nc.scalar.activation(xth[:, :, t * P:(t + 1) * P], ps[:, 2 * t:2 * t + 2].rearrange("p b (k t) -> p (b k) t", t=P),
                                 ACT.Copy).then_inc(gm_xh, 1)

        def gm_tensor(pe):
            pe.wait_ge(ld_const, 16)
            for t in range(TILES):
                pe.wait_ge(gm_xn, t + 1)
                for k in range(KD):
                    last = nc.tensor.transpose(ps[:, 2 * t + k // 4, (k % 4) * P:(k % 4 + 1) * P],
                                               xn[t][:, k * P:(k + 1) * P], ident)
                last.then_inc(gm_xT, 1)
            for a, s, n in ((0, ld_ws, 16), (1, ld_ws16, 16 * DECB)):
                pe.wait_ge(s, n)
                if a:
                    pe.wait_ge(gm_xl, TILES)
                for g in range(NSG):
                    last = nc.tensor.transpose(ps[:, 6 - 3 * a + g // 4, (g % 4) * P:(g % 4 + 1) * P], ws_raw[:, a, g], ident)
                last.then_inc(gm_wsT, 1)
            pe.wait_ge(gm_xl, TILES)
            for m in range(N_IN):
                if m == 1:
                    pe.wait_ge(gm_wst, 1)
                if m >= 2:
                    pe.wait_ge(z_read, TILES * (m - 1))
                wh, wl = [w[:].rearrange("p (k n) -> p k n", k=KD) for w in split_gm[m % 2]]
                last = split_product(pe, m, [[ps[:, 3 * (m % 2) + t]] for t in range(TILES)],
                                     lambda t, k: xth[:, k, t * P:(t + 1) * P], lambda t, k: xtl[:, k, t * P:(t + 1) * P],
                                     wh, wl, KD, 1)
                last.then_inc(w_used, 1)
            pe.wait_ge(v_ready, TILES)
            pe.wait_ge(z_read, TILES * N_IN)
            for t in range(TILES):
                for gp in range(NSG // 2):
                    n = t * 4 + gp
                    if n >= 6:
                        pe.wait_ge(us_ready, 2 * (n - 5))
                    for i in range(2):
                        g = 2 * gp + i
                        last = nc.tensor.matmul(ps[:, n % 6, i * SGW:(i + 1) * SGW], wst[:, 1 if t == SAMPLE else 0, g],
                                                vv[:, t, g * SGW:(g + 1) * SGW], start=True, stop=True)
                    last.then_inc(s_done, 1)
            for n in range(TILES * 4):
                t, q = divmod(n, 4)
                pe.wait_ge(us_ready, 8 * (t + 1))
                if n >= 2:
                    pe.wait_ge(utl_ready, n - 1)
                for j in range(4):
                    k = 4 * q + j
                    last = nc.tensor.transpose(ps[:, 6 + n % 2, j * P:(j + 1) * P], u[:, t, k * P:(k + 1) * P], ident)
                last.then_inc(uT_done, 1)
            pe.wait_ge(utl_ready, TILES * 4)
            for j in range(N_OUT):
                m = N_IN + j
                wh, wl = [w[:].rearrange("p (k n) -> p k n", k=KE) for w in split_gm[m % 2]]
                last = split_product(pe, m, [[ps[:, 2 * t], ps[:, 2 * t + 1]] for t in range(TILES)],
                                     lambda t, k: uth[:, 4 * j + k, t * P:(t + 1) * P],
                                     lambda t, k: utl[:, 4 * j + k, t * P:(t + 1) * P],
                                     wh, wl, KE, 2, start=j == 0, stop=j == N_OUT - 1)
                last.then_inc(w_used, 1)

        moe = ExitStack()
        split_moe = [[sb(f"moe_w{p}{i}", [P, WCOL], F32R, moe) for p in "hl"] for i in range(2)]
        split_moe.append([sb("moe_wh2", [P, WCOL], F32R, moe)])
        with ExitStack() as before:
            spare = sb("moe_spare", [P, 2, D], F32, before)
        split_moe[2].append(sb("moe_wl2", [P, WCOL], F32R, moe))
        rows = sb("moe_rows", [P, 4, D], F32, moe)
        xsplit = [[sb(f"moe_x{p}{i}", [P, KD, CAP], F32R, moe) for p in "hl"] for i in range(2)]
        sil = sb("moe_silu", [CAP, DE], F32, moe)
        hid = sb("moe_hidden", [CAP, DE], F32, moe)
        hth, htl = sb("moe_hTh", [P, KE, CAP], F32R, moe), sb("moe_hTl", [P, KE, CAP], F32R, moe)
        NT = NG + NE
        logit = sb("rt_logit", [P, TILES, NT], F32, moe)
        gsel = sb("rt_group", [P, TILES, NG], F32, moe)
        pen = sb("rt_penalty", [P, TILES, NG], F32, moe)
        lem = sb("rt_in_group", [P, TILES, NE], F32, moe)
        pick = [sb(f"rt_pick{i}", [P, TILES, NE], F32, moe) for i in range(2)]
        tmp = sb("rt_tmp", [P, TILES, NE], F32, moe)
        best = sb("rt_best", [P, 6, TILES], F32, moe)
        ex = sb("rt_exp", [P, TILES, NG + 1], F32, moe)
        wts = sb("rt_weight", [P, 2, TILES], F32, moe)
        picked = sb("rt_picked", [P, TILES, NE], F32, moe)
        rank = sb("rt_rank", [P, TILES + 1, NE], F32, moe)
        cat = sb("rt_counts", [P, 2 * NE], F32, moe)
        first = sb("rt_first", [P, 2 * NE], F32, moe)
        dst = sb("rt_dst", [P, TILES, 2], F32, moe)
        dst_i = sb("rt_dst_i", [P, TILES * 2], U32, moe)
        first_i = sb("rt_first_i", [P, NE], I32, moe)
        ov = sb("rt_over", [P, 4, NE], F32, moe)
        ovb = sb("rt_over_block", [P, EXTRA, NE], F32, moe)
        ovb2 = sb("rt_over_block2", [P, EXTRA, NE], F32, moe)
        ovt = sb("rt_over_table", [P, 2 * EXTRA + 1], F32, moe)
        ovt_i = sb("rt_over_table_i", [P, 2 * EXTRA + 1], I32, moe)
        moe.close()
        xT_rows, squares_junk = [rows[:, 3], spare[:, 0], rows[:, 3]], spare[:, 1]
        y_rows = [rows[:, i] for i in range(4)] + [spare[:, i] for i in range(2)]
        BX, BA, BB, BH, BY, BR = 0, 2, 3, 4, 5, 7

        ld_ffn, pad_written = sem("ld_ffn"), sem("pad_written")
        rt_xn, rt_xT, rt_xTc, rt_logits = sem("rt_xn"), sem("rt_xT"), sem("rt_xTc"), sem("rt_logits")
        rt_exp, rt_picked, rt_rank = sem("rt_expd"), sem("rt_pickd"), sem("rt_rankd")
        rt_dst, rt_table, scattered = sem("rt_dstd"), sem("rt_table"), sem("scattered")
        x_loaded = [sem("x_loaded0"), sem("x_loaded1")]
        xT_done, xh_ready, xl_ready = sem("xT_done"), sem("xh_ready"), sem("xl_ready")
        silu_done, hid_done = sem("silu_done"), sem("hid_done")
        hT_done, hh_ready, hl_ready = sem("hT_done"), sem("hh_ready"), sem("hl_ready")
        y_out, y_stored, y_final = sem("y_out"), sem("y_stored"), sem("y_final")
        y_back, combined = [sem(f"y_back{t}") for t in range(TILES)], sem("combined")
        over = [{k: sem(f"over{l}_{k}") for k in ("w", "x", "pe", "act", "hid", "st")} for l in range(2)]

        def at_least(eng, s, n):
            if not isinstance(n, int) or n > 0:
                eng.wait_ge(s, n)

        RAW_BASE = [N_IN // 2 + N_OUT // 2] * 2 + [0]

        def raw_count(l, s, q):
            return RAW_BASE[s] + NE * l + q + 1

        def w_in_expert(l, name, e):
            w = A[name][l, bass.ds(e, 1)]
            return w.rearrange("o (k p) n -> p (o k) n", p=P)

        def moe_w_view(w, nk):
            return w.rearrange("p (k n) -> p k n", k=nk)

        def moe_sync(sp, l):
            m0, E0 = M_MOE[l], NE * l

            def load(name, e, j, slot):
                if isinstance(j, int) and j < 3:
                    if l == 0:
                        sp.wait_ge(wl_ready, m0)
                    else:
                        sp.wait_ge(*[(at_proj, TILES), (sm_o, 1), (at_y, 1)][slot])
                else:
                    at_least(sp, wl_ready, m0 + j - 2)
                sp.dma_start(moe_w_view(raw[:, slot, :], KE if name == "moe_w2" else KD),
                             w_in_expert(l, name, e)).then_inc(raw_loaded[slot], 16)

            def load_x(e, par):
                row = sp.value_load(first_i[0:1, bass.ds(e, 1)], min_val=0, max_val=SLOTS)
                if not (isinstance(e, int) and e < 2):
                    at_least(sp, xT_done, E0 + e - 1)
                sp.dma_start(rows[0:CAP, par, :], xrows[bass.ds(row, CAP), :]).then_inc(x_loaded[par], 16)

            def store_y(e, par):
                row = sp.value_load(first_i[0:1, bass.ds(e, 1)], min_val=0, max_val=SLOTS)
                at_least(sp, y_stored, 16 * (E0 + e))
                if isinstance(e, int):
                    sp.wait_ge(y_out, E0 + e + 1)
                sp.dma_start(yrows[bass.ds(row, CAP), :], rows[0:CAP, 2 + par, :]).then_inc(y_stored, 16)

            load("moe_w1", 0, 0, 0)
            load("moe_w3", 0, 1, 1)
            load("moe_w1", 1, 2, 2)
            load("moe_w3", 1, 3, 0)
            load("moe_w2", 0, 4, 1)
            sp.wait_ge(scattered, 16 * 2 * TILES * (l + 1))
            sp.wait_ge(pad_written, 16)
            load_x(0, 0)
            load_x(1, 1)
            load("moe_w1", 2, 5, 2)

            def of_expert(e, par):
                if not (isinstance(e, int) and e == 2):
                    load("moe_w1", e, 3 * e - 1, 2)
                load_x(e, par)
                load("moe_w3", e, 3 * e, 0)
                if not (isinstance(e, int) and e < 4):
                    store_y(e - 4, par)
                load("moe_w2", e - 1, 3 * e + 1, 1)

            for e in range(2, 5):
                of_expert(e, e % 2)
            with sp.Fori(0, (NE - 6) // 2) as i:
                of_expert(2 * i + 5, 1)
                of_expert(2 * i + 6, 0)
            of_expert(NE - 1, 1)
            load("moe_w2", NE - 1, 3 * NE - 1, 2)
            for e in range(NE - 4, NE):
                store_y(e, e % 2)
            if l == 0:
                load_cache(sp)
            s = over[l]
            sp.wait_ge(y_stored, 16 * (E0 + NE))
            sp.wait_ge(wl_ready, m0 + 3 * NE)
            sp.wait_ge(rt_table, l + 1)
            n_over = sp.value_load(ovt_i[0:1, 2 * EXTRA:2 * EXTRA + 1], min_val=0, max_val=EXTRA)
            sp.sem_inc(s["st"], 16)
            with sp.Fori(0, EXTRA) as i:
                with sp.If(n_over > i):
                    e = sp.value_load(ovt_i[0:1, bass.ds(i, 1)], min_val=0, max_val=NE - 1)
                    row = sp.value_load(ovt_i[0:1, bass.ds(i + EXTRA, 1)], min_val=0, max_val=SLOTS)
                    at_least(sp, s["st"], 16 * i + 16)
                    sp.dma_start(rows[0:CAP, 0, :], xrows[bass.ds(row, CAP), :]).then_inc(s["x"], 16)
                    for slot, name in enumerate(("moe_w1", "moe_w3", "moe_w2")):
                        sp.dma_start(moe_w_view(raw[:, slot, :], KE if slot == 2 else KD),
                                     w_in_expert(l, name, e)).then_inc(s["w"], 16)
                    at_least(sp, s["act"], 4 * i + 4)
                    sp.dma_start(yrows[bass.ds(row, CAP), :], rows[0:CAP, 2, :]).then_inc(s["st"], 16)
            at_least(sp, s["st"], 16 * n_over + 16)
            sp.sem_inc(y_final, 1)

        def experts(eng, step):
            for e in range(3):
                step(e, e % 2)
            with eng.Fori(0, (NE - 4) // 2) as i:
                step(2 * i + 3, 1)
                step(2 * i + 4, 0)
            step(NE - 1, 1)

        def is_first(e):
            return isinstance(e, int) and e == 0

        def is_last(e):
            return isinstance(e, int) and e == NE - 1

        def moe_pool(g, l):
            if l == 0:
                g.dma_start(xrows[SLOTS:ROWS], A["x_prompt"][0, 0:CAP, :]).then_inc(pad_written, 16)
                g.wait_ge(wl_ready, N_IN + N_OUT - 1)
            g.dma_start(gain[:], A["norm_ffn"][l:l + 1, :].partition_broadcast(P)).then_inc(ld_ffn, 16)
            if l == 0:
                g.wait_ge(rt_xn, TILES)
                g.dma_start(gain[:], A["kv_norm"].rearrange("(a n) -> a n", a=1).partition_broadcast(P)).then_inc(ld_kvg, 16)
            g.wait_ge(rt_dst, l + 1)
            for t in range(TILES):
                for k in range(2):
                    g.indirect_dma_start(xrows[0:SLOTS], bass.IndirectOffsetOnAxis(ap=dst_i[:, 2 * t + k:2 * t + k + 1], axis=0),
                                         rows[:, t], None).then_inc(scattered, 16)
            g.wait_ge(y_final, l + 1)
            for t in range(TILES):
                for k in range(2):
                    g.indirect_dma_start(y_rows[2 * t + k], None, yrows[0:SLOTS],
                                         bass.IndirectOffsetOnAxis(ap=dst_i[:, 2 * t + k:2 * t + k + 1], axis=0)
                                         ).then_inc(y_back[t], 16)

        def first_max(v, x, n, out, value, key):
            shape = [P, TILES, n]
            t_ = tmp[:, :, 0:n]
            w = const[:, C_RANKW:C_RANKW + n].unsqueeze(1).to_broadcast(shape)
            dve_link(v, nc.vector.tensor_reduce(value, x, AX.X, ALU.max))
            dve_link(v, nc.vector.tensor_tensor(t_, x, value.unsqueeze(2).to_broadcast(shape), ALU.is_equal))
            dve_link(v, nc.vector.tensor_tensor(t_, t_, w, ALU.mult))
            dve_link(v, nc.vector.tensor_reduce(key, t_, AX.X, ALU.max))
            dve_link(v, nc.vector.tensor_tensor(out, t_, key.unsqueeze(2).to_broadcast(shape), ALU.is_equal))

        def weigh_rows(v, l, t):
            if t == 0:
                v.wait_ge(ld_ffn, 16 * (l + 1))
            v.wait_ge(h_mixed, TILES * l + t + 1)
            nc.vector.tensor_tensor(rows[:, t], h[:, t], gain[:], ALU.mult).then_inc(rt_xn, 1)

        def route_vector(v, l):
            if l == 0:
                moe_split_l(v, l, 1, 1)
            inverse_of_roots(v)
            for t in range(TILES):
                v.wait_ge(rt_xT, TILES * l + t + 1)
                dve_link(v, nc.vector.tensor_scalar(rows[:, t], rows[:, t], stat[:, 1, t:t + 1], None, ALU.mult))
            v.wait_ge(ld_route, 16 * 8)
            v.wait_ge(rt_logits, TILES * (l + 1))
            for t in range(TILES):
                dve_link(v, nc.vector.scalar_tensor_tensor(logit[:, t], ps[:, BR, 32 * t:32 * t + NT], stat[:, 1, t:t + 1],
                                                           broute[:, l, :], ALU.mult, ALU.add))
            lg, le = logit[:, :, 0:NG], logit[:, :, NG:NT]
            first_max(v, lg, NG, gsel[:], best[:, 0], best[:, 1])
            dve_link(v, nc.vector.tensor_tensor(ex[:, :, 0:NG], lg, best[:, 0].unsqueeze(2).to_broadcast([P, TILES, NG]),
                                                ALU.subtract))
            dve_link(v, nc.vector.tensor_scalar(pen[:], gsel[:], BIG, -BIG, ALU.mult, ALU.add))
            shape4 = [P, TILES, NG, EPG]
            lem4 = lem[:].rearrange("p t (g j) -> p t g j", g=NG)
            dve_link(v, nc.vector.tensor_tensor(lem4, le.rearrange("p t (g j) -> p t g j", g=NG),
                                                gsel[:].unsqueeze(3).to_broadcast(shape4), ALU.mult))
            dve_link(v, nc.vector.tensor_tensor(lem4, lem4, pen[:].unsqueeze(3).to_broadcast(shape4), ALU.add))
            first_max(v, lem[:], NE, pick[0][:], best[:, 2], best[:, 3])
            dve_link(v, nc.vector.scalar_tensor_tensor(lem[:], pick[0][:], -2 * BIG, lem[:], ALU.mult, ALU.add))
            first_max(v, lem[:], NE, pick[1][:], best[:, 4], best[:, 5])
            nc.vector.tensor_tensor(picked[:], pick[0][:], pick[1][:], ALU.add).then_inc(rt_picked, 1)
            nc.vector.tensor_tensor(ex[:, :, NG], best[:, 4], best[:, 2], ALU.subtract).then_inc(rt_picked, 1)
            moe_split_l(v, l, 2, 2)
            v.wait_ge(rt_rank, l + 1)
            dve_link(v, nc.vector.tensor_copy(rank[:], ps[:, BR, 128:192].rearrange("p (t e) -> p t e", e=NE)))
            count = rank[:, TILES]
            dve_link(v, nc.vector.tensor_scalar(cat[:, 0:NE], count, float(CAP), None, ALU.min))
            dve_link(v, nc.vector.tensor_tensor(cat[:, NE:], count, cat[:, 0:NE], ALU.subtract))
            dve_link(v, nc.vector.tensor_tensor_scan(first[:], ones[:, 0:2 * NE], cat[:], 0.0, ALU.mult, ALU.add))
            dve_link(v, nc.vector.tensor_tensor(first[:], first[:], cat[:], ALU.subtract))
            shape = [P, TILES, NE]
            dve_link(v, nc.vector.tensor_tensor(ov[:, 0], first[:, NE:], first[:, 0:NE], ALU.subtract))
            dve_link(v, nc.vector.tensor_scalar(ov[:, 0], ov[:, 0], -float(CAP), None, ALU.add))
            dve_link(v, nc.vector.tensor_scalar(tmp[:], rank[:, 0:TILES], float(CAP), None, ALU.is_ge))
            dve_link(v, nc.vector.tensor_tensor(tmp[:], tmp[:], ov[:, 0:1].to_broadcast(shape), ALU.mult))
            dve_link(v, nc.vector.tensor_tensor(tmp[:], tmp[:], rank[:, 0:TILES], ALU.add))
            dve_link(v, nc.vector.tensor_tensor(tmp[:], tmp[:], first[:, 0:NE].unsqueeze(1).to_broadcast(shape), ALU.add))
            for k in range(2):
                dve_link(v, nc.vector.tensor_tensor(lem[:], pick[k][:], tmp[:], ALU.mult))
                dve_link(v, nc.vector.tensor_reduce(dst[:, :, k], lem[:], AX.X, ALU.add))
            dve_link(v, nc.vector.tensor_copy(first_i[:], first[:, 0:NE]))
            nc.vector.tensor_copy(dst_i[:], dst[:].rearrange("p t k -> p (t k)")).then_inc(rt_dst, 1)
            v.wait_ge(rt_exp, l + 1)
            dve_link(v, nc.vector.tensor_reduce(best[:, 0], ex[:, :, 0:NG], AX.X, ALU.add))
            dve_link(v, nc.vector.scalar_tensor_tensor(best[:, 1], ex[:, :, NG], 1.0, best[:, 0], ALU.add, ALU.mult))
            dve_link(v, nc.vector.reciprocal(wts[:, 0], best[:, 1]))
            dve_link(v, nc.vector.tensor_tensor(wts[:, 1], ex[:, :, NG], wts[:, 0], ALU.mult))

        def table_vector(v):
            o = ov[0:1]
            c0 = cat[0:1, NE:]
            dve_link(v, nc.vector.tensor_scalar(o[:, 1], c0, 0.0, None, ALU.is_gt))
            for n in range(1, (TOK - 1) // CAP):
                dve_link(v, nc.vector.tensor_scalar(o[:, 2], c0, float(n * CAP), None, ALU.is_gt))
                dve_link(v, nc.vector.tensor_tensor(o[:, 1], o[:, 1], o[:, 2], ALU.add))
            dve_link(v, nc.vector.tensor_tensor_scan(o[:, 2], ones[0:1, 0:NE], o[:, 1], 0.0, ALU.mult, ALU.add))
            dve_link(v, nc.vector.tensor_tensor(o[:, 1], o[:, 2], o[:, 1], ALU.subtract))
            bshape = [1, EXTRA, NE]
            it = const[0:1, C_IOTA:C_IOTA + EXTRA].unsqueeze(2).to_broadcast(bshape)
            nc.vector.tensor_copy(ovt[0:1, 2 * EXTRA:2 * EXTRA + 1], o[:, 2, NE - 1:NE]).then_inc(dve_step, 1)
            steps["dve"] += 1
            dve_link(v, nc.vector.tensor_tensor(ovb[0:1], o[:, 1:2].to_broadcast(bshape), it, ALU.is_le))
            dve_link(v, nc.vector.tensor_tensor(ovb2[0:1], o[:, 2:3].to_broadcast(bshape), it, ALU.is_le))
            dve_link(v, nc.vector.tensor_tensor(ovb[0:1], ovb[0:1], ovb2[0:1], ALU.subtract))
            dve_link(v, nc.vector.tensor_tensor(ovb2[0:1], ovb[0:1], const[0:1, C_IOTA:C_IOTA + NE].unsqueeze(1).to_broadcast(bshape), ALU.mult))
            dve_link(v, nc.vector.tensor_reduce(ovt[0:1, 0:EXTRA], ovb2[0:1], AX.X, ALU.add))
            dve_link(v, nc.vector.scalar_tensor_tensor(o[:, 3], o[:, 1], -float(CAP), first[0:1, NE:], ALU.mult, ALU.add))
            dve_link(v, nc.vector.tensor_tensor(ovb2[0:1], ovb[0:1], o[:, 3:4].to_broadcast(bshape), ALU.mult))
            dve_link(v, nc.vector.tensor_reduce(ovt[0:1, EXTRA:2 * EXTRA], ovb2[0:1], AX.X, ALU.add))
            dve_link(v, nc.vector.scalar_tensor_tensor(ovt[0:1, EXTRA:2 * EXTRA], const[0:1, C_IOTA:C_IOTA + EXTRA], float(CAP),
                                                       ovt[0:1, EXTRA:2 * EXTRA], ALU.mult, ALU.add))
            nc.vector.tensor_copy(ovt_i[0:1, :], ovt[0:1, :]).then_inc(rt_table, 1)

        def route_scalar(a, l):
            def square(t):
                a.wait_ge(h_mixed, TILES * l + t + 1)
                act_link(a, nc.scalar.activation(squares_junk, h[:, t], ACT.Square, accum_out=stat[:, 0, t:t + 1]))

            def xT_copy(t):
                n = TILES * l + t
                a.wait_ge(rt_xT, n + 1)
                if t == 2:
                    a.wait_ge(rt_logits, n - 1)
                nc.scalar.activation(xT_rows[t].rearrange("p (b n) -> p b n", b=2), ps[:, 2 * t:2 * t + 2], ACT.Copy
                                     ).then_inc(rt_xTc, 1)

            square(0)
            xT_copy(0)
            if l == 0:
                moe_split_h(a, l, 1, 1, 0)
            xT_copy(1)
            square(1)
            square(2)
            xT_copy(2)
            nc.scalar.activation(stat[:, 1, 0:TILES], stat[:, 0, 0:TILES], ACT.Sqrt, bias=const[:, C_EPS:C_EPS + 1],
                                 scale=1.0 / D).then_inc(rms_ready, 1)
            moe_split_h(a, l, 2, 2, 0)
            a.wait_ge(rt_picked, 2 * l + 2)
            nc.scalar.activation(ex[:], ex[:], ACT.Exp).then_inc(rt_exp, 1)

        def route_tensor(pe, l):
            if l == 0:
                pe.wait_ge(ld_route, 16 * 8)
            def transpose_rows(t):
                pe.wait_ge(rt_xn, TILES * l + t + 1)
                for k in range(KD):
                    last = nc.tensor.transpose(ps[:, 2 * t + k // 4, (k % 4) * P:(k % 4 + 1) * P],
                                               rows[:, t, k * P:(k + 1) * P], ident)
                last.then_inc(rt_xT, 1)

            def logits(t):
                pe.wait_ge(rt_xTc, TILES * l + t + 1)
                for k in range(KD):
                    last = nc.tensor.matmul(ps[:, BR, 32 * t:32 * t + NT], xT_rows[t][:, k * P:(k + 1) * P],
                                            wroute[:, l, k, :], start=k == 0, stop=k == KD - 1)
                last.then_inc(rt_logits, 1)

            transpose_rows(0)
            transpose_rows(1)
            logits(0)
            transpose_rows(2)
            logits(1)
            logits(2)
            pe.wait_ge(rt_picked, 2 * l + 1)
            for t in range(TILES + 1):
                for s in range(min(t + 1, TILES)):
                    last = nc.tensor.matmul(ps[:, BR, 128 + t * NE:128 + (t + 1) * NE], upper if s == t else ones,
                                            picked[:, s], start=s == 0, stop=s == min(t, TILES - 1))
            last.then_inc(rt_rank, 1)

        def moe_split_h(a, l, j, slot, q):
            free = M_MOE[l] + (-1 if j == 0 and l == 0 else 0) if isinstance(j, int) and j < 3 else M_MOE[l] + j - 2
            split_h(a, M_MOE[l] + j, slot, split_moe[slot][0], raw_count(l, slot, q), free)

        def moe_split_l(v, l, j, slot):
            split_l(v, M_MOE[l] + j, slot, *split_moe[slot])

        def x_banks():
            return ps[:, BX:BX + 2, 0:4 * CAP].rearrange("p b (k t) -> p b k t", t=CAP)

        def x_part(x):
            return x[:].rearrange("p (b k) t -> p b k t", b=2)

        def moe_scalar(a, l):
            E0 = NE * l
            def x_high(e, par):
                a.wait_ge(xT_done, E0 + e + 1)
                nc.scalar.activation(x_part(xsplit[par][0]), x_banks(), ACT.Copy).then_inc(xh_ready, 1)

            def hidden_high(e):
                a.wait_ge(hT_done, E0 + e + 1)
                nc.scalar.activation(hth[:], ps[:, BH, 0:KE * CAP].rearrange("p (k t) -> p k t", t=CAP), ACT.Copy
                                     ).then_inc(hh_ready, 1)

            def y_copy(e, par):
                a.wait_ge(w_used, M_MOE[l] + (3 * NE if is_last(e) else 3 * e + 5))
                at_least(a, y_stored, 16 * (E0 + e - 1))
                nc.scalar.activation(rows[0:CAP, 2 + par].rearrange("p (b n) -> p b n", b=2), ps[0:CAP, BY:BY + 2],
                                     ACT.Copy).then_inc(y_out, 1)

            x_high(0, 0)

            def step(e, par):
                a.wait_ge(w_used, M_MOE[l] + (1 if is_first(e) else 3 * e))
                at_least(a, hid_done, E0 + e)
                nc.scalar.activation(sil[:], ps[0:CAP, BA], ACT.Silu).then_inc(silu_done, 1)
                if not is_first(e):
                    hidden_high(e - 1)
                if is_first(e):
                    moe_split_h(a, l, 3, 0, 1)
                else:
                    moe_split_h(a, l, 3 * e + 2, 2, e)
                if is_last(e):
                    y_copy(e - 1, 1 - par)
                    return
                x_high(e + 1, 1 - par)
                if is_first(e):
                    moe_split_h(a, l, 4, 1, 1)
                else:
                    moe_split_h(a, l, 3 * e + 3, 0, e + 1)
                    y_copy(e - 1, 1 - par)
                    moe_split_h(a, l, 3 * e + 4, 1, e + 1)

            experts(a, step)
            hidden_high(NE - 1)
            y_copy(NE - 1, 1)
            a.wait_ge(rt_table, l + 1)
            n_over = a.value_load(ovt_i[0:1, 2 * EXTRA:2 * EXTRA + 1], min_val=0, max_val=EXTRA)
            s = over[l]
            with a.Fori(0, EXTRA) as i:
                with a.If(n_over > i):
                    a.wait_ge(s["pe"], 4 * i + 1)
                    nc.scalar.activation(rows[:, 1, 0:KD * CAP].rearrange("p (b k t) -> p b k t", b=2, t=CAP), x_banks(),
                                         ACT.Copy).then_inc(s["act"], 1)
                    a.wait_ge(s["pe"], 4 * i + 2)
                    nc.scalar.activation(sil[:], ps[0:CAP, BA], ACT.Silu).then_inc(s["act"], 1)
                    a.wait_ge(s["pe"], 4 * i + 3)
                    nc.scalar.activation(rows[:, 3, 0:KE * CAP], ps[:, BH, 0:KE * CAP], ACT.Copy).then_inc(s["act"], 1)
                    a.wait_ge(s["pe"], 4 * i + 4)
                    nc.scalar.activation(rows[0:CAP, 2].rearrange("p (b n) -> p b n", b=2), ps[0:CAP, BY:BY + 2],
                                         ACT.Copy).then_inc(s["act"], 1)

        def moe_vector(v, l):
            E0 = NE * l

            def x_low(e, par):
                v.wait_ge(xh_ready, E0 + e + 1)
                nc.vector.tensor_tensor(x_part(xsplit[par][1]), x_banks(), x_part(xsplit[par][0]).bitcast(F32),
                                        ALU.subtract).then_inc(xl_ready, 1)

            def hidden_low(e):
                v.wait_ge(hh_ready, E0 + e + 1)
                nc.vector.tensor_tensor(htl[:], ps[:, BH, 0:KE * CAP].rearrange("p (k t) -> p k t", t=CAP),
                                        hth[:].bitcast(F32), ALU.subtract).then_inc(hl_ready, 1)

            x_low(0, 0)
            table_vector(v)

            def step(e, par):
                if not is_first(e):
                    hidden_low(e - 1)
                moe_split_l(v, l, 3 if is_first(e) else 3 * e + 2, 0 if is_first(e) else 2)
                v.wait_ge(w_used, M_MOE[l] + (2 if is_first(e) else 3 * e + 1))
                v.wait_ge(silu_done, E0 + e + 1)
                nc.vector.tensor_tensor(hid[:], sil[:], ps[0:CAP, BB], ALU.mult).then_inc(hid_done, 1)
                if is_last(e):
                    return
                x_low(e + 1, 1 - par)
                if is_first(e):
                    moe_split_l(v, l, 4, 1)
                else:
                    moe_split_l(v, l, 3 * e + 3, 0)
                    moe_split_l(v, l, 3 * e + 4, 1)

            experts(v, step)
            hidden_low(NE - 1)
            n_over = v.value_load(ovt_i[0:1, 2 * EXTRA:2 * EXTRA + 1], min_val=0, max_val=EXTRA)
            s = over[l]
            with v.Fori(0, EXTRA) as i:
                with v.If(n_over > i):
                    v.wait_ge(s["act"], 4 * i + 2)
                    nc.vector.tensor_tensor(hid[:], sil[:], ps[0:CAP, BB], ALU.mult).then_inc(s["hid"], 1)
            for t in range(TILES):
                v.wait_ge(y_back[t], 32 * (l + 1))
                dve_link(v, nc.vector.scalar_tensor_tensor(h[:, t], y_rows[2 * t], wts[:, 0, t:t + 1], h[:, t],
                                                           ALU.mult, ALU.add))
                nc.vector.scalar_tensor_tensor(h[:, t], y_rows[2 * t + 1], wts[:, 1, t:t + 1], h[:, t],
                                               ALU.mult, ALU.add).then_inc(combined, 1)
            v.wait_ge(combined, TILES * (l + 1))

        def moe_tensor(pe, l):
            E0, m0 = NE * l, M_MOE[l]

            def transpose_x(e, par):
                pe.wait_ge(x_loaded[par], 8 * (E0 + e - par) + 16)
                at_least(pe, xl_ready, E0 + e)
                for k in range(KD):
                    last = nc.tensor.transpose(ps[:, BX + k // 4, (k % 4) * CAP:(k % 4 + 1) * CAP],
                                               rows[0:CAP, par, k * P:(k + 1) * P], ident[0:CAP, 0:CAP])
                last.then_inc(xT_done, 1)

            def product_x(e, par, j, slot, bank):
                wh, wl = [moe_w_view(w[:], KD) for w in split_moe[slot]]
                xh, xl = xsplit[par]
                return split_product(pe, m0 + j, [[ps[0:CAP, bank]]], lambda t, k: xh[:, k], lambda t, k: xl[:, k],
                                     wh, wl, KD, 1)

            def transpose_hidden(e):
                pe.wait_ge(hid_done, E0 + e + 1)
                at_least(pe, hl_ready, E0 + e)
                for k in range(KE):
                    last = nc.tensor.transpose(ps[:, BH, k * CAP:(k + 1) * CAP], hid[:, k * P:(k + 1) * P],
                                               ident[0:CAP, 0:CAP])
                last.then_inc(hT_done, 1)

            def product_y(e, j, slot):
                pe.wait_ge(hl_ready, E0 + e + 1)
                at_least(pe, y_out, E0 + e)
                wh, wl = [moe_w_view(w[:], KE) for w in split_moe[slot]]
                split_product(pe, m0 + j, [[ps[0:CAP, BY], ps[0:CAP, BY + 1]]], lambda t, k: hth[:, k],
                              lambda t, k: htl[:, k], wh, wl, KE, 2).then_inc(w_used, 1)

            transpose_x(0, 0)

            def step(e, par):
                f = is_first(e)
                pe.wait_ge(xl_ready, E0 + e + 1)
                at_least(pe, silu_done, E0 + e)
                product_x(e, par, 0 if f else 3 * e - 1, 0 if f else 2, BA).then_inc(w_used, 1)
                if not f:
                    transpose_hidden(e - 1)
                at_least(pe, hid_done, E0 + e)
                product_x(e, par, 1 if f else 3 * e, 1 if f else 0, BB).then_inc(w_used, 1)
                if not is_last(e):
                    transpose_x(e + 1, 1 - par)
                if not f:
                    product_y(e - 1, 3 * e + 1, 1)

            experts(pe, step)
            transpose_hidden(NE - 1)
            product_y(NE - 1, 3 * NE - 1, 2)
            pe.wait_ge(rt_table, l + 1)
            n_over = pe.value_load(ovt_i[0:1, 2 * EXTRA:2 * EXTRA + 1], min_val=0, max_val=EXTRA)
            s = over[l]
            with pe.Fori(0, EXTRA) as i:
                with pe.If(n_over > i):
                    pe.wait_ge(s["x"], 16 * i + 16)
                    pe.wait_ge(s["st"], 16 * i + 16)
                    for k in range(KD):
                        last = nc.tensor.transpose(ps[:, BX + k // 4, (k % 4) * CAP:(k % 4 + 1) * CAP],
                                                   rows[0:CAP, 0, k * P:(k + 1) * P], ident[0:CAP, 0:CAP])
                    last.then_inc(s["pe"], 1)
                    pe.wait_ge(s["act"], 4 * i + 1)
                    pe.wait_ge(s["w"], 48 * i + 48)
                    for bank, slot in ((BA, 0), (BB, 1)):
                        for k in range(KD):
                            last = nc.tensor.matmul(ps[0:CAP, bank], rows[:, 1, k * CAP:(k + 1) * CAP],
                                                    moe_w_view(raw[:, slot], KD)[:, k], start=k == 0, stop=k == KD - 1)
                    last.then_inc(s["pe"], 1)
                    pe.wait_ge(s["hid"], i + 1)
                    for k in range(KE):
                        last = nc.tensor.transpose(ps[:, BH, k * CAP:(k + 1) * CAP], hid[:, k * P:(k + 1) * P],
                                                   ident[0:CAP, 0:CAP])
                    last.then_inc(s["pe"], 1)
                    pe.wait_ge(s["act"], 4 * i + 3)
                    for c in range(2):
                        for k in range(KE):
                            last = nc.tensor.matmul(ps[0:CAP, BY + c], rows[:, 3, k * CAP:(k + 1) * CAP],
                                                    moe_w_view(raw[:, 2], KE)[:, k, c * 512:c * 512 + 512],
                                                    start=k == 0, stop=k == KE - 1)
                    last.then_inc(s["pe"], 1)

        at = ExitStack()
        KC = 2 * P
        KALL = KC + P
        cst = sb("at_cache", [P, 2 * DECB, KVR + ROPE], F32, at)
        cTs = sb("at_cache_cT", [P, DECB, 2, KC], F32, at)
        w_uk = sb("at_w_uk", [P, 2, HEADS * NOPE], F32, at)
        krT = sb("at_krT", [QK, DECB + 1, KC], F32, at)
        rinv = sb("at_rinv", [P, DECB, KALL], F32, at)
        qa = sb("at_qa", [P, 2, DECB, HEADS * DECS], F32, at)
        sqT = qa[:].rearrange("p s b n -> p s (b n)")
        pcT = sb("at_pcT", [P, 2, HEADS, DECB, DECS], F32, at)
        wukT = pcT[0:QK].rearrange("p s h b q -> p (s h b q)").rearrange("p (h n) -> p h n", h=HEADS)
        gain2 = sb("at_gain", [P, D], F32, at)
        work = sb("at_work", [P, 4, D], F32, at)
        c_sb = sb("at_c", [P, TILES, KVR + ROPE], F32, at)
        q_sb = sb("at_q", [P, TILES, HEADS, QK], F32, at)
        kr = sb("at_krope", [P, TILES, ROPE], F32, at)
        rot = raw[:, 2, WCOL - 2 * 24 * 16:].rearrange("p (i n c) -> p i n c", i=2, c=ROPE // 2)
        g_kva, g_kr = sb("at_g_kva", [P, KVR], F32, at), sb("at_g_kr", [P, ROPE], F32, at)
        g_qa, g_qr = sb("at_g_qa", [P, QR], F32, at), sb("at_g_qr", [P, ROPE], F32, at)
        g_qk = sb("at_g_qk", [QK, 3], F32, at)
        ast = sb("at_stat", [P, 64], F32, at)
        qT = sb("at_qT", [QK, 2, HEADS, P], F32, at)
        qTs = gain2[0:QK].rearrange("p (b n) -> p b n", b=DECB)
        cqT = sb("at_cqT", [P, 3, P], F32, at)
        kst = sb("at_kstat", [P, 2, HEADS], F32, at)
        kcat = sb("at_kcat", [P, 2, HEADS, QK], F32, at)
        cq_sb = kcat[:].rearrange("p a h n -> p (a h n)")[:, 0:TILES * QR].rearrange("p (t n) -> p t n", t=TILES)
        kTp = raw[0:QK, 1, 0:HEADS * SEQ].rearrange("p (h k) -> p h k", h=HEADS)
        vp = raw[:, 1, HEADS * SEQ:HEADS * SEQ + 2 * HEADS * VD].rearrange("p (t n) -> p t n", t=2)
        new_rinv = sb("at_new_rinv", [P, P], F32, at)
        cTn = sb("at_cTn", [P, 2, P], F32, at)
        q_words = q_sb[:].rearrange("p t h n -> p (t h n)")
        s_sb = q_words[:, 0:2 * KALL].rearrange("p (a k) -> p a k", a=2)
        psT = q_words[:, 2 * KALL:4 * KALL].rearrange("p (a k) -> p a k", a=2)
        sst = sb("at_sample_stat", [P, 2, 3], F32, at)
        oT = sb("at_oT", [P, 4, TOK], F32, at)
        rmax = sb("at_rmax", [P, HEADS], F32, at)
        rsum = sb("at_rsum", [P, HEADS], F32, at)
        at.close()
        p_sb = work[:, 0:2].rearrange("p a n -> p (a n)")
        pT = work[:, 2:4].rearrange("p a n -> p (a n)")
        w_dkv = raw[:, 0, 0:KD * (KVR + ROPE)].rearrange("p (k n) -> p k n", k=KD)
        w_dq = raw[:, 1, 0:KD * QR].rearrange("p (k n) -> p k n", k=KD)
        w_uv = raw[:, 1, KD * QR:].rearrange("p (k n) -> p k n", k=2)
        uq_end = QR // P * HEADS * QK
        w_uq = raw[:, 2, 0:uq_end].rearrange("p (k n) -> p k n", k=QR // P)
        cT = raw[:, 2, uq_end:uq_end + 512].rearrange("p (a s t) -> p a s t", a=2, s=2)
        sq = raw[:, 2, uq_end + 512:uq_end + 1024]
        w_o = raw[:, 2, :].rearrange("p (k n) -> p k n", k=4)

        ld_at, ld_atg, ld_kvg, ld_wo = sem("ld_at"), sem("ld_atg"), sem("ld_kvg"), sem("ld_wo")
        ld_at2 = sem("ld_at2")
        lat_stored, ld_cache = sem("lat_stored"), [sem("ld_cache0"), sem("ld_cache1")]
        uk_T, uk_Tc, ch_T, ch_c, ch_K, ch_sq, ch_ssq, ch_rms, ch_rinv = map(
            sem, ["uk_T", "uk_Tc", "ch_T", "ch_cd", "ch_K", "ch_sqd", "ch_ssq", "ch_rmsd", "ch_rinvd"])
        nw_T, nw_Tc, nw_K, nw_sq, nw_ssq, nw_rinv, sq_ready = map(
            sem, ["nw_T", "nw_Tc", "nw_K", "nw_sqd", "nw_ssq", "nw_rinvd", "sq_readyd"])
        qa_done, qa_copied = sem("qa_done"), sem("qa_copied")
        sm_s, sm_step, sm_max, sm_exp, sm_rsum, sm_p, sm_pT, sm_pTc, sm_pc, sm_pcc = map(
            sem, ["sm_s", "sm_step", "sm_maxd", "sm_expd", "sm_rsum", "sm_p", "sm_pT", "sm_pTc", "sm_pc", "sm_pcc"])
        sm_o, pads_zeroed = sem("sm_o"), sem("pads_zeroed")
        at_xn, at_xT, at_xc, at_proj, at_projc = map(sem, ["at_xn", "at_xTd", "at_xc", "at_proj", "at_projc"])
        at_lat, at_cqn, at_cqT, at_cqTc, at_qd, at_qc = map(
            sem, ["at_lat", "at_cqn", "at_cqTd", "at_cqTc", "at_qd", "at_qc"])
        at_qn, at_qT, at_qTc = sem("at_qn"), sem("at_qTd"), sem("at_qTc")
        at_T, at_cTc, at_kv, at_sq, at_red, at_ms, at_rt = map(
            sem, ["at_T", "at_cTc", "at_kv", "at_sqd", "at_red", "at_ms", "at_rt"])
        at_v, at_kcat, at_KT, at_kT = sem("at_v"), sem("at_kcatd"), sem("at_KT"), sem("at_kTd")
        at_sc, at_p1, at_e, at_p2, at_PTc, at_pv, at_o = map(
            sem, ["at_sc", "at_p1", "at_e", "at_p2", "at_PTc", "at_pv", "at_o"])
        at_y = sem("at_y")
        NEW = 2

        def pairs_of(eng, step, n):
            step(0, 0)
            with eng.Fori(0, n // 2 - 1) as i:
                step(2 * i + 1, 1)
                step(2 * i + 2, 0)
            step(n - 1, 1)

        def load_cached(sp, half):
            n = slice(8 * half, 8 * half + 8)
            sp.dma_start(cst[:, n, 0:KVR], A["cache_ckv"].rearrange("b (t p) r -> p (b t) r", p=P)[:, n]
                         ).then_inc(ld_cache[half], 16)
            sp.dma_start(cst[:, n, KVR:], A["cache_krope"].rearrange("b (t p) r -> p (b t) r", p=P)[:, n]
                         ).then_inc(ld_cache[half], 16)

        def load_cache(sp):
            sp.dma_start(w_uk[:], A["w_uk"].rearrange("(k p) h n -> p k (h n)", p=P)).then_inc(ld_cache[0], 16)
            load_cached(sp, 0)

        def at_sync(sp):
            for t in range(TILES):
                sp.wait_ge(y_back[t], 32)
            sp.dma_start(w_dkv, A["w_dkv"].rearrange("(k p) n -> p k n", p=P)).then_inc(ld_at, 16)
            sp.dma_start(w_dq, A["w_dq"][0].rearrange("(k p) n -> p k n", p=P)).then_inc(ld_at, 16)
            load_cached(sp, 1)
            sp.dma_start(w_uq, A["w_uq"][0].rearrange("(k p) h n -> p k (h n)", p=P)).then_inc(ld_at2, 16)
            sp.dma_start(w_uv, A["w_uv"].rearrange("(k p) h n -> p k (h n)", p=P)).then_inc(ld_at2, 16)
            sp.wait_ge(at_qn, 1)
            sp.dma_start(w_o, A["w_o"][0].rearrange("(k p) n -> p k n", p=P)).then_inc(ld_wo, 16)

        def at_pool(g):
            g.dma_start(gain2[:], A["norm_mix"][1:2, :].partition_broadcast(P)).then_inc(ld_kvg, 16)
            g.wait_ge(combined, TILES)
            g.dma_start(g_kva[:], A["kv_a_norm"].rearrange("(a n) -> a n", a=1).partition_broadcast(P)).then_inc(ld_atg, 16)
            g.dma_start(g_kr[:], A["k_rope_norm"].rearrange("(a n) -> a n", a=1).partition_broadcast(P)).then_inc(ld_atg, 16)
            g.dma_start(g_qa[:], A["q_a_norm"].partition_broadcast(P)).then_inc(ld_atg, 16)
            g.dma_start(g_qr[:], A["q_rope_norm"].partition_broadcast(P)).then_inc(ld_atg, 16)
            g.dma_start(g_qk[0:NOPE, 0:1], A["q_nope_norm"][0].rearrange("(n a) -> n a", a=1),
                        allow_slow_non_contiguous=True).then_inc(ld_atg, 16)
            g.dma_start(g_qk[0:NOPE, 1:2], A["k_nope_norm"].rearrange("(n a) -> n a", a=1),
                        allow_slow_non_contiguous=True).then_inc(ld_atg, 16)
            g.wait_ge(at_lat, 1)
            for t in range(2):
                g.dma_start(O[2][0, t * P:(t + 1) * P, :], c_sb[:, t, 0:KVR]).then_inc(lat_stored, 16)
                g.dma_start(O[3][0, t * P:(t + 1) * P, :], kr[:, t, :]).then_inc(lat_stored, 16)
            g.dma_start(O[4].rearrange("b s r -> (b s) r"), c_sb[:, SAMPLE, 0:KVR]).then_inc(lat_stored, 16)
            g.dma_start(O[5].rearrange("b s r -> (b s) r"), kr[:, SAMPLE, :]).then_inc(lat_stored, 16)

        def mean_square_rows(v, x, a, b, st):
            n, w = x.shape[1], b - a
            j = work[:, 0:4].rearrange("p a n -> p (a n)")[:, 0:n * w].rearrange("p (n w) -> p n w", n=n)
            dve_link(v, nc.vector.tensor_tensor(j, x[:, :, a:b], x[:, :, a:b], ALU.mult))
            dve_link(v, nc.vector.tensor_reduce(st, j, AX.X, ALU.add))
            dve_link(v, nc.vector.tensor_scalar(st, st, 1.0 / w, None, ALU.mult))

        def scale_rows(v, x, a, b, st, gain_row=None):
            y = x[:, :, a:b]
            shape = [P, x.shape[1], b - a]
            last = nc.vector.tensor_tensor(y, y, st.unsqueeze(2).to_broadcast(shape), ALU.mult)
            if gain_row is not None:
                dve_link(v, last)
                last = nc.vector.tensor_tensor(y, y, gain_row.unsqueeze(1).to_broadcast(shape), ALU.mult)
            return last

        def rotate(v, x, out, cos, sin, shape):
            half = ROPE // 2
            x1, x2 = x[..., 0:half], x[..., half:ROPE]
            n = 1
            for s in shape[1:-1]:
                n *= s
            r = [rot[:, i, 0:n] if len(shape) == 3 else rot[:, i, 0:n].rearrange("p (t h) c -> p t h c", h=HEADS)
                 for i in range(2)]
            dve_link(v, nc.vector.tensor_tensor(r[0], x1, sin, ALU.mult))
            dve_link(v, nc.vector.tensor_tensor(r[1], x2, sin, ALU.mult))
            dve_link(v, nc.vector.tensor_tensor(out[..., 0:half], x1, cos, ALU.mult))
            dve_link(v, nc.vector.tensor_tensor(out[..., half:ROPE], x2, cos, ALU.mult))
            dve_link(v, nc.vector.tensor_tensor(out[..., 0:half], out[..., 0:half], r[1], ALU.subtract))
            dve_link(v, nc.vector.tensor_tensor(out[..., half:ROPE], out[..., half:ROPE], r[0], ALU.add))

        def at_vector(v):
            inverse_rms(v, work[:, 0])
            v.wait_ge(ld_kvg, 32)
            for t in range(TILES):
                if t:
                    v.wait_ge(at_xT, 2 * t)
                norm_rows(t, work[:, 0]).then_inc(at_xn, 1)
                nc.vector.scalar_tensor_tensor(work[:, 1], h[:, t], stat[:, 1, t:t + 1], gain2[:], ALU.mult, ALU.mult
                                               ).then_inc(at_xn, 1)
                if t == 0:
                    mean_squares(v, 0)
            inverse_key_rms(v, 0)
            nc.vector.memset(krT[0:NOPE], 0.0).then_inc(pads_zeroed, 1)
            nc.vector.memset(wukT[NOPE:QK], 0.0).then_inc(pads_zeroed, 1)
            dve_link(v, nc.vector.memset(g_qk[NOPE:QK, :], 1.0))
            v.wait_ge(ld_atg, 96)
            v.wait_ge(at_projc, 2 * TILES)
            c_all, cq_all = c_sb[:], cq_sb
            mean_square_rows(v, c_all, 0, KVR, ast[:, 0:3])
            mean_square_rows(v, c_all, KVR, KVR + ROPE, ast[:, 3:6])
            mean_square_rows(v, cq_all, 0, QR, ast[:, 6:9])
            rms_inverse(v, ast[:, 0:9], ast[:, 0:9], 1.0)
            scale_rows(v, cq_all, 0, QR, ast[:, 6:9], g_qa[:]).then_inc(at_cqn, 1)
            dve_link(v, nc.vector.tensor_tensor(g_qk[0:NOPE, 2:3], g_qk[0:NOPE, 0:1], g_qk[0:NOPE, 1:2], ALU.mult))
            dve_link(v, scale_rows(v, c_all, 0, KVR, ast[:, 0:3], g_kva[:]))
            dve_link(v, scale_rows(v, c_all, KVR, KVR + ROPE, ast[:, 3:6], g_kr[:]))
            cos3 = const[:, C_COS:C_COS + 48].rearrange("p (t c) -> p t c", t=TILES)
            sin3 = const[:, C_SIN:C_SIN + 48].rearrange("p (t c) -> p t c", t=TILES)
            rotate(v, c_sb[:, :, KVR:], kr[:], cos3, sin3, [P, TILES, 16])
            nc.vector.tensor_copy(c_sb[:, SAMPLE, KVR:], kr[:, SAMPLE]).then_inc(at_lat, 1)
            mean_squares(v, 1)
            inverse_key_rms(v, 1)
            for t in range(TILES):
                v.wait_ge(at_qc, t + 1)
                j = work[:, 0, 0:HEADS * QK].rearrange("p (h n) -> p h n", h=HEADS)
                dve_link(v, nc.vector.tensor_tensor(j, q_sb[:, t], q_sb[:, t], ALU.mult))
                for a_, b_, c_ in ((0, NOPE, 10), (NOPE, QK, 34)):
                    st = ast[:, c_ + HEADS * t:c_ + HEADS * (t + 1)]
                    dve_link(v, nc.vector.tensor_reduce(st, j[:, :, a_:b_], AX.X, ALU.add))
                    dve_link(v, nc.vector.tensor_scalar(st, st, 1.0 / (b_ - a_), None, ALU.mult))
            rms_inverse(v, ast[:, 10:58], ast[:, 10:58], 1.0)
            for n in range(NEW):
                key_rows(v, n)
            q24 = q_sb[:].rearrange("p t h n -> p (t h) n")
            dve_link(v, scale_rows(v, q24, 0, NOPE, ast[:, 10:34]))
            dve_link(v, scale_rows(v, q24, NOPE, QK, ast[:, 34:58], g_qr[:]))
            shape = [P, TILES, HEADS, 16]
            qr_ = q_sb[:, :, :, NOPE:QK]
            tmpq = work[:, 0, 0:TILES * HEADS * ROPE].rearrange("p (t h c) -> p t h c", t=TILES, h=HEADS)
            rotate(v, qr_, tmpq, cos3.unsqueeze(2).to_broadcast(shape), sin3.unsqueeze(2).to_broadcast(shape), shape)
            nc.vector.tensor_copy(qr_, tmpq).then_inc(at_qn, 1)
            v.wait_ge(nw_ssq, 1)
            nc.vector.tensor_scalar(new_rinv[:], ps[:, 7, 0:P], 1.0 / NOPE, EPS, ALU.mult, ALU.add).then_inc(nw_rinv, 1)
            for t in range(2):
                prompt_softmax(v, t)

            def step(b, par):
                v.wait_ge(sm_exp, b + 1)
                nc.vector.reciprocal(sst[:, par, 2:3], sst[:, par, 2:3]).then_inc(sm_rsum, 1)
                v.wait_ge(sm_rsum, b + 1)
                nc.vector.tensor_scalar(s_sb[:, par], s_sb[:, par], sst[:, par, 2:3], None, ALU.mult).then_inc(sm_p, 1)
                if not (isinstance(b, int) and b == DECB - 1):
                    scores(v, b + 1, 1 - par)

            pairs_of(v, step, DECB)
            v.wait_ge(sm_o, 1)
            o3 = ps[:, 0:2].rearrange("p b (h x q) -> p (b h) x q", h=2, x=2)
            nc.vector.tensor_copy(oT[0:VD, :, SEQ:], o3[0:VD, :, 0]).then_inc(at_o, 1)
            nc.vector.tensor_copy(oT[VD:P, :, SEQ:], o3[VD:P, :, 1]).then_inc(at_o, 1)
            moe_split_l(v, 1, 0, 0)
            moe_split_l(v, 1, 1, 1)
            v.wait_ge(at_y, 1)
            v.wait_ge(lat_stored, 96)
            for t in range(TILES):
                nc.vector.tensor_tensor(h[:, t].rearrange("p (c n) -> p c n", c=2), h[:, t].rearrange("p (c n) -> p c n", c=2),
                                        ps[:, 2 * t:2 * t + 2], ALU.add).then_inc(h_mixed, 1)
                weigh_rows(v, 1, t)

        def mean_squares(v, half):
            v.wait_ge(ch_ssq, 4 * half + 4)
            nc.vector.tensor_scalar(rinv[:, 4 * half:4 * half + 4, 0:KC], ps[:, 6:8].rearrange("p b (x k) -> p (b x) k", x=2),
                                    1.0 / NOPE, EPS, ALU.mult, ALU.add).then_inc(ch_rms, 1)

        def inverse_key_rms(v, half):
            v.wait_ge(ch_rinv, half + 1)
            x = rinv[:, 4 * half:4 * half + 4, 0:KC]
            dve_link(v, nc.vector.reciprocal(x, x))

        def scores(v, b, par):
            v.wait_ge(sm_s, b + 1)
            if not (isinstance(b, int) and b < 2):
                v.wait_ge(sm_pT, b - 1)
            x = s_sb[:, par]
            nc.vector.tensor_tensor(x, ps[:, par, 0:KALL], rinv[:, bass.ds(b, 1)].rearrange("p a k -> p (a k)"), ALU.mult
                                    ).then_inc(sm_step, 1)
            v.wait_ge(sm_step, 4 * b + 1)
            nc.vector.tensor_tensor(x, x, ps[:, 2 + par, 0:KALL], ALU.add).then_inc(sm_step, 1)
            v.wait_ge(sm_step, 4 * b + 2)
            own = const[:, bass.ds(C_OWN + P - DECS - DECS * b, P)]
            nc.vector.tensor_tensor(x[:, KC:], x[:, KC:], own, ALU.add).then_inc(sm_step, 1)
            v.wait_ge(sm_step, 4 * b + 3)
            nc.vector.tensor_reduce(sst[:, par, 0:1], x, AX.X, ALU.max).then_inc(sm_step, 1)
            v.wait_ge(sm_step, 4 * b + 4)
            nc.vector.tensor_scalar(sst[:, par, 1:2], sst[:, par, 0:1], -SCALE, None, ALU.mult).then_inc(sm_max, 1)

        def key_rows(v, n):
            k3 = ps[:, 1 + n].rearrange("p (h d) -> p h d", h=HEADS)
            v.wait_ge(at_sq, n + 1)
            nc.vector.tensor_reduce(kst[:, n], sq[:].rearrange("p (h d) -> p h d", h=HEADS), AX.X, ALU.add
                                    ).then_inc(at_red, 1)
            v.wait_ge(at_red, n + 1)
            nc.vector.tensor_scalar(kst[:, n], kst[:, n], 1.0 / NOPE, EPS, ALU.mult, ALU.add).then_inc(at_ms, 1)
            v.wait_ge(at_rt, 2 * n + 1)
            nc.vector.reciprocal(kst[:, n], kst[:, n]).then_inc(at_rt, 1)
            nc.vector.tensor_copy(kcat[:, n, :, NOPE:], kr[:, n].unsqueeze(1).to_broadcast([P, HEADS, ROPE])
                                  ).then_inc(at_kcat, 1)
            v.wait_ge(at_rt, 2 * n + 2)
            nc.vector.tensor_tensor(kcat[:, n, :, 0:NOPE], k3, kst[:, n].unsqueeze(2).to_broadcast([P, HEADS, NOPE]),
                                    ALU.mult).then_inc(at_kcat, 1)

        def softmax(v, t, x, shape):
            m, s = rmax[:], rsum[:]
            nc.vector.tensor_reduce(m, x, AX.X, ALU.max).then_inc(at_p2x, 1)
            v.wait_ge(at_p2x, 3 * t + 1)
            nc.vector.tensor_tensor(x, x, m.unsqueeze(2).to_broadcast(shape), ALU.subtract).then_inc(at_p1, 1)
            v.wait_ge(at_e, t + 1)
            nc.vector.tensor_reduce(s, x, AX.X, ALU.add).then_inc(at_p2x, 1)
            v.wait_ge(at_p2x, 3 * t + 2)
            nc.vector.reciprocal(s, s).then_inc(at_p2x, 1)
            v.wait_ge(at_p2x, 3 * t + 3)
            nc.vector.tensor_tensor(x, x, s.unsqueeze(2).to_broadcast(shape), ALU.mult).then_inc(at_p2, 1)

        at_p2x, at_ps = sem("at_p2x"), sem("at_ps")

        def prompt_softmax(v, t):
            nk = (t + 1) * P
            p3 = p_sb.rearrange("p (h k) -> p h k", h=HEADS)
            s3 = ps[:, 0:4].rearrange("p b (h k) -> p (b h) k", h=2)
            v.wait_ge(at_sc, t + 1)
            if t:
                v.wait_ge(at_PTx, t)
            else:
                v.wait_ge(at_qT, TILES)
            if t:
                nc.vector.tensor_scalar(p3[:, :, 0:P], s3[:, :, 0:P], SCALE, None, ALU.mult).then_inc(at_ps, 1)
            own = slice(t * P, (t + 1) * P)
            nc.vector.scalar_tensor_tensor(p3[:, :, own], s3[:, :, own], SCALE,
                                           const[:, C_MASK:C_MASK + P].unsqueeze(1).to_broadcast([P, HEADS, P]),
                                           ALU.mult, ALU.add).then_inc(at_ps, 1)
            v.wait_ge(at_ps, [1, 3][t])
            softmax(v, t, p3[:, :, 0:nk], [P, HEADS, nk])
            if t:
                v.wait_ge(sq_ready, 1)
                dve_link(v, nc.vector.reciprocal(new_rinv[:], new_rinv[:]))
                dve_link(v, nc.vector.tensor_copy(rinv[:, :, KC:], new_rinv[:].unsqueeze(1).to_broadcast([P, DECB, P])))
                scores(v, 0, 0)
            v.wait_ge(at_pv, t + 1)
            o3 = ps[:, 6:8].rearrange("p b (h x q) -> p (b h) x q", h=2, x=2)
            nc.vector.tensor_copy(oT[0:VD, :, t * P:(t + 1) * P], o3[0:VD, :, 0]).then_inc(at_o, 1)
            nc.vector.tensor_copy(oT[VD:P, :, t * P:(t + 1) * P], o3[VD:P, :, 1]).then_inc(at_o, 1)

        def at_scalar(a):
            a.wait_ge(uk_T, 1)
            nc.scalar.activation(wukT[0:NOPE].rearrange("p h n -> p (h n)"),
                                 ps[0:NOPE, 0:4].rearrange("p b n -> p (b n)"), ACT.Copy).then_inc(uk_Tc, 1)

            def cache_copies(b):
                a.wait_ge(ch_T, b + 1)
                nc.scalar.activation(cTs[:, bass.ds(b, 1)].rearrange("p a s k -> p (a s k)"), ps[:, 0], ACT.Copy
                                     ).then_inc(ch_c, 1)
                nc.scalar.activation(krT[NOPE:QK, bass.ds(b, 1)].rearrange("p a k -> p (a k)"), ps[NOPE:QK, 1, 0:KC],
                                     ACT.Copy).then_inc(ch_c, 1)

            def squares(b):
                if b % 4 == 0:
                    cache_copies(b)
                if b % 4 < 3:
                    cache_copies(b + 1)
                for i in range(2):
                    a.wait_ge(ch_K, 2 * b + i + 1)
                    if i == 0 and b >= 2:
                        a.wait_ge(ch_ssq, b - 1)
                    nc.scalar.activation(sqT[:, b % 2, i * 512:i * 512 + 512], ps[:, 2 + i], ACT.Square).then_inc(ch_sq, 1)

            for b in range(4):
                squares(b)
            root(a, stat[:, 1, 0:TILES])
            for t in range(TILES):
                if t == 1:
                    roots_of_keys(a, 0)
                for i in range(2):
                    a.wait_ge(at_xT, 2 * t + i + 1)
                    if t:
                        a.wait_ge(at_proj, t)
                    nc.scalar.activation(work[:, 2 + i].rearrange("p (b n) -> p b n", b=2), ps[:, 2 * i:2 * i + 2],
                                         ACT.Copy).then_inc(at_xc, 1)
                a.wait_ge(at_proj, t + 1)
                nc.scalar.activation(c_sb[:, t], ps[:, 4, 0:KVR + ROPE], ACT.Copy).then_inc(at_projc, 1)
                nc.scalar.activation(cq_sb[:, t], ps[:, 5, 0:QR], ACT.Copy).then_inc(at_projc, 1)
            squares(4)
            root(a, ast[:, 0:9])
            for b in range(5, DECB):
                squares(b)
            roots_of_keys(a, 1)
            for t in range(TILES):
                a.wait_ge(at_cqT, t + 1)
                if t:
                    a.wait_ge(at_qd, t)
                nc.scalar.activation(cqT[:], ps[:, 6, 0:QR].rearrange("p (k t) -> p k t", k=3), ACT.Copy).then_inc(at_cqTc, 1)
                a.wait_ge(at_qd, t + 1)
                nc.scalar.activation(q_sb[:, t].rearrange("p (b h) n -> p b (h n)", b=2), ps[:, 4:6, 0:QR], ACT.Copy
                                     ).then_inc(at_qc, 1)
            root(a, ast[:, 10:58])
            key_tiles(a)
            a.wait_ge(nw_T, 1)
            nc.scalar.activation(cTn[:].rearrange("p s k -> p (s k)"), ps[:, 6, 0:2 * P], ACT.Copy).then_inc(nw_Tc, 1)
            nc.scalar.activation(krT[NOPE:QK, DECB, 0:P], ps[NOPE:QK, 6, 2 * P:3 * P], ACT.Copy).then_inc(nw_Tc, 1)
            a.wait_ge(nw_K, 1)
            nc.scalar.activation(sqT[:, 0, 0:512], ps[:, 3], ACT.Square).then_inc(nw_sq, 1)
            for t in range(TILES):
                a.wait_ge(at_qT, t + 1)
                src = ps[0:QK, 0:2].rearrange("p c n -> p (c n)")
                if t < SAMPLE:
                    nc.scalar.activation(qT[:, t].rearrange("p h n -> p (h n)"), src, ACT.Copy,
                                         scale=g_qk[:, 0:1]).then_inc(at_qTc, 1)
                else:
                    nc.scalar.activation(qTs.rearrange("p b (h q) -> p h b q", h=HEADS),
                                         src.rearrange("p (h b q) -> p h b q", h=HEADS, b=DECB), ACT.Copy,
                                         scale=g_qk[:, 2:3]).then_inc(at_qTc, 1)
            a.wait_ge(nw_rinv, 1)
            nc.scalar.activation(new_rinv[:], new_rinv[:], ACT.Sqrt).then_inc(sq_ready, 1)
            for t in range(2):
                n = (t + 1) * P
                probabilities(a, t, p_sb.rearrange("p (h k) -> p h k", h=HEADS)[:, :, 0:n])
                if t == 0:
                    a.wait_ge(qa_done, 1)
                    for s in range(2):
                        nc.scalar.activation(qa[:, s].rearrange("p b (h q) -> p h b q", h=HEADS),
                                             ps[:, 2 * s:2 * s + 2].rearrange("p c (h b q) -> p (c h) b q", h=4, b=DECB),
                                             ACT.Copy).then_inc(qa_copied, 1)
                for c in range(t + 1):
                    a.wait_ge(at_PTx, [0, 1][t] + c + 1)
                    nc.scalar.activation(pT[:, c * D:(c + 1) * D].rearrange("p (b n) -> p b n", b=2),
                                         ps[:, 4 + 2 * c:6 + 2 * c], ACT.Copy).then_inc(at_PTc, 1)

            def step(b, par):
                a.wait_ge(sm_max, b + 1)
                nc.scalar.activation(s_sb[:, par], s_sb[:, par], ACT.Exp, bias=sst[:, par, 1:2], scale=SCALE,
                                     accum_out=sst[:, par, 2:3]).then_inc(sm_exp, 1)
                a.wait_ge(sm_pT, b + 1)
                nc.scalar.activation(psT[:, par], ps[:, 4 + par, 0:KALL], ACT.Copy).then_inc(sm_pTc, 1)
                a.wait_ge(sm_pc, b + 1)
                nc.scalar.activation(pcT[:, :, :, bass.ds(b, 1), :].rearrange("p s h a q -> p s h (a q)"),
                                     ps[:, 6 + par, 0:2 * P].rearrange("p (s h q) -> p s h q", s=2, h=HEADS),
                                     ACT.Copy).then_inc(sm_pcc, 1)

            pairs_of(a, step, DECB)
            a.wait_ge(sm_o, 1)
            moe_split_h(a, 1, 0, 0, 0)
            moe_split_h(a, 1, 1, 1, 0)

        at_PTx = sem("at_PTx")

        def roots_of_keys(a, half):
            a.wait_ge(ch_rms, half + 1)
            x = rinv[:, 4 * half:4 * half + 4, 0:KC]
            nc.scalar.activation(x, x, ACT.Sqrt).then_inc(ch_rinv, 1)

        def probabilities(a, t, x):
            a.wait_ge(at_p1, t + 1)
            nc.scalar.activation(x, x, ACT.Exp).then_inc(at_e, 1)

        def key_tiles(a):
            def c_copy(n):
                a.wait_ge(at_T, n + 1)
                nc.scalar.activation(cT[:, n], ps[:, 0, 0:KVR].rearrange("p (k t) -> p k t", k=2), ACT.Copy
                                     ).then_inc(at_cTc, 1)

            def kT_copy(n):
                a.wait_ge(at_KT, n + 1)
                nc.scalar.activation(kTp[:, :, n * P:(n + 1) * P].rearrange("p (b h) n -> p b h n", b=2),
                                     ps[0:QK, 4:6].rearrange("p b (h n) -> p b h n", h=4), ACT.Copy,
                                     scale=g_qk[:, 1:2]).then_inc(at_kT, 1)

            c_copy(0)
            for n in range(NEW):
                if n + 1 < NEW:
                    c_copy(n + 1)
                a.wait_ge(at_kv, n + 1)
                nc.scalar.activation(vp[:, n], ps[:, 3], ACT.Copy).then_inc(at_v, 1)
                at_least(a, at_red, n)
                nc.scalar.activation(sq[:], ps[:, 1 + n], ACT.Square).then_inc(at_sq, 1)
                if n:
                    kT_copy(n - 1)
                a.wait_ge(at_ms, n + 1)
                nc.scalar.activation(kst[:, n], kst[:, n], ACT.Sqrt).then_inc(at_rt, 1)
            kT_copy(NEW - 1)

        def at_tensor(pe):
            pe.wait_ge(ld_cache[0], 48)
            for s in range(2):
                for hh in range(HEADS):
                    last = nc.tensor.transpose(ps[0:NOPE, hh // 2, (hh % 2) * KVR + s * P:(hh % 2) * KVR + (s + 1) * P],
                                               w_uk[:, s, hh * NOPE:(hh + 1) * NOPE], ident)
            last.then_inc(uk_T, 1)
            pe.wait_ge(uk_Tc, 1)

            def turn_cache(b):
                if b:
                    pe.wait_ge(ch_c, 2 * b)
                for i in range(2):
                    row = cst[:, 2 * b + i]
                    for s in range(2):
                        nc.tensor.transpose(ps[:, 0, s * KC + i * P:s * KC + (i + 1) * P], row[:, s * P:(s + 1) * P], ident)
                    last = nc.tensor.transpose(ps[0:QK, 1, i * P:(i + 1) * P], row[:, KVR - NOPE:], ident)
                last.then_inc(ch_T, 1)

            def sum_squares(b, par):
                pe.wait_ge(ch_sq, 2 * b + 2)
                out = ps[:, 6 + b % 4 // 2, (b % 2) * KC:(b % 2 + 1) * KC]
                for hp in range(4):
                    last = nc.tensor.matmul(out, head_sums(hp), sqT[:, par, hp * KC:(hp + 1) * KC], start=hp == 0, stop=hp == 3)
                last.then_inc(ch_ssq, 1)

            def head_sums(hp):
                return const[:, C_HEADS + 96 - 32 * hp:C_HEADS + 96 - 32 * hp + P]

            def prepare(b, par):
                if b % 4 == 0:
                    pe.wait_ge(ld_cache[b // 4], 48 - 16 * (b // 4))
                    turn_cache(b)
                if b % 4 < 3:
                    turn_cache(b + 1)
                pe.wait_ge(ch_c, 2 * b + 1)
                for hp in range(4):
                    if hp % 2 == 0 and b:
                        pe.wait_ge(ch_sq, 2 * b + hp // 2 - 1)
                    for s in range(2):
                        last = nc.tensor.matmul(ps[:, 2 + hp // 2, (hp % 2) * KC:(hp % 2 + 1) * KC],
                                                w_uk[:, s, hp * P:(hp + 1) * P],
                                                cTs[:, b, s],
                                                start=s == 0, stop=s == 1)
                    if hp % 2:
                        last.then_inc(ch_K, 1)
                if b % 4:
                    sum_squares(b - 1, 1 - par)

            for b in range(4):
                prepare(b, b % 2)
            sum_squares(3, 1)
            pe.wait_ge(ld_at, 32)
            for t in range(TILES):
                for i in range(2):
                    pe.wait_ge(at_xn, 2 * t + i + 1)
                    if t:
                        pe.wait_ge(at_xc, 2 * t)
                    for k in range(KD):
                        last = nc.tensor.transpose(ps[:, 2 * i + k // 4, (k % 4) * P:(k % 4 + 1) * P],
                                                   work[:, i, k * P:(k + 1) * P], ident)
                    last.then_inc(at_xT, 1)
                at_least(pe, at_projc, 2 * t)
                pe.wait_ge(at_xc, 2 * t + 2)
                for i, (w, n) in enumerate(((w_dkv, KVR + ROPE), (w_dq, QR))):
                    for k in range(KD):
                        last = nc.tensor.matmul(ps[:, 4 + i, 0:n], work[:, 2 + i, k * P:(k + 1) * P], w[:, k],
                                                start=k == 0, stop=k == KD - 1)
                last.then_inc(at_proj, 1)
            pe.wait_ge(ch_rms, 1)
            for b in range(4, DECB):
                prepare(b, b % 2)
            sum_squares(DECB - 1, 1)
            pe.wait_ge(ld_at2, 32)
            pe.wait_ge(at_cqn, 1)
            pe.wait_ge(at_projc, 2 * TILES)
            pe.wait_ge(ch_rms, 2)
            for t in range(TILES):
                if t:
                    pe.wait_ge(at_cqTc, t)
                for k in range(3):
                    last = nc.tensor.transpose(ps[:, 6, k * P:(k + 1) * P], cq_sb[:, t, k * P:(k + 1) * P], ident)
                last.then_inc(at_cqT, 1)
                pe.wait_ge(at_cqTc, t + 1)
                if t:
                    pe.wait_ge(at_qc, t)
                for c in range(2):
                    for k in range(3):
                        last = nc.tensor.matmul(ps[:, 4 + c, 0:QR], cqT[:, k], w_uq[:, k, c * QR:(c + 1) * QR],
                                                start=k == 0, stop=k == 2)
                last.then_inc(at_qd, 1)
            pe.wait_ge(at_lat, 1)
            pe.wait_ge(at_qc, TILES)
            expand(pe)
            for s in range(2):
                nc.tensor.transpose(ps[:, 6, s * P:(s + 1) * P], c_sb[:, SAMPLE, s * P:(s + 1) * P], ident)
            nc.tensor.transpose(ps[0:QK, 6, 2 * P:3 * P], c_sb[:, SAMPLE, KVR - NOPE:], ident).then_inc(nw_T, 1)
            pe.wait_ge(nw_Tc, 2)
            pe.wait_ge(at_v, NEW)
            for hp in range(4):
                for s in range(2):
                    last = nc.tensor.matmul(ps[:, 3, hp * P:(hp + 1) * P], w_uk[:, s, hp * P:(hp + 1) * P], cTn[:, s],
                                            start=s == 0, stop=s == 1)
            last.then_inc(nw_K, 1)
            pe.wait_ge(nw_sq, 1)
            for hp in range(4):
                last = nc.tensor.matmul(ps[:, 7, 0:P], head_sums(hp), sqT[:, 0, hp * P:(hp + 1) * P], start=hp == 0, stop=hp == 3)
            last.then_inc(nw_ssq, 1)
            pe.wait_ge(at_qn, 1)
            for t in range(TILES):
                at_least(pe, at_qTc, t)
                for hh in range(HEADS):
                    last = nc.tensor.transpose(ps[0:QK, hh // 4, (hh % 4) * P:(hh % 4 + 1) * P], q_sb[:, t, hh], ident)
                last.then_inc(at_qT, 1)
            pe.wait_ge(at_qTc, TILES)
            pe.wait_ge(at_kT, NEW)
            def sample_scores(b, par):
                if b >= 2:
                    pe.wait_ge(sm_max, b - 1)
                for cols, keys in ((slice(0, KC), cTs[:, b]), (slice(KC, KALL), cTn)):
                    for s in range(2):
                        nc.tensor.matmul(ps[:, par, cols], qa[:, s, b], keys[:, s], start=s == 0, stop=s == 1)
                nc.tensor.matmul(ps[:, 2 + par, 0:KC], qTs[:, b], krT[:, b],
                                 start=True, stop=True)
                nc.tensor.matmul(ps[:, 2 + par, KC:KALL], qTs[:, b], krT[:, DECB, 0:P], start=True, stop=True).then_inc(sm_s, 1)

            def latent_queries():
                for hh in range(HEADS):
                    for s in range(2):
                        last = nc.tensor.matmul(ps[:, 2 * s + hh // 4, (hh % 4) * P:(hh % 4 + 1) * P],
                                                wukT[:, hh, s * P:(s + 1) * P], qTs[:, :, hh * DECS:(hh + 1) * DECS],
                                                start=True, stop=True)
                last.then_inc(qa_done, 1)

            pe.wait_ge(pads_zeroed, 2)
            for t in range(2):
                if t:
                    pe.wait_ge(qa_copied, 2)
                for hh in range(HEADS):
                    last = nc.tensor.matmul(ps[:, hh // 2, (hh % 2) * SEQ:(hh % 2) * SEQ + (t + 1) * P],
                                            qT[:, t, hh], kTp[:, hh, 0:(t + 1) * P], start=True, stop=True)
                last.then_inc(at_sc, 1)
                pe.wait_ge(at_ps, [1, 3][t])
                if t == 0:
                    latent_queries()
                else:
                    sample_scores(0, 0)
                    sample_scores(1, 1)
                pe.wait_ge(at_p2, t + 1)
                for c in range(t + 1):
                    if t and c == 0:
                        pe.wait_ge(at_PTc, 1)
                    if c:
                        pe.wait_ge(at_o, 2)
                    for hh in range(HEADS):
                        last = nc.tensor.transpose(ps[:, 4 + 2 * c + hh // 4, (hh % 4) * P:(hh % 4 + 1) * P],
                                                   p_sb[:, hh * SEQ + c * P:hh * SEQ + (c + 1) * P], ident)
                    last.then_inc(at_PTx, 1)
                pe.wait_ge(at_PTc, [1, 3][t])
                for hp in range(HEADS // 2):
                    for c in range(t + 1):
                        last = nc.tensor.matmul(ps[:, 6 + hp // 2, (hp % 2) * 256:(hp % 2) * 256 + 256],
                                                vp[:, c, hp * P:(hp + 1) * P],
                                                pT[:, c * D + hp * 256:c * D + hp * 256 + 256], start=c == 0, stop=c == t)
                last.then_inc(at_pv, 1)
            pe.wait_ge(at_o, 4)

            def step(b, par):
                if 0 < b < DECB - 1:
                    sample_scores(b + 1, 1 - par)
                pe.wait_ge(sm_p, b + 1)
                for c in range(3):
                    last = nc.tensor.transpose(ps[:, 4 + par, c * P:(c + 1) * P], s_sb[:, par, c * P:(c + 1) * P], ident)
                last.then_inc(sm_pT, 1)
                if b >= 2:
                    pe.wait_ge(sm_pcc, b - 1)
                pe.wait_ge(sm_pTc, b + 1)
                for s in range(2):
                    for c in range(3):
                        rows_ = c_sb[:, SAMPLE] if c == 2 else cst[:, 2 * b + c]
                        last = nc.tensor.matmul(ps[:, 6 + par, s * P:(s + 1) * P], rows_[:, s * P:(s + 1) * P],
                                                psT[:, par, c * P:(c + 1) * P], start=c == 0, stop=c == 2)
                last.then_inc(sm_pc, 1)

            for b in range(DECB):
                step(b, b % 2)
            pe.wait_ge(sm_pcc, DECB)
            for hh in range(HEADS):
                for s in range(2):
                    last = nc.tensor.matmul(ps[:, hh // 4, (hh % 4) * P:(hh % 4 + 1) * P],
                                            w_uv[:, s, (hh // 2) * P:(hh // 2 + 1) * P],
                                            pcT[:, s, hh].rearrange("p b q -> p (b q)"), start=s == 0, stop=s == 1)
            last.then_inc(sm_o, 1)
            pe.wait_ge(ld_wo, 16)
            pe.wait_ge(at_o, 6)
            for t in range(TILES):
                for c in range(2):
                    for k in range(4):
                        last = nc.tensor.matmul(ps[:, 2 * t + c], oT[:, k, t * P:(t + 1) * P],
                                                w_o[:, k, c * 512:c * 512 + 512], start=k == 0, stop=k == 3)
            last.then_inc(at_y, 1)

        def expand(pe):
            def turn(n):
                at_least(pe, at_cTc, n)
                for k in range(2):
                    last = nc.tensor.transpose(ps[:, 0, k * P:(k + 1) * P], c_sb[:, n, k * P:(k + 1) * P], ident)
                last.then_inc(at_T, 1)

            def turn_keys(n):
                pe.wait_ge(at_kcat, 2 * n + 2)
                at_least(pe, at_kT, n)
                for hh in range(HEADS):
                    last = nc.tensor.transpose(ps[0:QK, 4 + hh // 4, (hh % 4) * P:(hh % 4 + 1) * P], kcat[:, n, hh], ident)
                last.then_inc(at_KT, 1)

            turn(0)
            for n in range(NEW):
                if n + 1 < NEW:
                    turn(n + 1)
                pe.wait_ge(at_cTc, n + 1)
                at_least(pe, at_v, n)
                for k in range(2):
                    nc.tensor.matmul(ps[:, 1 + n], cT[:, n, k], w_uk[:, k], start=k == 0, stop=k == 1)
                for k in range(2):
                    last = nc.tensor.matmul(ps[:, 3], cT[:, n, k], w_uv[:, k], start=k == 0, stop=k == 1)
                last.then_inc(at_kv, 1)
                if n:
                    turn_keys(n - 1)
            turn_keys(NEW - 1)

        out_stored = sem("out_stored")
        block = top.enter_context(nc.Block())

        @block.sync
        def _(sp):
            gm_sync(sp)
            moe_sync(sp, 0)
            at_sync(sp)
            moe_sync(sp, 1)
            for t in range(TILES):
                sp.wait_ge(combined, TILES + t + 1)
                out = O[0][0, t * P:(t + 1) * P, :] if t < SAMPLE else O[1].rearrange("b s d -> (b s) d")
                sp.dma_start(out, h[:, t]).then_inc(out_stored, 16)
            sp.wait_ge(out_stored, 16 * TILES)
            sp.wait_ge(v_stored, 16)
            sp.wait_ge(lat_stored, 96)

        @block.gpsimd
        def _(g):
            gm_pool(g)
            moe_pool(g, 0)
            at_pool(g)
            moe_pool(g, 1)

        @block.scalar
        def _(a):
            gm_scalar(a)
            route_scalar(a, 0)
            moe_scalar(a, 0)
            at_scalar(a)
            route_scalar(a, 1)
            moe_scalar(a, 1)

        @block.vector
        def _(v):
            gm_vector(v)
            route_vector(v, 0)
            moe_vector(v, 0)
            at_vector(v)
            route_vector(v, 1)
            moe_vector(v, 1)

        @block.tensor
        def _(pe):
            gm_tensor(pe)
            route_tensor(pe, 0)
            moe_tensor(pe, 0)
            at_tensor(pe)
            route_tensor(pe, 1)
            moe_tensor(pe, 1)


_INS = ['x_prompt', 'x_sample', 'cache_ckv', 'cache_krope', 'norm_mix', 'norm_ffn', 'gm_w_in', 'gm_b_in', 'gm_ln_g',
        'gm_ln_b', 'gm_w_s', 'gm_b_s', 'gm_w_out', 'gm_b_out', 'kv_norm', 'w_dkv', 'kv_a_norm', 'k_rope_norm', 'w_uk',
        'w_uv', 'k_nope_norm', 'w_dq', 'q_a_norm', 'w_uq', 'q_nope_norm', 'q_rope_norm', 'w_o', 'moe_w_group',
        'moe_b_group', 'moe_w_expert', 'moe_b_expert', 'moe_w1', 'moe_w3', 'moe_w2']
_OUTS = [((1, SEQ, D), 'float32'), ((DECB, DECS, D), 'float32'), ((1, SEQ, KVR), 'float32'),
         ((1, SEQ, ROPE), 'float32'), ((DECB, DECS, KVR), 'float32'), ((DECB, DECS, ROPE), 'float32'),
         ((1, DECB, DECS, DG), 'float32')]


def kernel(**inputs):
    import numpy as _np
    import concourse.bacc as _bacc
    from concourse import mybir as _mybir
    from concourse.bass_utils import run_bass_kernel_spmd as _run

    nc = _bacc.Bacc("TRN2", target_bir_lowering=False, num_devices=1)
    arrays, ins, outs = {}, {}, []
    for name in _INS:
        a = _np.ascontiguousarray(inputs[name])
        arrays[f"in_{name}_dram"] = a
        ins[name] = nc.dram_tensor(f"in_{name}_dram", a.shape, _mybir.dt.from_np(a.dtype), kind="ExternalInput").ap()
    arrays["in_const_dram"] = constants()
    ins["const"] = nc.dram_tensor("in_const_dram", (P, CONST_W), _mybir.dt.float32, kind="ExternalInput").ap()
    for i, (shape, dtype) in enumerate(_OUTS):
        dt = _mybir.dt.from_np(_np.dtype(dtype))
        outs.append(nc.dram_tensor(f"out_{i}_dram", shape, dt, kind="ExternalOutput").ap())
    build(nc, ins, outs)
    r = _run(nc, [arrays], core_ids=[0])
    return tuple(r.results[0][f"out_{i}_dram"] for i in range(len(_OUTS)))
```
